# Optimizing a Trainium2 kernel written in Bass

```python
import math
import jax
import jax.numpy as jnp
from jax import lax
import numpy as np
import jax, jax.numpy as jnp

D_MODEL = 1024
BATCH = 1
SEQ = 256
DEPTH = 2

PLE_DIM = 256
D_FF = 2816
EPS = 1e-6
Q_BLOCK = 128
MLA_HEADS = 8
MLA_Q_LORA = 384
MLA_KV_LORA = 256
MLA_NOPE = 64
MLA_ROPE = 32
MLA_V = 64
MLA_QK = MLA_NOPE + MLA_ROPE
ROPE_THETA = 10000.0
GDN_HEADS = 4
GDN_DK = 128
GDN_DV = 128
GDN_CONV = 4
GDN_CHUNK = 64
GDN_KW = GDN_HEADS * GDN_DK
GDN_VW = GDN_HEADS * GDN_DV
GDN_CONV_CH = 2 * GDN_KW + GDN_VW
DSA_HEADS = 8
DSA_KV_HEADS = 2
DSA_HEAD_DIM = 128
IDX_HEADS = 8
IDX_DIM = 64
DSA_TOPK = 256
EVEN_IN = MLA_Q_LORA + MLA_KV_LORA + MLA_ROPE + GDN_CONV_CH + GDN_VW + 2 * GDN_HEADS
EVEN_OUT = MLA_HEADS * MLA_V + GDN_VW
ODD_IN = DSA_HEADS * DSA_HEAD_DIM + 2 * DSA_KV_HEADS * DSA_HEAD_DIM + IDX_HEADS * IDX_DIM + IDX_DIM + IDX_HEADS
ODD_OUT = DSA_HEADS * DSA_HEAD_DIM


def rms_norm(x, g):
    xf = x.astype(jnp.float32)
    y = xf * lax.rsqrt(jnp.mean(xf * xf, axis=-1, keepdims=True) + EPS)
    return (y * g.astype(jnp.float32)).astype(x.dtype)

def l2_norm(x):
    return x * lax.rsqrt(jnp.sum(x * x, axis=-1, keepdims=True) + EPS)

def split_last(t, sizes):
    out, off = [], 0
    for s in sizes:
        out.append(t[..., off:off + s])
        off += s
    return out

def swiglu(h, w_gu, w_down):
    g, u = jnp.split(h @ w_gu, 2, axis=-1)
    return (jax.nn.silu(g) * u) @ w_down

def rope_tail(x, pos):
    half = MLA_ROPE // 2
    inv_freq = ROPE_THETA ** (-jnp.arange(half, dtype=jnp.float32) / half)
    ang = pos.astype(jnp.float32)[:, None] * inv_freq[None, :]
    cos = jnp.cos(ang)[None, :, None, :]
    sin = jnp.sin(ang)[None, :, None, :]
    xf = x.astype(jnp.float32)
    keep, x1, x2 = xf[..., :-MLA_ROPE], xf[..., -MLA_ROPE:-half], xf[..., -half:]
    return jnp.concatenate([keep, x1 * cos - x2 * sin, x2 * cos + x1 * sin], axis=-1).astype(x.dtype)

def to_blocks(t):
    b, s = t.shape[0], t.shape[1]
    return jnp.moveaxis(t.reshape((b, s // Q_BLOCK, Q_BLOCK) + t.shape[2:]), 1, 0)

def from_blocks(t):
    t = jnp.moveaxis(t, 0, 1)
    return t.reshape((t.shape[0], t.shape[1] * t.shape[2]) + t.shape[3:])

def causal_attention(q, k, v):
    S, dk = q.shape[1], q.shape[-1]
    scale = dk ** -0.5
    kpos = jnp.arange(S)
    qpos = jnp.arange(S).reshape(S // Q_BLOCK, Q_BLOCK)

    def one_block(blk):
        qb, pb = blk
        s = jnp.einsum('bqhd,bkhd->bhqk', qb, k).astype(jnp.float32) * scale
        s = jnp.where(kpos[None, None, None, :] <= pb[None, None, :, None], s, -jnp.inf)
        pr = jax.nn.softmax(s, axis=-1).astype(v.dtype)
        return jnp.einsum('bhqk,bkhd->bqhd', pr, v)

    return from_blocks(lax.map(one_block, (to_blocks(q), qpos)))

def causal_depthwise_conv(x, w):
    K, C = w.shape
    return lax.conv_general_dilated(x, w[:, None, :].astype(x.dtype), window_strides=(1,),
                                    padding=[(K - 1, 0)], dimension_numbers=('NWC', 'WIO', 'NWC'),
                                    feature_group_count=C)

def gated_delta_chunked(q, k, v, g, beta):
    B, S, H, DK = q.shape
    DV = v.shape[-1]
    C = GDN_CHUNK
    N = S // C

    def chunks(t):
        return jnp.moveaxis(t.reshape((B, N, C, H) + t.shape[3:]), 3, 1)

    qc = chunks(q) * DK ** -0.5
    kc, vc = chunks(k), chunks(v)
    gc = jnp.cumsum(chunks(g), axis=-1)
    bc = chunks(beta)
    incl = jnp.tril(jnp.ones((C, C), dtype=bool))
    strict = jnp.tril(jnp.ones((C, C), dtype=bool), -1)
    decay = jnp.exp(jnp.where(incl, gc[..., :, None] - gc[..., None, :], -jnp.inf))
    kb = kc * bc[..., None]
    vb = vc * bc[..., None]
    a_low = jnp.where(strict, jnp.einsum('bhncd,bhnsd->bhncs', kb, kc) * decay, 0.0)
    eye = jnp.eye(C, dtype=jnp.float32)
    t_inv = lax.linalg.triangular_solve(a_low + eye, jnp.broadcast_to(eye, a_low.shape),
                                        left_side=True, lower=True, unit_diagonal=True)
    u = jnp.einsum('bhncs,bhnse->bhnce', t_inv, vb)
    w = jnp.einsum('bhncs,bhnsd->bhncd', t_inv, kb * jnp.exp(gc)[..., None])
    qk = jnp.einsum('bhncd,bhnsd->bhncs', qc, kc) * decay
    qg = qc * jnp.exp(gc)[..., None]
    kd = kc * jnp.exp(gc[..., -1:] - gc)[..., None]
    g_last = jnp.exp(gc[..., -1])

    def step(state, xs):
        u_n, w_n, qk_n, qg_n, kd_n, gl_n = xs
        v_new = u_n - jnp.einsum('bhcd,bhde->bhce', w_n, state)
        o_n = jnp.einsum('bhcd,bhde->bhce', qg_n, state) + jnp.einsum('bhcs,bhse->bhce', qk_n, v_new)
        state = state * gl_n[..., None, None] + jnp.einsum('bhcd,bhce->bhde', kd_n, v_new)
        return state, o_n

    xs = tuple(jnp.moveaxis(t, 2, 0) for t in (u, w, qk, qg, kd, g_last))
    state0 = jnp.zeros((B, H, DK, DV), jnp.float32)
    _, o = lax.scan(step, state0, xs)
    return jnp.transpose(o, (1, 0, 3, 2, 4)).reshape(B, S, H, DV)

def dsa_sparse_attention(q, k, v, q_idx, k_idx, w_idx, topk):
    B, S, HQ, DH = q.shape
    HKV = k.shape[2]
    G = HQ // HKV
    scale = DH ** -0.5
    kpos = jnp.arange(S)
    qpos = jnp.arange(S).reshape(S // Q_BLOCK, Q_BLOCK)
    bidx = jnp.arange(B)[:, None, None]

    def one_block(blk):
        qb, qib, wb, pb = blk
        rel = jax.nn.relu(jnp.einsum('bthd,bsd->bths', qib, k_idx).astype(jnp.float32))
        score = jnp.einsum('bth,bths->bts', wb.astype(jnp.float32), rel)
        score = jnp.where(kpos[None, None, :] <= pb[None, :, None], score, -jnp.inf)
        _, sel = lax.top_k(score, topk)
        valid = sel <= pb[None, :, None]
        k_sel = k[bidx, sel]
        v_sel = v[bidx, sel]
        qg = qb.reshape(B, Q_BLOCK, HKV, G, DH)
        s = jnp.einsum('btngd,btjnd->btngj', qg, k_sel).astype(jnp.float32) * scale
        s = jnp.where(valid[:, :, None, None, :], s, -jnp.inf)
        pr = jax.nn.softmax(s, axis=-1).astype(v.dtype)
        o = jnp.einsum('btngj,btjnd->btngd', pr, v_sel)
        return o.reshape(B, Q_BLOCK, HQ, DH)

    out = lax.map(one_block, (to_blocks(q), to_blocks(q_idx), to_blocks(w_idx), qpos))
    return from_blocks(out)

def even_mixer(h, w_in, q_a_norm, w_q_up, kv_a_norm, w_kv_up, q_norm, k_norm,
               conv_w, a_log, dt_bias, out_norm, w_out):
    B, S, _ = h.shape
    c_q, c_kv, k_pe, qkv, z, a, b = split_last(
        h @ w_in, [MLA_Q_LORA, MLA_KV_LORA, MLA_ROPE, GDN_CONV_CH, GDN_VW, GDN_HEADS, GDN_HEADS])
    pos = jnp.arange(S)
    q = (rms_norm(c_q, q_a_norm) @ w_q_up).reshape(B, S, MLA_HEADS, MLA_QK)
    kv = (rms_norm(c_kv, kv_a_norm) @ w_kv_up).reshape(B, S, MLA_HEADS, MLA_NOPE + MLA_V)
    k_nope, v = kv[..., :MLA_NOPE], kv[..., MLA_NOPE:]
    k = jnp.concatenate([k_nope, jnp.broadcast_to(k_pe[:, :, None, :], (B, S, MLA_HEADS, MLA_ROPE))], axis=-1)
    q = rope_tail(rms_norm(q, q_norm), pos)
    k = rope_tail(rms_norm(k, k_norm), pos)
    o_a = causal_attention(q, k, v).reshape(B, S, MLA_HEADS * MLA_V)
    qkv = jax.nn.silu(causal_depthwise_conv(qkv, conv_w)).astype(jnp.float32)
    gq, gk, gv = split_last(qkv, [GDN_KW, GDN_KW, GDN_VW])
    gq = l2_norm(gq.reshape(B, S, GDN_HEADS, GDN_DK))
    gk = l2_norm(gk.reshape(B, S, GDN_HEADS, GDN_DK))
    gv = gv.reshape(B, S, GDN_HEADS, GDN_DV)
    g = -jnp.exp(a_log.astype(jnp.float32)) * jax.nn.softplus(a.astype(jnp.float32) + dt_bias.astype(jnp.float32))
    beta = jax.nn.sigmoid(b.astype(jnp.float32))
    o_b = gated_delta_chunked(gq, gk, gv, g, beta)
    o_b = rms_norm(o_b, out_norm) * jax.nn.silu(z.astype(jnp.float32).reshape(B, S, GDN_HEADS, GDN_DV))
    o_b = o_b.reshape(B, S, GDN_VW).astype(h.dtype)
    return jnp.concatenate([o_a, o_b], axis=-1) @ w_out

def odd_mixer(h, w_in, q_norm, k_norm, kidx_norm, w_out):
    B, S, _ = h.shape
    q, k, v, q_idx, k_idx, w_idx = split_last(
        h @ w_in, [DSA_HEADS * DSA_HEAD_DIM, DSA_KV_HEADS * DSA_HEAD_DIM, DSA_KV_HEADS * DSA_HEAD_DIM,
                   IDX_HEADS * IDX_DIM, IDX_DIM, IDX_HEADS])
    q = rms_norm(q.reshape(B, S, DSA_HEADS, DSA_HEAD_DIM), q_norm)
    k = rms_norm(k.reshape(B, S, DSA_KV_HEADS, DSA_HEAD_DIM), k_norm)
    v = v.reshape(B, S, DSA_KV_HEADS, DSA_HEAD_DIM)
    q_idx = q_idx.reshape(B, S, IDX_HEADS, IDX_DIM)
    k_idx = rms_norm(k_idx, kidx_norm)
    topk = min(DSA_TOPK, S // 4)
    o = dsa_sparse_attention(q, k, v, q_idx, k_idx, w_idx, topk)
    return o.reshape(B, S, ODD_OUT) @ w_out

def first_inputs(seed: int = 0) -> dict:
    key = jax.random.key(seed)
    keys = jax.random.split(key, 40)
    ctr = iter(range(40))
    ne = (DEPTH + 1) // 2
    no = DEPTH // 2

    def nk():
        return keys[next(ctr)]

    def w(shape, fan_in):
        return jax.random.normal(nk(), shape, jnp.float32) * fan_in ** -0.5

    def gain(shape):
        return 1.0 + 0.02 * jax.random.normal(nk(), shape, jnp.float32)

    x = jax.random.normal(nk(), (BATCH, SEQ, D_MODEL), jnp.float32)
    p = jax.random.normal(nk(), (DEPTH, BATCH, SEQ, PLE_DIM), jnp.float32)
    a_log = jnp.log(jax.random.uniform(nk(), (ne, GDN_HEADS), jnp.float32, 1.0, 16.0))
    dt = jnp.exp(jax.random.uniform(nk(), (ne, GDN_HEADS), jnp.float32, math.log(1e-3), math.log(1e-1)))
    dt_bias = dt + jnp.log(-jnp.expm1(-dt))
    return {
        'x': x,
        'p': p,
        'ln_ffn1': gain((DEPTH, D_MODEL)),
        'ffn1_w_gu': w((DEPTH, D_MODEL, 2 * D_FF), D_MODEL),
        'ffn1_w_down': w((DEPTH, D_FF, D_MODEL), D_FF),
        'ln_mix': gain((DEPTH, D_MODEL)),
        'even_w_in': w((ne, D_MODEL, EVEN_IN), D_MODEL),
        'mla_q_a_norm': gain((ne, MLA_Q_LORA)),
        'mla_w_q_up': w((ne, MLA_Q_LORA, MLA_HEADS * MLA_QK), MLA_Q_LORA),
        'mla_kv_a_norm': gain((ne, MLA_KV_LORA)),
        'mla_w_kv_up': w((ne, MLA_KV_LORA, MLA_HEADS * (MLA_NOPE + MLA_V)), MLA_KV_LORA),
        'mla_q_norm': gain((ne, MLA_QK)),
        'mla_k_norm': gain((ne, MLA_QK)),
        'gdn_conv_w': w((ne, GDN_CONV, GDN_CONV_CH), GDN_CONV),
        'gdn_a_log': a_log,
        'gdn_dt_bias': dt_bias,
        'gdn_out_norm': gain((ne, GDN_DV)),
        'even_w_out': w((ne, EVEN_OUT, D_MODEL), EVEN_OUT),
        'odd_w_in': w((no, D_MODEL, ODD_IN), D_MODEL),
        'dsa_q_norm': gain((no, DSA_HEAD_DIM)),
        'dsa_k_norm': gain((no, DSA_HEAD_DIM)),
        'dsa_kidx_norm': gain((no, IDX_DIM)),
        'odd_w_out': w((no, ODD_OUT, D_MODEL), ODD_OUT),
        'ln_ffn2': gain((DEPTH, D_MODEL)),
        'ffn2_w_gu': w((DEPTH, D_MODEL, 2 * D_FF), D_MODEL),
        'ffn2_w_down': w((DEPTH, D_FF, D_MODEL), D_FF),
        'ln_ple': gain((DEPTH, D_MODEL)),
        'ple_w_in': w((DEPTH, PLE_DIM, D_MODEL), PLE_DIM),
        'ple_w_gate': w((DEPTH, D_MODEL, D_MODEL), D_MODEL),
    }

def first_block(x, p, ln_ffn1, ffn1_w_gu, ffn1_w_down, ln_mix, even_w_in, mla_q_a_norm, mla_w_q_up,
              mla_kv_a_norm, mla_w_kv_up, mla_q_norm, mla_k_norm, gdn_conv_w, gdn_a_log, gdn_dt_bias,
              gdn_out_norm, even_w_out, odd_w_in, dsa_q_norm, dsa_k_norm, dsa_kidx_norm, odd_w_out,
              ln_ffn2, ffn2_w_gu, ffn2_w_down, ln_ple, ple_w_in, ple_w_gate):
    for i in range(DEPTH):
        j = i // 2
        x = x + 0.5 * swiglu(rms_norm(x, ln_ffn1[i]), ffn1_w_gu[i], ffn1_w_down[i])
        h = rms_norm(x, ln_mix[i])
        if i % 2 == 0:
            x = x + even_mixer(h, even_w_in[j], mla_q_a_norm[j], mla_w_q_up[j], mla_kv_a_norm[j],
                               mla_w_kv_up[j], mla_q_norm[j], mla_k_norm[j], gdn_conv_w[j], gdn_a_log[j],
                               gdn_dt_bias[j], gdn_out_norm[j], even_w_out[j])
        else:
            x = x + odd_mixer(h, odd_w_in[j], dsa_q_norm[j], dsa_k_norm[j], dsa_kidx_norm[j], odd_w_out[j])
        x = x + 0.5 * swiglu(rms_norm(x, ln_ffn2[i]), ffn2_w_gu[i], ffn2_w_down[i])
        gate = jax.nn.sigmoid(rms_norm(x, ln_ple[i]) @ ple_w_gate[i])
        x = x + gate * (p[i] @ ple_w_in[i])
    return x


DEPTH_2 = 1

CHUNK = 64
D_A = D_MODEL
CONV_A = 3
D_B = D_MODEL
LRU_HEADS = 16
LRU_BW = D_B // LRU_HEADS
CONV_B = 4
LRU_C = 8.0
D_C = D_MODEL
RWKV_HEAD = 64
RWKV_HEADS = D_C // RWKV_HEAD
R_W = 64
R_A = 64
R_V = 32
R_G = 128
LNX_EPS = RWKV_HEAD * 1e-5
D_FF_2 = 4 * D_MODEL
N_BRANCH = 3
COLS_A = 3 * D_A
COLS_B = 2 * D_B
COLS_GATE = N_BRANCH * D_MODEL
COLS_C = 3 * D_C + R_W + R_A + R_G
N_IN = COLS_A + COLS_B + COLS_GATE + COLS_C


def _split(t, sizes):
    out, o = [], 0
    for s in sizes:
        out.append(t[..., o:o + s])
        o += s
    return out

def rms_norm_2(x, g):
    xf = x.astype(jnp.float32)
    y = xf * lax.rsqrt(jnp.mean(xf * xf, axis=-1, keepdims=True) + EPS)
    return (y * g.astype(jnp.float32)).astype(x.dtype)

def causal_dwconv(x, w, b=None):
    K = w.shape[0]
    S = x.shape[1]
    xp = jnp.pad(x, ((0, 0), (K - 1, 0), (0, 0)))
    y = xp[:, K - 1:K - 1 + S] * w[K - 1]
    for j in range(K - 1):
        y = y + xp[:, j:j + S] * w[j]
    return y if b is None else y + b

def token_shift(p, mu):
    prev = jnp.pad(p, ((0, 0), (1, 0), (0, 0)))[:, :-1]
    return p + (prev - p) * mu

def rg_lru(x, w_a, b_a, w_i, b_i, a_param):
    Bsz, S, C = x.shape
    f32 = jnp.float32
    xb = x.reshape(Bsz, S, LRU_HEADS, LRU_BW)
    gate_a = jax.nn.sigmoid((jnp.einsum('bshi,hij->bshj', xb, w_a).reshape(Bsz, S, C) + b_a).astype(f32))
    gate_i = jax.nn.sigmoid((jnp.einsum('bshi,hij->bshj', xb, w_i).reshape(Bsz, S, C) + b_i).astype(f32))
    log_a = -LRU_C * gate_a * jax.nn.softplus(a_param.astype(f32))
    a = jnp.exp(log_a)
    mult = jnp.sqrt(-jnp.expm1(2.0 * log_a))
    mult = jnp.where(jnp.arange(S)[None, :, None] == 0, 1.0, mult)
    u = x.astype(f32) * gate_i * mult

    def combine(left, right):
        a_l, u_l = left
        a_r, u_r = right
        return a_l * a_r, a_r * u_l + u_r

    _, h = lax.associative_scan(combine, (a, u), axis=1)
    return h.astype(x.dtype)

def rwkv7_recurrence(r, decay, k, v, kk, a):
    Bsz, S, H, N = r.shape
    nc = S // CHUNK

    def to_chunks(t):
        return t.reshape(Bsz, nc, CHUNK, H, N).transpose(1, 2, 0, 3, 4)

    def step(state, inp):
        r_t, w_t, k_t, v_t, kk_t, a_t = inp
        sa = jnp.einsum('bhvk,bhk->bhv', state, -kk_t)
        state = (state * w_t[:, :, None, :]
                 + sa[..., None] * (kk_t * a_t)[:, :, None, :]
                 + v_t[..., None] * k_t[:, :, None, :])
        y_t = jnp.einsum('bhvk,bhk->bhv', state, r_t)
        return state, y_t

    def chunk_step(state, chunk_inp):
        return lax.scan(step, state, chunk_inp)

    state0 = jnp.zeros((Bsz, H, N, N), jnp.float32)
    inputs = (to_chunks(r), to_chunks(decay), to_chunks(k), to_chunks(v), to_chunks(kk), to_chunks(a))
    _, y = lax.scan(chunk_step, state0, inputs)
    return y.transpose(2, 0, 1, 3, 4).reshape(Bsz, S, H, N)

def rwkv7_mix(pc, h, v_first, w0, w2, a0, a2, g2, k_k, k_a, r_k, lnx_g, lnx_b, vres):
    f32 = jnp.float32
    r, k, v, xw, xa, xg = _split(pc, (D_C, D_C, D_C, R_W, R_A, R_G))
    w_log = -jax.nn.softplus(-(w0 + jnp.tanh(xw) @ w2).astype(f32)) - 0.5
    decay = jnp.exp(-jnp.exp(w_log))
    if vres is None:
        v_first = v
    else:
        v0, v1, v2 = vres
        v = v + (v_first - v) * jax.nn.sigmoid(v0 + (h @ v1) @ v2)
    a = jax.nn.sigmoid(a0 + xa @ a2)
    g = jax.nn.sigmoid(xg) @ g2

    def heads(t):
        return t.reshape(t.shape[:-1] + (RWKV_HEADS, RWKV_HEAD)).astype(f32)

    kk = heads(k * k_k)
    kk = kk / jnp.maximum(jnp.sqrt(jnp.sum(kk * kk, axis=-1, keepdims=True)), 1e-12)
    k = k * (1.0 + (a - 1.0) * k_a)
    rh, kh, vh, ah = heads(r), heads(k), heads(v), heads(a)
    y = rwkv7_recurrence(rh, heads(decay), kh, vh, kk, ah)
    mu = jnp.mean(y, axis=-1, keepdims=True)
    var = jnp.mean(jnp.square(y - mu), axis=-1, keepdims=True)
    y = (y - mu) * lax.rsqrt(var + LNX_EPS)
    y = y + jnp.sum(rh * kh * r_k.astype(f32), axis=-1, keepdims=True) * vh
    y = y.reshape(y.shape[:2] + (D_C,))
    return y, g, v_first

def second_inputs(seed: int = 0) -> dict:
    key = jax.random.key(seed)
    ks = iter(jax.random.split(key, 48))
    L = DEPTH_2

    def nrm(shape, scale):
        return jax.random.normal(next(ks), shape, jnp.float32) * scale

    def uni(shape, lo, hi):
        return jax.random.uniform(next(ks), shape, jnp.float32, lo, hi)

    rad = uni((L, D_B), 0.9, 0.999)
    lru_a_param = jnp.log(jnp.expm1(-jnp.log(rad)))
    LV = max(L - 1, 0)
    return {
        "x": nrm((BATCH, SEQ, D_MODEL), 1.0),
        "norm1_g": 1.0 + nrm((L, D_MODEL), 0.05),
        "w_in": nrm((L, D_MODEL, N_IN), D_MODEL ** -0.5),
        "merge_b": nrm((L, COLS_GATE), 0.01),
        "conv_a_w": nrm((L, CONV_A, D_A), CONV_A ** -0.5),
        "lru_conv_w": nrm((L, CONV_B, D_B), CONV_B ** -0.5),
        "lru_conv_b": nrm((L, D_B), 0.01),
        "lru_wa": nrm((L, LRU_HEADS, LRU_BW, LRU_BW), LRU_BW ** -0.5),
        "lru_ba": nrm((L, D_B), 0.01),
        "lru_wi": nrm((L, LRU_HEADS, LRU_BW, LRU_BW), LRU_BW ** -0.5),
        "lru_bi": nrm((L, D_B), 0.01),
        "lru_a_param": lru_a_param,
        "rwkv_mu": uni((L, COLS_C), 0.0, 1.0),
        "rwkv_w0": uni((L, D_C), -6.0, 1.0),
        "rwkv_w2": nrm((L, R_W, D_C), 0.1 * R_W ** -0.5),
        "rwkv_a0": nrm((L, D_C), 0.1),
        "rwkv_a2": nrm((L, R_A, D_C), 0.1 * R_A ** -0.5),
        "rwkv_g2": nrm((L, R_G, D_C), R_G ** -0.5),
        "rwkv_kk": 0.85 + nrm((L, D_C), 0.05),
        "rwkv_ka": 1.0 + nrm((L, D_C), 0.05),
        "rwkv_rk": nrm((L, RWKV_HEADS, RWKV_HEAD), 0.1),
        "rwkv_lnx_g": 1.0 + nrm((L, D_C), 0.05),
        "rwkv_lnx_b": nrm((L, D_C), 0.01),
        "rwkv_v0": 1.0 + nrm((LV, D_C), 0.1),
        "rwkv_v1": nrm((LV, D_MODEL, R_V), D_MODEL ** -0.5),
        "rwkv_v2": nrm((LV, R_V, D_C), 0.1 * R_V ** -0.5),
        "w_out": nrm((L, D_MODEL, D_MODEL), D_MODEL ** -0.5),
        "norm2_g": 1.0 + nrm((L, D_MODEL), 0.05),
        "mlp_w1": nrm((L, D_MODEL, D_FF_2), D_MODEL ** -0.5),
        "mlp_w2": nrm((L, D_FF_2, D_MODEL), D_FF_2 ** -0.5),
        "final_g": 1.0 + nrm((D_MODEL,), 0.05),
    }

def second_block(x, norm1_g, w_in, merge_b, conv_a_w, lru_conv_w, lru_conv_b, lru_wa, lru_ba, lru_wi,
              lru_bi, lru_a_param, rwkv_mu, rwkv_w0, rwkv_w2, rwkv_a0, rwkv_a2, rwkv_g2, rwkv_kk,
              rwkv_ka, rwkv_rk, rwkv_lnx_g, rwkv_lnx_b, rwkv_v0, rwkv_v1, rwkv_v2, w_out, norm2_g,
              mlp_w1, mlp_w2, final_g):
    v_first = None
    for l in range(DEPTH_2):
        h = rms_norm_2(x, norm1_g[l])
        p = h @ w_in[l]
        pa, pb, pg, pc = _split(p, (COLS_A, COLS_B, COLS_GATE, COLS_C))

        b_a, c_a, x_a = _split(pa, (D_A, D_A, D_A))
        y_a = b_a * causal_dwconv(c_a * x_a, conv_a_w[l])

        x_b, g_b = _split(pb, (D_B, D_B))
        u = causal_dwconv(x_b, lru_conv_w[l], lru_conv_b[l])
        y_b = rg_lru(u, lru_wa[l], lru_ba[l], lru_wi[l], lru_bi[l], lru_a_param[l]) * jax.nn.gelu(g_b, approximate=True)

        pc = token_shift(pc, rwkv_mu[l])
        vres = None if l == 0 else (rwkv_v0[l - 1], rwkv_v1[l - 1], rwkv_v2[l - 1])
        f32 = jnp.float32
        r, k, v, xw, xa, xg = _split(pc, (D_C, D_C, D_C, R_W, R_A, R_G))
        w_log = -jax.nn.softplus(-(rwkv_w0[l] + jnp.tanh(xw) @ rwkv_w2[l]).astype(f32)) - 0.5
        decay = jnp.exp(-jnp.exp(w_log))
        if vres is None:
            v_first = v
        else:
            v0, v1, v2 = vres
            v = v + (v_first - v) * jax.nn.sigmoid(v0 + (h @ v1) @ v2)
        a = jax.nn.sigmoid(rwkv_a0[l] + xa @ rwkv_a2[l])
        g_c = jax.nn.sigmoid(xg) @ rwkv_g2[l]
        hs = x.shape[:2] + (RWKV_HEADS, RWKV_HEAD)
        kk = (k * rwkv_kk[l]).astype(f32).reshape(hs)
        kk = kk / jnp.maximum(jnp.sqrt(jnp.sum(kk * kk, axis=-1, keepdims=True)), 1e-12)
        k = k * (1.0 + (a - 1.0) * rwkv_ka[l])
        rh = r.astype(f32).reshape(hs)
        kh = k.astype(f32).reshape(hs)
        vh = v.astype(f32).reshape(hs)
        ah = a.astype(f32).reshape(hs)
        yc = rwkv7_recurrence(rh, decay.reshape(hs), kh, vh, kk, ah)
        mu = jnp.mean(yc, axis=-1, keepdims=True)
        var = jnp.mean(jnp.square(yc - mu), axis=-1, keepdims=True)
        yc = ((yc - mu) * lax.rsqrt(var + LNX_EPS)).reshape(x.shape[:2] + (D_C,))
        yc = yc * rwkv_lnx_g[l].astype(f32) + rwkv_lnx_b[l].astype(f32)
        bonus = jnp.sum(rh * kh * rwkv_rk[l].astype(f32), axis=-1, keepdims=True) * vh
        yc = yc + bonus.reshape(x.shape[:2] + (D_C,))
        y_c = (yc * g_c.astype(f32)).astype(x.dtype)

        gate_a, gate_b, gate_c = _split(jax.nn.sigmoid(pg + merge_b[l]), (D_MODEL, D_MODEL, D_MODEL))
        m = gate_a * y_a + gate_b * y_b + gate_c * y_c
        x = x + m @ w_out[l]

        h2 = rms_norm_2(x, norm2_g[l])
        x = x + jnp.square(jax.nn.relu(h2 @ mlp_w1[l])) @ mlp_w2[l]
    return rms_norm_2(x, final_g)


def setup_inputs(seed=0):
    out = dict(first_inputs(seed))
    for name, value in second_inputs(seed + 1).items():
        if name != "x":
            out[name + "_2"] = value
    return out


def reference(
    x, p, ln_ffn1, ffn1_w_gu, ffn1_w_down, ln_mix, even_w_in, mla_q_a_norm, mla_w_q_up,
    mla_kv_a_norm, mla_w_kv_up, mla_q_norm, mla_k_norm, gdn_conv_w, gdn_a_log, gdn_dt_bias,
    gdn_out_norm, even_w_out, odd_w_in, dsa_q_norm, dsa_k_norm, dsa_kidx_norm, odd_w_out,
    ln_ffn2, ffn2_w_gu, ffn2_w_down, ln_ple, ple_w_in, ple_w_gate, norm1_g_2, w_in_2, merge_b_2,
    conv_a_w_2, lru_conv_w_2, lru_conv_b_2, lru_wa_2, lru_ba_2, lru_wi_2, lru_bi_2,
    lru_a_param_2, rwkv_mu_2, rwkv_w0_2, rwkv_w2_2, rwkv_a0_2, rwkv_a2_2, rwkv_g2_2, rwkv_kk_2,
    rwkv_ka_2, rwkv_rk_2, rwkv_lnx_g_2, rwkv_lnx_b_2, rwkv_v0_2, rwkv_v1_2, rwkv_v2_2, w_out_2,
    norm2_g_2, mlp_w1_2, mlp_w2_2, final_g_2,
):
    x = first_block(
        x, p, ln_ffn1, ffn1_w_gu, ffn1_w_down, ln_mix, even_w_in, mla_q_a_norm, mla_w_q_up,
        mla_kv_a_norm, mla_w_kv_up, mla_q_norm, mla_k_norm, gdn_conv_w, gdn_a_log, gdn_dt_bias,
        gdn_out_norm, even_w_out, odd_w_in, dsa_q_norm, dsa_k_norm, dsa_kidx_norm, odd_w_out,
        ln_ffn2, ffn2_w_gu, ffn2_w_down, ln_ple, ple_w_in, ple_w_gate,
    )
    return second_block(
        x, norm1_g_2, w_in_2, merge_b_2, conv_a_w_2, lru_conv_w_2, lru_conv_b_2, lru_wa_2,
        lru_ba_2, lru_wi_2, lru_bi_2, lru_a_param_2, rwkv_mu_2, rwkv_w0_2, rwkv_w2_2, rwkv_a0_2,
        rwkv_a2_2, rwkv_g2_2, rwkv_kk_2, rwkv_ka_2, rwkv_rk_2, rwkv_lnx_g_2, rwkv_lnx_b_2,
        rwkv_v0_2, rwkv_v1_2, rwkv_v2_2, w_out_2, norm2_g_2, mlp_w1_2, mlp_w2_2, final_g_2,
    )


_drawn_inputs = setup_inputs


def setup_inputs(seed=0):
    import zlib

    import numpy as np

    out = dict(_drawn_inputs(seed))
    spreads = {}
    factors = {'ln_ffn1': 2.765,
     'mla_q_a_norm': 7.411,
     'mla_kv_a_norm': 5.783,
     'mla_q_norm': 6.294,
     'mla_k_norm': 6.507,
     'gdn_out_norm': 3.519,
     'dsa_q_norm': 24.041,
     'dsa_k_norm': 23.803,
     'dsa_kidx_norm': 10.585,
     'ln_ffn2': 3.251,
     'ln_ple': 25.818,
     'merge_b_2': 63.698,
     'lru_conv_b_2': 200.0,
     'lru_ba_2': 200.0,
     'lru_bi_2': 200.0,
     'rwkv_w2_2': 46.566,
     'rwkv_a0_2': 6.18,
     'rwkv_a2_2': 6.927,
     'rwkv_kk_2': 157.205,
     'rwkv_ka_2': 14.56,
     'rwkv_lnx_g_2': 32.749,
     'rwkv_lnx_b_2': 200.0,
     'lru_wa_2': 64.0,
     'lru_wi_2': 26.028,
     'lru_a_param_2': 46.992,
     'norm2_g_2': 6.411,
     'lru_conv_w_2': 4.408}
    for name, (base, spread) in spreads.items():
        noise = np.random.default_rng([zlib.crc32(name.encode()), seed]).standard_normal(out[name].shape)
        drawn = base * np.exp(spread * noise) if base else spread * noise
        out[name] = jnp.asarray(drawn.astype(out[name].dtype))
    for name, factor in factors.items():
        out[name] = (out[name] * factor).astype(out[name].dtype)
    return out
```

```python
import numpy as np
import concourse.bass as bass
from concourse import mybir
from contextlib import ExitStack

T, P, D = 256, 128, 1024
KT = D // P
NB = T // P
UNIT = 8 * P
RING = 6
D_FF, D_FF2 = 2816, 4096
FJ, FJ2 = D_FF // P, D_FF2 // P
EPS = 1e-6
NEG, TAKEN = -1e30, -3e38
MLA_H, MLA_QK, MLA_NOPE, MLA_V = 8, 96, 64, 64
GH, GD = 4, 128
DSA_H, DSA_KV, IDX_H, IDX_D, TOPK = 8, 2, 8, 64, 64
RH, RN, RC = 16, 64, 64
LNX_EPS = RN * 1e-5
LOG_DECAY = -float(np.exp(np.float32(-0.5)))

STAGES = ["ffn0", "even", "ffn1", "ple0", "ffn2", "odd", "ffn3", "ple1", "second", "mlp"]
NORM_OF = {"ffn0": "ln_ffn1_0", "even": "ln_mix_0", "ffn1": "ln_ffn2_0", "ple0": "ln_ple_0",
           "ffn2": "ln_ffn1_1", "odd": "ln_mix_1", "ffn3": "ln_ffn2_1", "ple1": "ln_ple_1",
           "second": "norm1", "mlp": "norm2"}

PARAMS = [("ln_ffn1_0", 8), ("ln_mix_0", 8), ("ln_ffn2_0", 8), ("ln_ple_0", 8),
          ("ln_ffn1_1", 8), ("ln_mix_1", 8), ("ln_ffn2_1", 8), ("ln_ple_1", 8),
          ("norm1", 8), ("norm2", 8), ("final", 8),
          ("q_a", 3), ("kv_a", 2), ("mla_q", 1), ("mla_k", 1), ("gconv", 48),
          ("a_log", 1), ("dt_bias", 1), ("out_norm", 1),
          ("dsa_q", 1), ("dsa_k", 1), ("kidx", 1),
          ("merge_b", 24), ("conv_a", 24), ("lru_conv", 32), ("lru_cb", 8), ("lru_ba", 8),
          ("lru_bi", 8), ("lru_a", 8), ("mu", 26), ("w0", 8), ("a0", 8), ("kk", 8), ("ka", 8),
          ("rk", 8), ("lnx_g", 8), ("lnx_b", 8)]
CONSTS = [("ident", 128), ("ones", 128), ("pairs", 128), ("onehot", 31), ("onehot2", 30),
          ("sel", 16 * 128), ("sel2", 8 * 128), ("levels", 7 * 128), ("incl", 128), ("strict64", 128),
          ("incl64", 128), ("causal", 256), ("cos", 256), ("sin", 256), ("rot", 96), ("reset64", 256),
          ("rms", 8)]


def offsets(table):
    out, at = {}, 0
    for name, n in table:
        out[name] = (at, n)
        at += n
    return out, at


def shape_constants():
    off, n = offsets(CONSTS)
    c = np.zeros((P, n), np.float32)

    def put(name, a):
        at, _ = off[name]
        a = np.asarray(a, np.float32)
        c[:a.shape[0], at:at + a.shape[1]] = a
    p, i = np.arange(P)[:, None], np.arange(P)[None, :]
    put("ident", p == i)
    put("ones", np.ones((P, P)))
    put("pairs", p // 64 == i // 64)
    oh = np.zeros((P, 31)); oh[:, 15] = 1
    put("onehot", oh)
    oh2 = np.zeros((P, 30)); oh2[:64, 14] = 1; oh2[64:, 15] = 1
    put("onehot2", oh2)
    sel = np.zeros((P, 16, P))
    for n_ in range(16):
        sel[n_, n_], sel[32 + n_, n_] = 1, 1
    put("sel", sel.reshape(P, -1))
    sel2 = np.zeros((P, 8, P))
    for t in range(8):
        sel2[2 * t, t, :64], sel2[2 * t + 1, t, 64:] = 1, 1
    put("sel2", sel2.reshape(P, -1))
    lv = [(p // (2 * b) == i // (2 * b)) & ((i // b) % 2 == 1) & ((p // b) % 2 == 0)
          for b in (1, 2, 4, 8, 16, 32, 64)]
    put("levels", np.concatenate(lv, 1))
    put("incl", p <= i)
    put("strict64", (p < i) & (p // 64 == i // 64))
    put("incl64", (p <= i) & (p // 64 == i // 64))
    put("causal", np.concatenate([np.zeros((P, P)), np.where(i <= p, 0, NEG)], 1))
    half = 16
    inv = (np.float32(10000.0) ** (-np.arange(half, dtype=np.float32) / np.float32(half))).astype(np.float32)
    ang = (np.arange(T, dtype=np.float32)[None, :] * inv[:, None]).astype(np.float32)
    cos, sin = np.ones((96, T)), np.zeros((96, T))
    cos[64:80], cos[80:96], sin[64:80], sin[80:96] = np.cos(ang), np.cos(ang), np.sin(ang), np.sin(ang)
    put("cos", cos)
    put("sin", sin)
    rot = np.zeros((96, 96))
    for m in range(16):
        rot[80 + m, 64 + m], rot[64 + m, 80 + m] = -1, 1
    put("rot", rot)
    put("reset64", np.tile(np.arange(T) % RC != 0, (P, 1)))
    rms = np.zeros((P, 8), np.float32)
    rms[:, 0], rms[:, 1] = 1.0, EPS
    rms[0, 0], rms[1, 0] = 1 / 384, 1 / 256
    rms[:, 2], rms[:, 3] = 1 / 96, EPS
    rms[:, 4], rms[:, 5] = 1 / 128, EPS
    rms[10, 4] = 1 / 64
    rms[:, 6], rms[:, 7] = 1 / 64, LNX_EPS
    put("rms", rms)
    return c


def columns(v):
    v = np.asarray(v).reshape(-1)
    pad = np.zeros(-(-v.size // P) * P, v.dtype)
    pad[:v.size] = v
    return pad.reshape(-1, P).T


def parameter_columns(a):
    off, n = offsets(PARAMS)
    out = np.zeros((P, n), np.float32)

    def put(name, c):
        at, w = off[name]
        assert c.shape[1] == w, name
        out[:c.shape[0], at:at + w] = c
    for l in range(2):
        for name in ("ln_ffn1", "ln_mix", "ln_ffn2", "ln_ple"):
            put(f"{name}_{l}", columns(a[name][l]))
    put("norm1", columns(a["norm1_g_2"][0]))
    put("norm2", columns(a["norm2_g_2"][0]))
    put("final", columns(a["final_g_2"]))
    put("q_a", columns(a["mla_q_a_norm"][0]))
    put("kv_a", columns(a["mla_kv_a_norm"][0]))
    put("mla_q", columns(a["mla_q_norm"][0]))
    put("mla_k", columns(a["mla_k_norm"][0]))
    put("gconv", np.concatenate([columns(a["gdn_conv_w"][0][j]) for j in range(4)], 1))
    put("a_log", columns(a["gdn_a_log"][0]))
    put("dt_bias", columns(a["gdn_dt_bias"][0]))
    put("out_norm", columns(a["gdn_out_norm"][0]))
    put("dsa_q", columns(a["dsa_q_norm"][0]))
    put("dsa_k", columns(a["dsa_k_norm"][0]))
    put("kidx", columns(np.tile(a["dsa_kidx_norm"][0], 2)))
    put("merge_b", columns(a["merge_b_2"][0]))
    put("conv_a", np.concatenate([columns(a["conv_a_w_2"][0][j]) for j in range(3)], 1))
    put("lru_conv", np.concatenate([columns(a["lru_conv_w_2"][0][j]) for j in range(4)], 1))
    for name, src in (("lru_cb", "lru_conv_b_2"), ("lru_ba", "lru_ba_2"), ("lru_bi", "lru_bi_2"),
                      ("lru_a", "lru_a_param_2"), ("mu", "rwkv_mu_2"), ("w0", "rwkv_w0_2"),
                      ("a0", "rwkv_a0_2"), ("kk", "rwkv_kk_2"), ("ka", "rwkv_ka_2"), ("rk", "rwkv_rk_2"),
                      ("lnx_g", "rwkv_lnx_g_2"), ("lnx_b", "rwkv_lnx_b_2")):
        put(name, columns(a[src][0]))
    return out


def as_unit(m):
    u = np.zeros((P, UNIT), m.dtype)
    k = m.shape[0] // P
    u[:, :k * P] = m.reshape(k, P, P).transpose(1, 0, 2).reshape(P, k * P)
    return u


def tiles_unit(tiles):
    u = np.zeros((P, UNIT), np.float32)
    for i, m in enumerate(tiles):
        u[:m.shape[0], i * P:i * P + m.shape[1]] = m
    return u


def placed(w, parts):
    out = np.zeros((w.shape[0], P), w.dtype)
    for at, first, n in parts:
        out[:, at:at + n] = w[:, first:first + n]
    return out


def col_units(w, first, n):
    return [as_unit(w[:, first + i * P:first + (i + 1) * P]) for i in range(n)]


def ffn_units(gu, down, width, gated):
    out, n = [], width // P
    for j in range(n + 1):
        if j < n:
            out += col_units(gu, j * P, 1)
            if gated:
                out += col_units(gu, width + j * P, 1)
        if j >= 1:
            out.append(np.ascontiguousarray(down[(j - 1) * P:j * P]))
    return out


def stage_units(name, a):
    if name.startswith("ffn"):
        k = int(name[3])
        pre = ("ffn1", "ffn2")[k % 2]
        return ffn_units(a[pre + "_w_gu"][k // 2], a[pre + "_w_down"][k // 2], D_FF, True)
    if name.startswith("ple"):
        l = int(name[3])
        pin = a["ple_w_in"][l]
        return [tiles_unit([pin[k * P:(k + 1) * P, m * P:(m + 1) * P] for m in range(4 * g, 4 * g + 4)
                            for k in range(2)]) for g in range(2)] + col_units(a["ple_w_gate"][l], 0, 8)
    if name == "even":
        w = a["even_w_in"][0]
        out = col_units(w, 0, 5)
        ab = 640 + 32 + 1536 + 512
        out.append(as_unit(placed(w, [(0, ab, 4), (32, ab + 4, 4), (64, 640, 32)])))
        out += col_units(w, 672, 16)
        q, kv = a["mla_w_q_up"][0], a["mla_w_kv_up"][0]
        qt = [q[k * P:(k + 1) * P, h * 96:(h + 1) * 96] for h in range(8) for k in range(3)]
        out += [tiles_unit(qt[8 * i:8 * i + 8]) for i in range(3)]
        kv = kv.reshape(256, 8, 128)
        kn = kv[:, :, :64].reshape(256, 512)
        out.append(tiles_unit([kn[k * P:(k + 1) * P, m * P:(m + 1) * P] for m in range(4) for k in range(2)]))
        vv = kv[:, :, 64:].reshape(256, 512)
        out.append(np.concatenate([vv[:P], vv[P:]], 1))
        return out + col_units(a["even_w_out"][0], 0, 8)
    if name == "odd":
        w = a["odd_w_in"][0]
        out = col_units(w, 0, 10)
        ki = 1024 + 512 + 512
        out.append(as_unit(placed(w, [(0, ki, 64), (64, ki, 64)])))
        out += col_units(w, 1536, 4)
        vw = np.concatenate([w[:, 1280:1536], w[:, ki + 64:ki + 72]], 1).reshape(8, P, 264)
        for ks in ((0, 1, 2), (3, 4, 5), (6, 7)):
            u = np.zeros((P, UNIT), w.dtype)
            for n, k in enumerate(ks):
                u[:, n * 264:(n + 1) * 264] = vw[k]
            out.append(u)
        return out + col_units(a["odd_w_out"][0], 0, 8)
    if name == "second":
        w = a["w_in_2"][0]
        base_c = 3 * D + 2 * D + 3 * D
        out = col_units(w, base_c + 3 * D, 2)
        wa, wi = a["lru_wa_2"][0], a["lru_wi_2"][0]
        for t in range(8):
            cols = [D, 2 * D, 0, 5 * D, 3 * D, 4 * D, 6 * D, None, base_c, base_c + D, base_c + 2 * D, 7 * D]
            for c in cols:
                if c is not None:
                    out += col_units(w, c + t * P, 1)
                    continue
                s = slice(t * P, (t + 1) * P)
                u = np.zeros((P, UNIT), w.dtype)
                u[:64, 0:64], u[64:, 64:128] = wa[2 * t], wa[2 * t + 1]
                u[:64, 128:192], u[64:, 192:256] = wi[2 * t], wi[2 * t + 1]
                u[:64, 256:384] = a["rwkv_w2_2"][0][:, s]
                u[64:, 384:512] = a["rwkv_a2_2"][0][:, s]
                u[:, 512:640] = a["rwkv_g2_2"][0][:, s]
                out.append(u)
        return out + col_units(a["w_out_2"][0], 0, 8)
    assert name == "mlp"
    return ffn_units(a["mlp_w1_2"][0], a["mlp_w2_2"][0], D_FF2, False)


UNITS_OF = {"ffn": 3 * FJ, "ple": 10, "eve": 22 + 5 + 8, "odd": 18 + 8, "sec": 2 + 96 + 8, "mlp": 2 * FJ2}


class Steps:

    def __init__(self, sem, names):
        self.sem, self.names, self.n = sem, list(names), 0
        assert len(set(self.names)) == len(self.names)

    def step(self, name):
        assert self.names[self.n] == name, (name, self.names[self.n])
        self.n += 1
        return 1

    def after(self, name):
        return self.names.index(name) + 1


def build(nc, a_x, a_p, a_w, a_par, a_con, out, stages=STAGES):
    f32 = mybir.dt.float32
    ALU, ACT, AX = mybir.AluOpType, mybir.ActivationFunctionType, mybir.AxisListType
    MUL, ADD, SUB, MAXOP, MINOP = ALU.mult, ALU.add, ALU.subtract, ALU.max, ALU.min
    par_off, par_n = offsets(PARAMS)
    con_off, con_n = offsets(CONSTS)
    unit_base, total_units = {}, 0
    for s in stages:
        unit_base[s] = total_units
        total_units += UNITS_OF[s[:3]]

    ctx = ExitStack()
    with ctx:
        def sb(name, shape):
            return ctx.enter_context(nc.sbuf_tensor(name, shape, f32))

        def sem(name):
            return ctx.enter_context(nc.semaphore(name))

        x = sb("x", [P, KT, T])
        h = sb("h", [P, KT, T])
        ring = sb("ring", [P, RING, UNIT])
        par = sb("par", [P, par_n])
        con = sb("con", [P, con_n])
        pin = sb("pin", [P, 2, 2, T])
        rstd = sb("rstd", [P, T])
        ps = ctx.enter_context(nc.psum_tensor("ps", [P, 8, 512], f32))
        ARENA = 33792
        arena = sb("arena", [P, ARENA])

        class Carve:
            def __init__(self):
                self.at = 0

            def __call__(self, *shape):
                n = int(np.prod(shape))
                ap = arena[:, self.at:self.at + n]
                self.at += n
                assert self.at <= ARENA, self.at
                names = " ".join("abcd"[:len(shape)])
                if len(shape) == 1:
                    return ap
                return ap.rearrange(f"p ({names}) -> p {names}", **dict(zip("abcd", shape)))

        def C(name):
            at, n = con_off[name]
            return con[:, at:at + n]

        def G(name, i=0, rows=P):
            at = par_off[name][0] + i
            return par[0:rows, at:at + 1]

        def over(ap, n):
            return ap.unsqueeze(1).to_broadcast([ap.shape[0], n, ap.shape[1]])

        def each(ap, n):
            return ap.unsqueeze(2).to_broadcast([ap.shape[0], ap.shape[1], n])

        ident, ones, pairs = C("ident"), C("ones"), C("pairs")
        sel = C("sel").rearrange("p (n m) -> p n m", n=16)
        sel2 = C("sel2").rearrange("p (n m) -> p n m", n=8)
        levels = C("levels").rearrange("p (n m) -> p n m", n=7)

        arrived = [sem(f"weights_in_{s}") for s in range(RING)]
        products = [sem(f"products_done_{s}") for s in range(RING)]
        s_const, s_out = sem("constants_in"), sem("out_stored")
        s_x = sem("x_ready")
        s_sq, s_sum, s_sd, s_h = sem("norm_squares"), sem("norm_sum"), sem("norm_sqrt"), sem("h_ready")
        s_vc = sem("vector_chain")
        s_nl, s_act = sem("nonlinearity_done"), sem("ffn_act_ready")
        s_gate, s_pw = sem("ple_gate_ready"), sem("ple_tile_added")
        s_add = sem("projection_added")
        order = {s: n for n, s in enumerate(stages)}
        n_ple = {s: n for n, s in enumerate([s for s in stages if s[:3] == "ple"])}
        n_lin = {s: n for n, s in enumerate([s for s in stages if s in ("even", "odd", "second")])}
        ffn_j0, at = {}, 0
        for s in stages:
            ffn_j0[s] = at
            at += FJ if s[:3] == "ffn" else FJ2 if s == "mlp" else 0

        def sems_of(stage):
            return sem(stage + "_tensor_steps"), sem(stage + "_scalar_steps"), sem(stage + "_vector_steps")

        V, A, TE = nc.vector, nc.scalar, nc.tensor
        
        class Links:
            n = 0

            def step(self):
                self.n += 1
                return 1
        vc = Links()

        def tile_of(u, k, m=P):
            return ring[:, u % RING, k * P:k * P + m]

        def loads(u, i=None):
            return 16 * (u // RING + 1) if i is None else i * 16 + 16 * (u // RING + 1)

        def uses(u, i=None):
            return u // RING + 1 if i is None else i + (u // RING + 1)

        def mm(o, lhsT, rhs, start=True, stop=True):
            return TE.matmul(o, lhsT, rhs, start=start, stop=stop, skip_group_check=True)

        def linear(pe, u, o, rhs=h, n=KT, i=None):
            pe.wait_ge(arrived[u % RING], loads(u, i))
            for k in range(n):
                last = mm(o, tile_of(u, k), rhs[:, k, :], k == 0, k == n - 1)
            last.then_inc(products[u % RING], 1)

        eps_col = con[:, con_off["rms"][0] + 1:con_off["rms"][0] + 2]

        def norm_act(act, n):
            if n:
                act.wait_ge(s_x, n)
            A.activation(h[:, :, :], x[:, :, :], ACT.Square).then_inc(s_sq, 1)
            act.wait_ge(s_sum, n + 1)
            A.activation(rstd[:, :], ps[:, 7, 0:T], ACT.Sqrt, bias=eps_col, scale=1.0 / D).then_inc(s_sd, 1)

        def norm_pe(pe, n):
            pe.wait_ge(s_sq, n + 1)
            for k in range(KT):
                last = mm(ps[:, 7, 0:T], ones, h[:, k, :], k == 0, k == KT - 1)
            last.then_inc(s_sum, 1)

        def norm_dve(dve, n, name, dst=h):
            dve.wait_ge(s_sd, n + 1)
            V.reciprocal(rstd[:, :], rstd[:, :]).then_inc(s_vc, vc.step())
            V.wait_ge(s_vc, vc.n)
            for k in range(KT):
                last = V.scalar_tensor_tensor(dst[:, k, :], x[:, k, :], G(name, k), rstd[:, :], MUL, MUL)
            last.then_inc(s_h, 1)

        sg, ab = sb("nonlinear", [P, 3, T]), sb("ffn_act", [P, 3, T])

        class Ffn:
            def __init__(self, stage):
                self.gated = stage != "mlp"
                self.per, self.n = (3, FJ) if self.gated else (2, FJ2)
                self.bufs = RING // self.per
                self.u0, self.j0 = unit_base[stage], ffn_j0[stage]
                self.rounds = (self.n - 2) // self.bufs

            def up(self, j):
                return self.u0 + (self.per * j - 1 if j else 0)

            def down(self, j):
                return self.u0 + (self.per * (j + 2) - 2 if j < self.n - 1 else self.per * self.n - 1)

        def turns(eng, f, body):
            body(0, None)
            body(1, None)
            with eng.Fori(0, f.rounds) as i:
                for j in range(2, 2 + f.bufs):
                    body(j, i)

        def count(f, j, i):
            return f.j0 + j + 1 if i is None else i * f.bufs + (f.j0 + j + 1)

        def ffn_pe(pe, f):
            def down(j, i):
                pe.wait_ge(s_act, count(f, j, i))
                u = f.down(j)
                pe.wait_ge(arrived[u % RING], loads(u, i))
                for m in range(KT):
                    first = j == 0 and m % 2 == 0
                    last = mm(ps[:, m // 2, m % 2 * T:m % 2 * T + T], tile_of(u, m), ab[:, j % f.bufs, :],
                              first, j == f.n - 1)
                last.then_inc(products[u % RING], 1)

            def body(j, i):
                if j >= f.bufs:
                    pe.wait_ge(s_act, count(f, j - f.bufs, i))
                for half in range(f.per - 1):
                    linear(pe, f.up(j) + half, ps[:, 4 + j % f.bufs, half * T:half * T + T], i=i)
                if j >= 1:
                    down(j - 1, i)
            turns(pe, f, body)
            down(f.n - 1, None)

        def ffn_act(act, f):
            def body(j, i):
                act.wait_ge(products[(f.up(j) + f.per - 2) % RING], uses(f.up(j) + f.per - 2, i))
                if j >= f.bufs:
                    act.wait_ge(s_act, count(f, j - f.bufs, i))
                A.activation(sg[:, j % f.bufs, :], ps[:, 4 + j % f.bufs, 0:T],
                             ACT.Silu if f.gated else ACT.Relu).then_inc(s_nl, 1)
            turns(act, f, body)

        def ffn_dve(dve, f):
            def body(j, i):
                dve.wait_ge(s_nl, count(f, j, i))
                if j >= f.bufs:
                    dve.wait_ge(products[(f.down(j - f.bufs)) % RING], uses(f.down(j - f.bufs), i))
                b = sg[:, j % f.bufs, :]
                V.tensor_tensor(ab[:, j % f.bufs, :], b, ps[:, 4 + j % f.bufs, T:2 * T] if f.gated else b,
                                MUL).then_inc(s_act, 1)
            turns(dve, f, body)
            dve.wait_ge(products[(f.down(f.n - 1)) % RING], uses(f.down(f.n - 1)))
            for b in range(4):
                last = V.scalar_tensor_tensor(x[:, 2 * b:2 * b + 2, :],
                                              ps[:, b, :].rearrange("p (a t) -> p a t", a=2),
                                              0.5 if f.gated else 1.0, x[:, 2 * b:2 * b + 2, :], MUL, ADD)
            last.then_inc(s_x, 1)

        def ple_in_pe(pe, s):
            pe.wait_ge(s_x, order[s])
            for g in range(2):
                u = unit_base[s] + g
                pe.wait_ge(arrived[u % RING], loads(u))
                for m in range(4 * g, 4 * g + 4):
                    for k in range(2):
                        last = mm(ps[:, m // 2, m % 2 * T:m % 2 * T + T], tile_of(u, (m % 4) * 2 + k),
                                  pin[:, int(s[3]), k, :], k == 0, k == 1)
                last.then_inc(products[u % RING], 1)

        def ple_pe(pe, s):
            base = 8 * n_ple[s]
            for m in range(KT):
                if m >= 3:
                    pe.wait_ge(s_gate, base + m - 2)
                linear(pe, unit_base[s] + 2 + m, ps[:, 4 + m % 3, 0:T])

        def ple_act(act, s):
            base = 8 * n_ple[s]
            for m in range(KT):
                act.wait_ge(products[(unit_base[s] + 2 + m) % RING], uses(unit_base[s] + 2 + m))
                if m >= 3:
                    act.wait_ge(s_pw, base + m - 2)
                A.activation(sg[:, m % 3, :], ps[:, 4 + m % 3, 0:T], ACT.Sigmoid).then_inc(s_gate, 1)

        def ple_dve(dve, s):
            base = 8 * n_ple[s]
            for m in range(KT):
                dve.wait_ge(s_gate, base + m + 1)
                if m == 0:
                    dve.wait_ge(products[(unit_base[s] + 1) % RING], uses(unit_base[s] + 1))
                V.tensor_tensor(ab[:, m % 3, :], sg[:, m % 3, :],
                                ps[:, m // 2, m % 2 * T:m % 2 * T + T], MUL).then_inc(s_pw, 1)
                dve.wait_ge(s_pw, base + m + 1)
                last = V.tensor_tensor(x[:, m, :], x[:, m, :], ab[:, m % 3, :], ADD)
            last.then_inc(s_x, 1)

        def out_pe(pe, s, u0, src):
            base = (KT - 1) * n_lin[s]
            for m in range(KT):
                if m >= 3:
                    pe.wait_ge(s_add, base + m - 2)
                linear(pe, u0 + m, ps[:, 4 + m % 3, 0:T], src)

        def out_dve(dve, s, u0):
            for m in range(KT):
                dve.wait_ge(products[(u0 + m) % RING], uses(u0 + m))
                V.tensor_tensor(x[:, m, :], x[:, m, :], ps[:, 4 + m % 3, 0:T], ADD)\
                    .then_inc(s_add if m < KT - 1 else s_x, 1)

        class Att:
            def __init__(self, S, PT, mx, sm, q, k, v, o, evac, scale, mask):
                self.S, self.PT, self.mx, self.sm = S, PT, mx, sm
                self.q, self.k, self.v, self.o, self.evac = q, k, v, o, evac
                self.scale, self.mask = scale, mask

            def scores(self, qb):
                nk = (qb + 1) * P
                return self.S.rearrange("p a b -> p (a b)")[:, 0:8 * nk].rearrange("p (a b) -> p a b", b=nk)

        def att_steps():
            pe = [f"{n}{qb}_{b}" for qb in range(2) for n, k in (("s", 2 * qb + 2), ("t", 2 * qb + 2), ("o", 1))
                  for b in range(k)]
            act = [n for qb in range(2) for n in [f"exp{qb}"] + [f"pt{qb}_{b}" for b in range(2 * qb + 2)]]
            dve = [f"{n}{qb}" for qb in range(2) for n in ("max", "prob", "out")]
            return pe, act, dve

        def att_pe(pe, a, pe_s, act_s, dve_s):
            for qb in range(2):
                per = 4 // (qb + 1)
                nk = (qb + 1) * P
                if qb:
                    pe.wait_ge(dve_s.sem, dve_s.after("out0"))
                for b in range(2 * qb + 2):
                    for n in range(per):
                        hd = b * per + n
                        last = mm(ps[:, b, n * nk:(n + 1) * nk], a.q(hd, qb), a.k(hd, nk))
                    last.then_inc(pe_s.sem, pe_s.step(f"s{qb}_{b}"))
                pe.wait_ge(dve_s.sem, dve_s.after(f"prob{qb}"))
                S = a.scores(qb)
                for i in range(8 * (qb + 1)):
                    hd, kb = i // (qb + 1), i % (qb + 1)
                    last = TE.transpose(ps[:, 4 + i // 4, i % 4 * P:i % 4 * P + P],
                                        S[:, hd, kb * P:kb * P + P], ident)
                    if i % 4 == 3:
                        last.then_inc(pe_s.sem, pe_s.step(f"t{qb}_{i // 4}"))
                for hd in range(8):
                    i = hd * (qb + 1)
                    pe.wait_ge(act_s.sem, act_s.after(f"pt{qb}_{(i + qb) // 4}"))
                    for kb in range(qb + 1):
                        last = mm(a.o(hd), a.v(hd, kb), a.PT[:, i + kb, :], kb == 0, kb == qb)
                last.then_inc(pe_s.sem, pe_s.step(f"o{qb}_0"))

        def att_act(act, a, pe_s, act_s, dve_s):
            for qb in range(2):
                act.wait_ge(dve_s.sem, dve_s.after(f"max{qb}"))
                S = a.scores(qb)
                for hd in range(8):
                    last = A.activation(S[:, hd, :], S[:, hd, :], ACT.Exp, bias=a.mx[:, hd:hd + 1],
                                        accum_out=a.sm[:, hd:hd + 1])
                last.then_inc(act_s.sem, act_s.step(f"exp{qb}"))
                for b in range(2 * qb + 2):
                    act.wait_ge(pe_s.sem, pe_s.after(f"t{qb}_{b}"))
                    A.activation(a.PT[:, 4 * b:4 * b + 4, :],
                                            ps[:, 4 + b, :].rearrange("p (a b) -> p a b", a=4), ACT.Copy).then_inc(act_s.sem, act_s.step(f"pt{qb}_{b}"))

        def att_dve(dve, a, pe_s, act_s, dve_s):
            for qb in range(2):
                per, nk = 4 // (qb + 1), (qb + 1) * P
                S = a.scores(qb)
                if qb:
                    dve.wait_ge(pe_s.sem, pe_s.after("t0_1"))
                for b in range(2 * qb + 2):
                    dve.wait_ge(pe_s.sem, pe_s.after(f"s{qb}_{b}"))
                    last = V.scalar_tensor_tensor(S[:, b * per:(b + 1) * per, :],
                                                  ps[:, b, :].rearrange("p (a b) -> p a b", b=nk), a.scale,
                                                  over(a.mask(qb), per), MUL, ADD)
                last.then_inc(s_vc, vc.step())
                V.wait_ge(s_vc, vc.n)
                V.tensor_reduce(a.mx, S, AX.X, MAXOP).then_inc(s_vc, vc.step())
                V.wait_ge(s_vc, vc.n)
                V.tensor_scalar(a.mx, a.mx, -1.0, None, MUL).then_inc(dve_s.sem, dve_s.step(f"max{qb}"))
                dve.wait_ge(act_s.sem, act_s.after(f"exp{qb}"))
                V.reciprocal(a.sm, a.sm).then_inc(s_vc, vc.step())
                V.wait_ge(s_vc, vc.n)
                V.tensor_tensor(S, S, each(a.sm, nk), MUL).then_inc(dve_s.sem, dve_s.step(f"prob{qb}"))
                dve.wait_ge(pe_s.sem, pe_s.after(f"o{qb}_0"))
                a.evac(qb).then_inc(dve_s.sem, dve_s.step(f"out{qb}"))

        def even_mixer():
            u0 = unit_base["even"]
            cv = Carve()
            low = cv(5, T)
            misc = cv(T)
            qkv = cv(12, T)
            zs = cv(4, T)
            sq = cv(16, T)
            rr = cv(T)
            oT = cv(8, T)
            mark = cv.at
            qT, kT = cv(8, T), cv(8, T)
            vm = cv(2, 512)
            S, PT = cv(8, T), cv(16, P)
            mx, sm = cv(8), cv(8)
            tmp = cv(2, T)
            cv.at = mark
            gcB, beB, egB = cv(4, T), cv(4, T), cv(4, T)
            gcol, bcol = cv(NB, 4), cv(NB, 4)
            dl = cv(NB, 4)
            ktok, vtok = cv(NB, 4, P), cv(NB, 4, P)
            Dm, AT, QK = cv(NB, 4, P), cv(NB, 4, P), cv(NB, 4, P)
            X, Ti, TT, Y = cv(NB, 4, P), cv(NB, 4, P), cv(NB, 4, P), cv(NB, 4, P)
            kbg, qg = cv(4, T), cv(4, T)
            rhs, vn, St = cv(4, P), cv(4, P), cv(4, P)
            tensor_done, scalar_done, vector_done = sems_of("even")
            ape, aact, advn = att_steps()
            LV = 7
            pe_names = (["n1", "bc1", "n2"] + [x_ for p in range(8) for x_ in (f"b2_{p}", f"rot{p}")] + ape
                        + ["gb"] + ["gcol", "kk0", "kk1", "tr0", "tr1", "tr2", "tr3"]
                        + [f"{n}{l}_{c}" for l in range(LV) for n in ("y", "inv") for c in range(NB)]
                        + ["vn0", "og0", "st0", "ks1", "vn1", "og1"] + ["n3", "bc3"])
            act_names = (["low", "misc", "z0", "z1", "z2", "z3", "qkv", "sq1", "sd1", "q0", "q1", "q2", "q3", "k", "sq2", "sd2"]
                         + aact + ["gabs", "gexp", "gln", "beta", "eg", "dm0", "dm1", "edl", "ktr0", "ktr1"]
                         + ["sq3", "sd3"])
            dve_names = ([f"cv{n}" for n in range(12)] + ["r1", "lown", "l2", "kn", "r2"]
                         + [x_ for p in range(8) for x_ in (f"nm{p}", f"rope{p}")] + advn
                         + ["g", "gc", "kk", "gcols", "dd0", "dd1", "aqk", "vb",  "x0"]
                         + [f"{n}{l}_{c}" for l in range(LV) for n in ("yc", "tc") for c in range(NB)]
                         + ["r0", "v0", "o0", "s0", "r1b", "v1", "o1", "r3", "ob"])
            tensor = Steps(tensor_done, pe_names)
            scalar = Steps(scalar_done, act_names)
            vector = Steps(vector_done, dve_names)

            def o_tile(hd):
                return ps[64 * (hd % 2):64 * (hd % 2) + 64, 0, hd // 2 * P:hd // 2 * P + P]

            def evac(qb):
                return V.tensor_copy(oT[:, 0:4, qb * P:qb * P + P], ps[:, 0, :].rearrange("p (a b) -> p a b", a=4))
            causal = C("causal")
            att = Att(S, PT, mx, sm,
                      lambda hd, qb: qT[0:96, hd, qb * P:qb * P + P], lambda hd, nk: kT[0:96, hd, 0:nk],
                      lambda hd, kb: vm[:, kb, hd * 64:hd * 64 + 64], o_tile, evac, MLA_QK ** -0.5,
                      lambda qb: causal[:, P - qb * P:2 * P])
            rms = C("rms")
            in_bank = lambda n: 4 + n % 3
            pair_bank = (6, 7, 0, 1)

            def pair(b, rows=P):
                return ps[0:rows, b, :].rearrange("p (a b) -> p a b", a=2)

            def in_read(eng, n):
                if n < 5:
                    eng.wait_ge(scalar_done, scalar.after("low"))
                elif n == 5:
                    eng.wait_ge(scalar_done, scalar.after("misc"))
                elif n < 18:
                    eng.wait_ge(vector_done, vector.after(f"cv{n - 6}"))
                else:
                    eng.wait_ge(scalar_done, scalar.after(f"z{n - 18}"))

            def blk(c):
                return slice(c * P, (c + 1) * P)

            def pe_prog(pe):
                for n in range(22):
                    if n < 5:
                        b = n
                    else:
                        b = 5 + (n - 5) % 3
                        if n >= 8:
                            in_read(pe, n - 3)
                    linear(pe, u0 + n, ps[:, b, 0:T])
                pe.wait_ge(scalar_done, scalar.after("sq1"))
                for n in range(13):
                    row = 0 if n < 3 else 1 if n < 5 else n - 3
                    last = mm(ps[0:16, 0, 0:T], C("onehot")[:, 15 - row:31 - row], sq[:, n, :], n == 0, n == 12)
                last.then_inc(tensor_done, tensor.step("n1"))
                pe.wait_ge(vector_done, vector.after("r1"))
                in_read(pe, 21)
                for r in range(10):
                    last = mm(ps[:, 1 + r // 2, r % 2 * T:r % 2 * T + T], sel[0:16, r, :], rr[0:16, :])
                last.then_inc(tensor_done, tensor.step("bc1"))
                pe.wait_ge(vector_done, vector.after("lown"))
                for hd in range(8):
                    for k in range(3):
                        t = hd * 3 + k
                        if t % 8 == 0:
                            pe.wait_ge(arrived[(u0 + 22 + t // 8) % RING], loads(u0 + 22 + t // 8))
                        last = mm(ps[0:96, pair_bank[hd // 2], hd % 2 * T:hd % 2 * T + T],
                                  tile_of(u0 + 22 + t // 8, t % 8, 96), low[:, k, :], k == 0, k == 2)
                        if t % 8 == 7:
                            last.then_inc(products[(u0 + 22 + t // 8) % RING], 1)
                pe.wait_ge(vector_done, vector.after("l2"))
                pe.wait_ge(arrived[(u0 + 25) % RING], loads(u0 + 25))
                for hd in range(8):
                    for k in range(2):
                        o = (hd // 2 * 2 + k) * P + hd % 2 * 64
                        last = mm(ps[0:64, 2 + hd // 2, hd % 2 * T:hd % 2 * T + T],
                                  ring[:, (u0 + 25) % RING, o:o + 64], low[:, 3 + k, :], k == 0, k == 1)
                last.then_inc(products[(u0 + 25) % RING], 1)
                pe.wait_ge(arrived[(u0 + 26) % RING], loads(u0 + 26))
                pe.wait_ge(scalar_done, scalar.after("q1"))
                for tb in range(NB):
                    for k in range(2):
                        last = mm(ps[:, 6 + tb, :], low[:, 3 + k, blk(tb)],
                                  ring[:, (u0 + 26) % RING, k * 512:(k + 1) * 512], k == 0, k == 1)
                last.then_inc(products[(u0 + 26) % RING], 1)
                pe.wait_ge(scalar_done, scalar.after("sq2"))
                for n in range(16):
                    last = mm(ps[0:16, 0, 0:T], C("onehot")[0:96, 15 - n:31 - n], sq[0:96, n, :], n == 0, n == 15)
                last.then_inc(tensor_done, tensor.step("n2"))
                pe.wait_ge(vector_done, vector.after("r2"))
                for p_ in range(8):
                    if p_ >= 2:
                        pe.wait_ge(vector_done, vector.after(f"nm{p_ - 2}"))
                    for r in (2 * p_, 2 * p_ + 1):
                        last = mm(ps[0:96, 1 + p_ % 2, r % 2 * T:r % 2 * T + T], sel[0:16, r, 0:96], rr[0:16, :])
                    last.then_inc(tensor_done, tensor.step(f"b2_{p_}"))
                    pe.wait_ge(vector_done, vector.after(f"nm{p_}"))
                    src = (qT if p_ < 4 else kT)[0:96, p_ % 4 * 2:p_ % 4 * 2 + 2, :]
                    mm(ps[0:96, 3 + p_ % 2, :], C("rot")[0:96, :], src).then_inc(tensor_done, tensor.step(f"rot{p_}"))
                pe.wait_ge(vector_done, vector.after("rope7"))
                att_pe(pe, att, tensor, scalar, vector)
                pe.wait_ge(vector_done, vector.after("gc"))
                pe.wait_ge(scalar_done, scalar.after("beta"))
                for g in range(4):
                    mm(ps[:, 4 + g // 2, g % 2 * T:g % 2 * T + T], sel[0:4, g, :], rr[0:4, :])
                    last = mm(ps[:, 6 + g // 2, g % 2 * T:g % 2 * T + T], sel[32:36, g, :], rr[32:36, :])
                last.then_inc(tensor_done, tensor.step("gb"))
                for c in range(NB):
                    mm(ps[:, 0, 4 * c:4 * c + 4], rr[0:4, blk(c)], ident[0:4, 0:4])
                    last = mm(ps[:, 1, 4 * c:4 * c + 4], rr[32:36, blk(c)], ident[32:36, 32:36])
                last.then_inc(tensor_done, tensor.step("gcol"))
                pe.wait_ge(vector_done, vector.after("gcols"))
                pe.wait_ge(scalar_done, scalar.after("eg"))
                pe.wait_ge(vector_done, vector.after("kk"))
                for c in range(NB):
                    for g in range(4):
                        k_, q_ = qkv[:, 4 + g, blk(c)], qkv[:, g, blk(c)]
                        mm(ps[:, c, g * P:g * P + P], k_, k_)
                        last = mm(ps[:, 2 + c, g * P:g * P + P], k_, q_)
                    last.then_inc(tensor_done, tensor.step(f"kk{c}"))
                for c in range(NB):
                    for j in range(2):
                        for g in range(4):
                            last = TE.transpose(ps[:, 4 + 2 * c + j, g * P:g * P + P],
                                                qkv[:, 4 + 4 * j + g, blk(c)], ident)
                        last.then_inc(tensor_done, tensor.step(f"tr{2 * c + j}"))
                pe.wait_ge(vector_done, vector.after("vb"))
                pe.wait_ge(scalar_done, scalar.after("ktr1"))
                for l in range(LV):
                    for c in range(NB):
                        if l == 0:
                            pe.wait_ge(vector_done, vector.after("x0"))
                        else:
                            pe.wait_ge(vector_done, vector.after(f"tc{l - 1}_{c}"))
                        for g in range(4):
                            last = mm(ps[:, c, g * P:g * P + P], X[:, c, g, :], Ti[:, c, g, :])
                        last.then_inc(tensor_done, tensor.step(f"y{l}_{c}"))
                    for c in range(NB):
                        pe.wait_ge(vector_done, vector.after(f"yc{l}_{c}"))
                        for g in range(4):
                            mm(ps[:, 2 + c, g * P:g * P + P], TT[:, c, g, :], Y[:, c, g, :])
                            last = mm(ps[:, 4 + c, g * P:g * P + P], Y[:, c, g, :], TT[:, c, g, :])
                        last.then_inc(tensor_done, tensor.step(f"inv{l}_{c}"))
                for c in range(NB):
                    if c:
                        pe.wait_ge(vector_done, vector.after("s0"))
                        for g in range(4):
                            last = mm(ps[:, 6, g * P:g * P + P], kbg[:, g, blk(c)], St[:, g, :])
                        last.then_inc(tensor_done, tensor.step("ks1"))
                    pe.wait_ge(vector_done, vector.after("r0" if c == 0 else "r1b"))
                    for g in range(4):
                        last = mm(ps[:, 7, g * P:g * P + P], TT[:, c, g, :], rhs[:, g, :])
                    last.then_inc(tensor_done, tensor.step(f"vn{c}"))
                    pe.wait_ge(vector_done, vector.after(f"v{c}"))
                    for g in range(4):
                        if c:
                            mm(ps[:, c, g * P:g * P + P], St[:, g, :], qg[:, g, blk(c)], True, False)
                        last = mm(ps[:, c, g * P:g * P + P], vn[:, g, :], QK[:, c, g, :], c == 0, True)
                    last.then_inc(tensor_done, tensor.step(f"og{c}"))
                    if c == 0:
                        for g in range(4):
                            last = mm(ps[:, 5, g * P:g * P + P], ktok[:, 0, g, :], vn[:, g, :])
                        last.then_inc(tensor_done, tensor.step("st0"))
                pe.wait_ge(scalar_done, scalar.after("sq3"))
                for g in range(4):
                    last = mm(ps[0:16, 2, 0:T], C("onehot")[:, 15 - g:31 - g], sq[:, g, :], g == 0, g == 3)
                last.then_inc(tensor_done, tensor.step("n3"))
                pe.wait_ge(vector_done, vector.after("r3"))
                for g in range(4):
                    last = mm(ps[:, 3 + g // 2, g % 2 * T:g % 2 * T + T], sel[0:4, g, :], rr[0:4, :])
                last.then_inc(tensor_done, tensor.step("bc3"))
                pe.wait_ge(vector_done, vector.after("ob"))
                out_pe(pe, "even", u0 + 27, oT)

            def act_prog(act):
                for n in range(5):
                    act.wait_ge(products[(u0 + n) % RING], uses(u0 + n))
                    A.activation(low[:, n, :], ps[:, n, 0:T], ACT.Copy)
                    last = A.activation(sq[:, n, :], ps[:, n, 0:T], ACT.Square)
                last.then_inc(scalar_done, scalar.step("low"))
                act.wait_ge(products[(u0 + 5) % RING], uses(u0 + 5))
                A.activation(misc, ps[:, 5, 0:T], ACT.Copy).then_inc(scalar_done, scalar.step("misc"))
                for n in range(18, 22):
                    act.wait_ge(products[(u0 + n) % RING], uses(u0 + n))
                    A.activation(zs[:, n - 18, :], ps[:, 5 + (n - 5) % 3, 0:T], ACT.Silu).then_inc(scalar_done, scalar.step(f"z{n - 18}"))
                act.wait_ge(vector_done, vector.after("cv11"))
                A.activation(qkv, qkv, ACT.Silu).then_inc(scalar_done, scalar.step("qkv"))
                act.wait_ge(scalar_done, scalar.after("qkv"))
                A.activation(sq[:, 5:13, :], qkv[:, 0:8, :], ACT.Square).then_inc(scalar_done, scalar.step("sq1"))
                act.wait_ge(tensor_done, tensor.after("n1"))
                A.activation(rr[0:16, :], ps[0:16, 0, 0:T], ACT.Sqrt, bias=rms[0:16, 1:2],
                                      scale=rms[0:16, 0:1]).then_inc(scalar_done, scalar.step("sd1"))
                for p_ in range(4):
                    act.wait_ge(products[(u0 + 22 + min(2, (6 * p_ + 5) // 8)) % RING], uses(u0 + 22 + min(2, (6 * p_ + 5) // 8)))
                    b = pair_bank[p_]
                    A.activation(qT[0:96, 2 * p_:2 * p_ + 2, :], pair(b, 96), ACT.Copy)
                    A.activation(sq[0:96, 2 * p_:2 * p_ + 2, :], pair(b, 96), ACT.Square).then_inc(scalar_done, scalar.step(f"q{p_}"))
                act.wait_ge(products[(u0 + 25) % RING], uses(u0 + 25))
                for p_ in range(4):
                    last = A.activation(kT[0:64, 2 * p_:2 * p_ + 2, :], pair(2 + p_, 64), ACT.Copy)
                last.then_inc(scalar_done, scalar.step("k"))
                act.wait_ge(products[(u0 + 26) % RING], uses(u0 + 26))
                for tb in range(NB):
                    A.activation(vm[:, tb, :], ps[:, 6 + tb, :], ACT.Copy)
                act.wait_ge(vector_done, vector.after("kn"))
                act.wait_ge(scalar_done, scalar.after("k"))
                A.activation(sq[0:96, 8:16, :], kT[0:96, :, :], ACT.Square).then_inc(scalar_done, scalar.step("sq2"))
                act.wait_ge(tensor_done, tensor.after("n2"))
                A.activation(rr[0:16, :], ps[0:16, 0, 0:T], ACT.Sqrt, bias=rms[0:16, 3:4],
                                      scale=rms[0:16, 2:3]).then_inc(scalar_done, scalar.step("sd2"))
                att_act(act, att, tensor, scalar, vector)
                A.activation(tiny[0:4, 0, :], misc[0:4, :], ACT.Abs, bias=G("dt_bias", 0, 4)).then_inc(scalar_done, scalar.step("gabs"))
                act.wait_ge(scalar_done, scalar.after("gabs"))
                A.activation(tiny[0:4, 3, 0:1], G("a_log", 0, 4), ACT.Exp)
                A.activation(tiny[0:4, 0, :], tiny[0:4, 0, :], ACT.Exp, scale=-1.0).then_inc(scalar_done, scalar.step("gexp"))
                act.wait_ge(scalar_done, scalar.after("gexp"))
                A.activation(tiny[0:4, 1, :], tiny[0:4, 0, :], ACT.Ln, bias=1.0).then_inc(scalar_done, scalar.step("gln"))
                A.activation(rr[32:36, :], misc[32:36, :], ACT.Sigmoid).then_inc(scalar_done, scalar.step("beta"))
                act.wait_ge(tensor_done, tensor.after("gb"))
                for g in range(2):
                    last = A.activation(egB[:, 2 * g:2 * g + 2, :], pair(4 + g), ACT.Exp)
                last.then_inc(scalar_done, scalar.step("eg"))
                for c in range(NB):
                    act.wait_ge(vector_done, vector.after(f"dd{c}"))
                    A.activation(Dm[:, c, :, :], Dm[:, c, :, :], ACT.Exp).then_inc(scalar_done, scalar.step(f"dm{c}"))
                A.activation(dl, dl, ACT.Exp).then_inc(scalar_done, scalar.step("edl"))
                act.wait_ge(scalar_done, scalar.after("edl"))
                for c in range(NB):
                    act.wait_ge(tensor_done, tensor.after(f"tr{2 * c}"))
                    for g in range(4):
                        last = A.activation(ktok[:, c, g, :], ps[:, 4 + 2 * c, g * P:g * P + P], ACT.Copy,
                                            scale=dl[:, c, g:g + 1])
                    last.then_inc(scalar_done, scalar.step(f"ktr{c}"))
                act.wait_ge(vector_done, vector.after("o1"))
                A.activation(sq[:, 0:4, :], oT[:, 4:8, :], ACT.Square).then_inc(scalar_done, scalar.step("sq3"))
                act.wait_ge(tensor_done, tensor.after("n3"))
                A.activation(rr[0:4, :], ps[0:4, 2, 0:T], ACT.Sqrt, bias=rms[0:4, 5:6],
                                      scale=rms[0:4, 4:5]).then_inc(scalar_done, scalar.step("sd3"))

            tiny = sq[:, 12:16, :]

            def dve_prog(dve):
                for n in range(12):
                    u = u0 + 6 + n
                    dve.wait_ge(products[u % RING], uses(u))
                    src, dst = ps[:, 5 + (n + 1) % 3, 0:T], qkv[:, n, :]
                    V.tensor_scalar(dst, src, G("gconv", 36 + n), None, MUL).then_inc(s_vc, vc.step())
                    V.wait_ge(s_vc, vc.n)
                    for d in (1, 2, 3):
                        last = V.scalar_tensor_tensor(dst[:, d:T], src[:, 0:T - d], G("gconv", 12 * (3 - d) + n),
                                                      dst[:, d:T], MUL, ADD)
                        if d < 3:
                            last.then_inc(s_vc, vc.step())
                            V.wait_ge(s_vc, vc.n)
                    last.then_inc(vector_done, vector.step(f"cv{n}"))
                dve.wait_ge(scalar_done, scalar.after("sd1"))
                V.reciprocal(rr[0:16, :], rr[0:16, :]).then_inc(vector_done, vector.step("r1"))
                dve.wait_ge(tensor_done, tensor.after("bc1"))
                for n in range(5):
                    last = V.scalar_tensor_tensor(low[:, n, :], low[:, n, :],
                                                  G("q_a", n) if n < 3 else G("kv_a", n - 3),
                                                  ps[:, 1, (n // 3) * T:(n // 3) * T + T], MUL, MUL)
                last.then_inc(vector_done, vector.step("lown"))
                for n in range(4):
                    last = V.tensor_tensor(qkv[:, 2 * n:2 * n + 2, :], qkv[:, 2 * n:2 * n + 2, :], pair(2 + n), MUL)
                last.then_inc(vector_done, vector.step("l2"))
                dve.wait_ge(scalar_done, scalar.after("misc"))
                V.tensor_copy(kT[64:96, :, :], over(misc[64:96, :], 8)).then_inc(vector_done, vector.step("kn"))
                dve.wait_ge(scalar_done, scalar.after("sd2"))
                V.reciprocal(rr[0:16, :], rr[0:16, :]).then_inc(vector_done, vector.step("r2"))
                for p_ in range(8):
                    buf = (qT if p_ < 4 else kT)[0:96, p_ % 4 * 2:p_ % 4 * 2 + 2, :]
                    dve.wait_ge(tensor_done, tensor.after(f"b2_{p_}"))
                    V.scalar_tensor_tensor(buf, buf, G("mla_q" if p_ < 4 else "mla_k", 0, 96),
                                                    pair(1 + p_ % 2, 96), MUL, MUL).then_inc(vector_done, vector.step(f"nm{p_}"))
                    dve.wait_ge(tensor_done, tensor.after(f"rot{p_}"))
                    V.tensor_tensor(tmp[0:96, :, :], pair(3 + p_ % 2, 96), over(C("sin")[0:96, :], 2), MUL)
                    V.tensor_tensor(buf, buf, over(C("cos")[0:96, :], 2), MUL).then_inc(s_vc, vc.step())
                    V.wait_ge(s_vc, vc.n)
                    V.tensor_tensor(buf, buf, tmp[0:96, :, :], ADD).then_inc(vector_done, vector.step(f"rope{p_}"))
                att_dve(dve, att, tensor, scalar, vector)
                dve.wait_ge(scalar_done, scalar.after("gln"))
                V.tensor_scalar(tiny[0:4, 2, :], misc[0:4, :], G("dt_bias", 0, 4), 0.0, ADD, MAXOP).then_inc(s_vc, vc.step())
                V.wait_ge(s_vc, vc.n)
                V.tensor_tensor(tiny[0:4, 2, :], tiny[0:4, 2, :], tiny[0:4, 1, :], ADD).then_inc(s_vc, vc.step())
                V.wait_ge(s_vc, vc.n)
                V.tensor_scalar(tiny[0:4, 2, :], tiny[0:4, 2, :], tiny[0:4, 3, 0:1], -1.0, MUL, MUL).then_inc(vector_done, vector.step("g"))
                dve.wait_ge(vector_done, vector.after("g"))
                for c in range(NB):
                    last = V.tensor_tensor_scan(rr[0:4, blk(c)], ones[0:4, :], tiny[0:4, 2, blk(c)], 0.0, MUL, ADD)
                last.then_inc(vector_done, vector.step("gc"))
                dve.wait_ge(tensor_done, tensor.after("gb"))
                dve.wait_ge(scalar_done, scalar.after("eg"))
                for g in range(2):
                    V.tensor_copy(gcB[:, 2 * g:2 * g + 2, :], pair(4 + g))
                    last = V.tensor_copy(beB[:, 2 * g:2 * g + 2, :], pair(6 + g))
                last.then_inc(vector_done, vector.step("kk"))
                dve.wait_ge(tensor_done, tensor.after("gcol"))
                V.tensor_copy(gcol.rearrange("p a b -> p (a b)"), ps[:, 0, 0:8])
                V.tensor_copy(bcol.rearrange("p a b -> p (a b)"), ps[:, 1, 0:8]).then_inc(vector_done, vector.step("gcols"))
                dve.wait_ge(vector_done, vector.after("gcols"))
                for c in range(NB):
                    for g in range(4):
                        last = V.tensor_scalar(Dm[:, c, g, :], gcB[:, g, blk(c)], gcol[:, c, g:g + 1], 0.0, SUB, MINOP)
                    V.tensor_tensor(dl[:, c, :], gcB[:, :, c * P + P - 1], gcol[:, c, :], SUB).then_inc(vector_done, vector.step(f"dd{c}"))
                V.tensor_tensor(kbg, qkv[:, 4:8, :], beB, MUL).then_inc(s_vc, vc.step())
                V.wait_ge(s_vc, vc.n)
                V.tensor_tensor(kbg, kbg, egB, MUL).then_inc(s_vc, vc.step())
                V.wait_ge(s_vc, vc.n)
                V.scalar_tensor_tensor(qg.rearrange("p a b -> p (a b)"), qkv[:, 0:4, :].rearrange("p a b -> p (a b)"), GD ** -0.5,
                                       egB.rearrange("p a b -> p (a b)"), MUL, MUL)
                for c in range(NB):
                    dve.wait_ge(tensor_done, tensor.after(f"kk{c}"))
                    dve.wait_ge(scalar_done, scalar.after(f"dm{c}"))
                    f = lambda ap: ap[:, c, :, :].rearrange("p a b -> p (a b)")
                    V.tensor_tensor(f(AT), ps[:, c, :], f(Dm), MUL)
                    V.scalar_tensor_tensor(f(QK), ps[:, 2 + c, :], GD ** -0.5, f(Dm), MUL, MUL).then_inc(s_vc, vc.step())
                    V.wait_ge(s_vc, vc.n)
                    V.tensor_tensor(AT[:, c, :, :], AT[:, c, :, :], beB[:, :, blk(c)], MUL)
                    last = V.tensor_tensor(QK[:, c, :, :], QK[:, c, :, :], over(C("incl"), 4), MUL)
                last.then_inc(vector_done, vector.step("aqk"))
                for c in range(NB):
                    dve.wait_ge(tensor_done, tensor.after(f"tr{2 * c + 1}"))
                    for g in range(4):
                        last = V.tensor_scalar(vtok[:, c, g, :], ps[:, 5 + 2 * c, g * P:g * P + P],
                                               bcol[:, c, g:g + 1], None, MUL)
                last.then_inc(vector_done, vector.step("vb"))
                dve.wait_ge(vector_done, vector.after("vb"))
                for c in range(NB):
                    V.tensor_copy(Ti[:, c, :, :], over(ident, 4))
                    V.tensor_copy(TT[:, c, :, :], over(ident, 4))
                    last = V.tensor_tensor(X[:, c, :, :], AT[:, c, :, :], over(levels[:, 0, :], 4), MUL)
                last.then_inc(vector_done, vector.step("x0"))
                for l in range(LV):
                    for c in range(NB):
                        dve.wait_ge(tensor_done, tensor.after(f"y{l}_{c}"))
                        V.tensor_copy(Y[:, c, :, :], ps[:, c, :].rearrange("p (a b) -> p a b", a=4)).then_inc(vector_done, vector.step(f"yc{l}_{c}"))
                        if l + 1 < LV:
                            V.tensor_tensor(X[:, c, :, :], AT[:, c, :, :], over(levels[:, l + 1, :], 4), MUL)
                    for c in range(NB):
                        dve.wait_ge(tensor_done, tensor.after(f"inv{l}_{c}"))
                        f = lambda ap: ap[:, c, :, :].rearrange("p a b -> p (a b)")
                        V.tensor_tensor(f(Ti), f(Ti), ps[:, 2 + c, :], SUB)
                        V.tensor_tensor(f(TT), f(TT), ps[:, 4 + c, :], SUB).then_inc(vector_done, vector.step(f"tc{l}_{c}"))
                flat = lambda ap: ap.rearrange("p a b -> p (a b)")
                V.tensor_copy(rhs, vtok[:, 0, :, :]).then_inc(vector_done, vector.step("r0"))
                dve.wait_ge(tensor_done, tensor.after("vn0"))
                V.tensor_copy(flat(vn), ps[:, 7, :]).then_inc(vector_done, vector.step("v0"))
                dve.wait_ge(tensor_done, tensor.after("og0"))
                V.tensor_copy(oT[:, 4:8, 0:P], ps[:, 0, :].rearrange("p (a b) -> p a b", a=4)).then_inc(vector_done, vector.step("o0"))
                dve.wait_ge(tensor_done, tensor.after("st0"))
                V.tensor_copy(flat(St), ps[:, 5, :]).then_inc(vector_done, vector.step("s0"))
                dve.wait_ge(tensor_done, tensor.after("ks1"))
                V.tensor_tensor(flat(rhs), vtok[:, 1, :, :].rearrange("p a b -> p (a b)"), ps[:, 6, :], SUB).then_inc(vector_done, vector.step("r1b"))
                dve.wait_ge(tensor_done, tensor.after("vn1"))
                V.tensor_copy(flat(vn), ps[:, 7, :]).then_inc(vector_done, vector.step("v1"))
                dve.wait_ge(tensor_done, tensor.after("og1"))
                V.tensor_copy(oT[:, 4:8, P:T], ps[:, 1, :].rearrange("p (a b) -> p a b", a=4)).then_inc(vector_done, vector.step("o1"))
                dve.wait_ge(scalar_done, scalar.after("sd3"))
                V.reciprocal(rr[0:4, :], rr[0:4, :]).then_inc(vector_done, vector.step("r3"))
                V.tensor_tensor(zs, zs, oT[:, 4:8, :], MUL).then_inc(s_vc, vc.step())
                V.wait_ge(s_vc, vc.n)
                dve.wait_ge(tensor_done, tensor.after("bc3"))
                for g in range(2):
                    last = V.scalar_tensor_tensor(oT[:, 4 + 2 * g:6 + 2 * g, :], zs[:, 2 * g:2 * g + 2, :],
                                                  G("out_norm"), pair(3 + g), MUL, MUL)
                last.then_inc(vector_done, vector.step("ob"))
                out_dve(dve, "even", u0 + 27)
            return pe_prog, act_prog, dve_prog

        def odd_mixer():
            u0 = unit_base["odd"]
            cv = Carve()
            qk = cv(11, T)
            qi = cv(4, T)
            sq = cv(11, T)
            rr = cv(T)
            vt = cv(NB, 264)
            rl = cv(4, T)
            sc = cv(NB, T)
            wk = cv(NB, T)
            m8 = cv(8)
            S, PT = cv(8, T), cv(16, P)
            mx, sm = cv(8), cv(8)
            oT = cv(8, T)
            ape, aact, advn = att_steps()
            every = [(qb, hd) for qb in range(NB) for hd in range(IDX_H)]
            tensor_done, scalar_done, vector_done = sems_of("odd")
            tensor = Steps(tensor_done, ["n1", "bc1"] + [f"ix{i}" for i in range(16)] + ape)
            scalar = Steps(scalar_done, [f"in{n}" for n in range(15)] + ["sd1"] + [f"rl{i}" for i in range(16)] + aact)
            vector = Steps(vector_done, ["vt", "r1", "nq"] + [f"sc{i}" for i in range(16)] + ["mask"] + advn)
            causal, rms = C("causal"), C("rms")

            def keys(qb):
                return causal[:, P - qb * P:2 * P]

            def evac(qb):
                V.tensor_copy(oT[:, 0:4, qb * P:qb * P + P], ps[:, 0, :].rearrange("p (a b) -> p a b", a=4))
                return V.tensor_copy(oT[:, 4:8, qb * P:qb * P + P], ps[:, 1, :].rearrange("p (a b) -> p a b", a=4))
            att = Att(S, PT, mx, sm,
                      lambda hd, qb: qk[:, hd, qb * P:qb * P + P], lambda hd, nk: qk[:, 8 + hd // 4, 0:nk],
                      lambda hd, kb: vt[:, kb, hd // 4 * P:hd // 4 * P + P],
                      lambda hd: ps[:, hd // 4, hd % 4 * P:hd % 4 * P + P], evac, P ** -0.5,
                      lambda qb: wk[:, qb, 0:(qb + 1) * P])

            def pe_prog(pe):
                for n in range(15):
                    if n >= 3:
                        pe.wait_ge(scalar_done, scalar.after(f"in{n - 3}"))
                    linear(pe, u0 + n, ps[:, 4 + n % 3, 0:T])
                for g, ks in enumerate(((0, 1, 2), (3, 4, 5), (6, 7))):
                    u = u0 + 15 + g
                    pe.wait_ge(arrived[u % RING], loads(u))
                    for j, k in enumerate(ks):
                        for tb in range(NB):
                            last = mm(ps[:, tb, 0:264], h[:, k, tb * P:tb * P + P],
                                      ring[:, u % RING, j * 264:j * 264 + 264], k == 0, k == 7)
                    last.then_inc(products[u % RING], 1)
                pe.wait_ge(scalar_done, scalar.after("in10"))
                for n in range(11):
                    rows = P if n < 10 else IDX_D
                    last = mm(ps[0:16, 2, 0:T], C("onehot")[0:rows, 15 - n:31 - n], sq[0:rows, n, :], n == 0, n == 10)
                last.then_inc(tensor_done, tensor.step("n1"))
                pe.wait_ge(vector_done, vector.after("r1"))
                pe.wait_ge(scalar_done, scalar.after("in14"))
                for r in range(11):
                    last = mm(ps[:, 2 + r // 2, r % 2 * T:r % 2 * T + T], sel[0:16, r, :], rr[0:16, :])
                last.then_inc(tensor_done, tensor.step("bc1"))
                pe.wait_ge(vector_done, vector.after("nq"))
                for i, (qb, hd) in enumerate(every):
                    r = slice(64 * (hd % 2), 64 * (hd % 2) + 64)
                    if i >= 4:
                        pe.wait_ge(scalar_done, scalar.after(f"rl{i - 4}"))
                    mm(ps[:, i % 4, 0:(qb + 1) * P], qi[r, hd // 2, qb * P:qb * P + P],
                                qk[r, 10, 0:(qb + 1) * P]).then_inc(tensor_done, tensor.step(f"ix{i}"))
                pe.wait_ge(scalar_done, scalar.after("rl15"))
                att_pe(pe, att, tensor, scalar, vector)
                pe.wait_ge(vector_done, vector.after("out1"))
                out_pe(pe, "odd", u0 + 18, oT)

            def act_prog(act):
                for n in range(15):
                    act.wait_ge(products[(u0 + n) % RING], uses(u0 + n))
                    src = ps[:, 4 + n % 3, 0:T]
                    if n < 11:
                        A.activation(qk[:, n, :], src, ACT.Copy)
                        A.activation(sq[:, n, :], src, ACT.Square).then_inc(scalar_done, scalar.step(f"in{n}"))
                    else:
                        A.activation(qi[:, n - 11, :], src, ACT.Copy).then_inc(scalar_done, scalar.step(f"in{n}"))
                act.wait_ge(tensor_done, tensor.after("n1"))
                A.activation(rr[0:16, :], ps[0:16, 2, 0:T], ACT.Sqrt, bias=rms[0:16, 5:6],
                                      scale=rms[0:16, 4:5]).then_inc(scalar_done, scalar.step("sd1"))
                for i, (qb, hd) in enumerate(every):
                    act.wait_ge(tensor_done, tensor.after(f"ix{i}"))
                    if i >= 4:
                        act.wait_ge(vector_done, vector.after(f"sc{i - 4}"))
                    A.activation(rl[:, i % 4, 0:(qb + 1) * P], ps[:, i % 4, 0:(qb + 1) * P], ACT.Relu).then_inc(scalar_done, scalar.step(f"rl{i}"))
                att_act(act, att, tensor, scalar, vector)

            def dve_prog(dve):
                dve.wait_ge(products[(u0 + 17) % RING], uses(u0 + 17))
                for tb in range(NB):
                    last = V.tensor_copy(vt[:, tb, :], ps[:, tb, 0:264])
                last.then_inc(vector_done, vector.step("vt"))
                dve.wait_ge(scalar_done, scalar.after("sd1"))
                V.reciprocal(rr[0:16, :], rr[0:16, :]).then_inc(vector_done, vector.step("r1"))
                dve.wait_ge(tensor_done, tensor.after("bc1"))
                for g in range(5):
                    V.scalar_tensor_tensor(qk[:, 2 * g:2 * g + 2, :], qk[:, 2 * g:2 * g + 2, :],
                                           G("dsa_q" if g < 4 else "dsa_k"),
                                           ps[:, 2 + g, :].rearrange("p (a b) -> p a b", a=2), MUL, MUL)
                V.scalar_tensor_tensor(qk[:, 10, :], qk[:, 10, :], G("kidx"), ps[:, 7, 0:T], MUL, MUL).then_inc(vector_done, vector.step("nq"))
                dve.wait_ge(vector_done, vector.after("vt"))
                for i, (qb, hd) in enumerate(every):
                    n = (qb + 1) * P
                    dve.wait_ge(scalar_done, scalar.after(f"rl{i}"))
                    if hd:
                        dve.wait_ge(vector_done, vector.after(f"sc{i - 1}"))
                    V.scalar_tensor_tensor(sc[:, qb, 0:n], rl[:, i % 4, 0:n], vt[:, qb, 256 + hd:257 + hd],
                                                    sc[:, qb, 0:n] if hd else keys(qb), MUL, ADD).then_inc(vector_done, vector.step(f"sc{i}"))
                dve.wait_ge(vector_done, vector.after("sc15"))
                for qb in range(NB):
                    n = (qb + 1) * P
                    w = wk[:, qb, 0:n]
                    for j in range(TOPK // 8):
                        src = sc[:, qb, 0:n] if j == 0 else w
                        V.max(m8, src).then_inc(s_vc, vc.step())
                        V.wait_ge(s_vc, vc.n)
                        V.match_replace(w, m8, src, TAKEN).then_inc(s_vc, vc.step())
                        V.wait_ge(s_vc, vc.n)
                    V.tensor_scalar(w, w, 0.5 * TAKEN, -NEG, ALU.is_le, MUL).then_inc(s_vc, vc.step())
                    V.wait_ge(s_vc, vc.n)
                    last = V.scalar_tensor_tensor(w, w, NEG, keys(qb), ADD, ADD)
                last.then_inc(vector_done, vector.step("mask"))
                dve.wait_ge(vector_done, vector.after("mask"))
                att_dve(dve, att, tensor, scalar, vector)
                out_dve(dve, "odd", u0 + 18)
            return pe_prog, act_prog, dve_prog

        def second_mixer():
            u0 = unit_base["second"]
            cv = Carve()
            AR = cv(KT, 2, T)
            BT, KP, VT = cv(KT, T), cv(KT, T), cv(KT, T)
            M, GC = cv(KT, T), cv(KT, T)
            EC = cv(KT, T // RC)
            S2 = cv(KT, P)
            lx = cv(2, T)
            col = cv(11, 8)
            omm = cv(26)
            mark = cv.at
            bufs = [[cv(T) for _ in range(30)] for _ in range(2)]
            cv.at = mark
            tok = cv(3, KT * P)
            AB, AK = cv(RH, 2, P), cv(RH, 2, P)
            Ti, TT, Y = cv(RH, P), cv(RH, P), cv(RH, P)
            X = h.rearrange("p a b -> p (a b)").rearrange("p (a b) -> p a b", b=P)
            RHS, SA = Ti.rearrange("p a b -> p (a b)")[:, 0:1024], Ti.rearrange("p a b -> p (a b)")[:, 1024:2048]
            rr = lx[:, 0, :]
            LV = 6
            lv_groups = [(l, g) for l in range(LV) for g in range(4)]

            def lv_order(l):
                return [("Y", 0), ("Y", 1), ("U", 0), ("Y", 2), ("U", 1), ("Y", 3), ("U", 2), ("U", 3)]

            tensor_done, scalar_done, vector_done = sems_of("second")
            pe_names, act_names, dve_names = [], ["spa", "spe", "spl", "lora"], ["omm", "sp1", "sp", "lx"]
            for t in range(KT):
                pe_names += [f"{t}_lru", f"{t}_small", f"{t}_kk", f"{t}_bonus"]
                act_names += [f"{t}_{n}" for n in ("ca", "ga", "gb", "gtb", "lg", "wd", "ea", "dec", "gc", "mult", "nk")]
                dve_names += [f"{t}_{n}" for n in ("xa", "ba", "u", "t1", "cum", "r", "k", "v", "k2", "bp", "bo")]
            for b in range(NB):
                pe_names += [f"tok{b}_{j}" for j in range(3)] + [f"A{b}_{g}" for g in range(4)]
                pe_names += [f"{k}{b}_{0}_{g}" for g in range(4) for k in "Y"]
                pe_names += [f"{k}{b}_{l}_{g}" for l in range(1, LV) for k, g in lv_order(l)]
                act_names += [f"tk{b}_{j}" for j in range(3)]
                act_names += [f"yc{b}_{l}_{g}" for l in range(1, LV) for g in range(4)]
                dve_names += [f"am{b}_{g}" for g in range(4)] + [f"x{b}"]
                dve_names += [f"tc{b}_{l}_{g}" for l in range(LV) for g in range(4)] + [f"z{b}"]
                for c in (2 * b, 2 * b + 1):
                    pe_names += [f"rhs{c}", f"sa{c}", f"y{c}"] + ([f"st{c}"] if c < 3 else [])
                    act_names += [f"sac{c}"]
                    dve_names += [f"rh{c}", f"yo{c}"] + ([f"s{c}"] if c < 3 else [])
            pe_names += ["mean", "var", "bc"]
            act_names += ["sqy", "sd"]
            dve_names += ["cen", "rs", "m"]
            tensor = Steps(tensor_done, pe_names)
            scalar = Steps(scalar_done, act_names)
            vector = Steps(vector_done, dve_names)
            small = 7

            def unit(t, i):
                return u0 + 2 + 12 * t + (i if i < 7 else i - 4)

            reader = {0: ("a", "ca"), 1: ("v", "xa"), 2: ("v", "ba"), 3: ("a", "ga"), 4: ("v", "u"), 5: ("a", "gb"),
                      6: ("a", "gtb"), 7: ("a", "lg"), 8: ("a", "lg"), 9: ("a", "wd"), 10: ("a", "wd"),
                      11: ("a", "wd"), 12: ("v", "r"), 13: ("v", "k"), 14: ("v", "v"), 15: ("a", "gc"),
                      16: ("a", "nk"), 17: ("v", "bo")}

            def bank(i):
                return ps[:, i % 6, 0:T]

            def bank_free(pe, t, i):
                tt_, j = (t, i - 6) if i >= 6 else (t - 1, i + 12)
                if tt_ >= 0:
                    e, name = reader[j]
                    by = scalar if e == "a" else vector
                    pe.wait_ge(by.sem, by.after(f"{tt_}_{name}"))

            def toks(c):
                return slice(RC * c, RC * c + RC)

            def pe_prog(pe):
                for n in range(2):
                    linear(pe, u0 + n, bank(n))
                pe.wait_ge(vector_done, vector.after("lx"))
                pe.wait_ge(scalar_done, scalar.after("lora"))
                for t in range(KT):
                    for i in range(7):
                        bank_free(pe, t, i)
                        linear(pe, unit(t, i), bank(i))
                    u = u0 + 2 + 12 * t + small
                    pe.wait_ge(arrived[u % RING], loads(u))
                    pe.wait_ge(vector_done, vector.after(f"{t}_u"))
                    for i in (7, 8):
                        bank_free(pe, t, i)
                        last = mm(bank(i), tile_of(u, i - 7), dv(t, "u"))
                    last.then_inc(tensor_done, tensor.step(f"{t}_lru"))
                    for i in (9, 10, 11):
                        bank_free(pe, t, i)
                    mm(bank(9), ring[0:64, u % RING, 256:384], lx[0:64, 0, :])
                    mm(bank(10), ring[64:128, u % RING, 384:512], lx[64:128, 0, :])
                    mm(bank(11), ring[:, u % RING, 512:640], lx[:, 1, :]).then_inc(tensor_done, tensor.step(f"{t}_small"))
                    for i in range(12, 16):
                        bank_free(pe, t, i)
                        if i == 12:
                            pe.wait_ge(arrived[(unit(t, i)) % RING], loads(unit(t, i)))
                            for k in range(KT):
                                last = mm(bank(i), tile_of(unit(t, i), k), h[:, k, :], k == 0, k == KT - 1)
                                if k == 0:
                                    last.then_inc(products[u % RING], 1)
                            last.then_inc(products[(unit(t, i)) % RING], 1)
                        else:
                            linear(pe, unit(t, i), bank(i))
                    bank_free(pe, t, 16)
                    pe.wait_ge(vector_done, vector.after(f"{t}_k2"))
                    mm(bank(16), pairs, dv(t, "k2")).then_inc(tensor_done, tensor.step(f"{t}_kk"))
                    bank_free(pe, t, 17)
                    pe.wait_ge(vector_done, vector.after(f"{t}_bp"))
                    mm(bank(17), pairs, dv(t, "bp")).then_inc(tensor_done, tensor.step(f"{t}_bonus"))
                for b in range(NB):
                    bs = slice(b * P, b * P + P)
                    if b == 0:
                        pe.wait_ge(vector_done, vector.after("7_bo"))
                    else:
                        pe.wait_ge(vector_done, vector.after("s1"))
                    for j, src in enumerate((BT, KP, VT)):
                        for t in range(KT):
                            last = TE.transpose(ps[:, 2 * j + t // 4, t % 4 * P:t % 4 * P + P], src[:, t, bs], ident)
                        last.then_inc(tensor_done, tensor.step(f"tok{b}_{j}"))
                    for g in range(4):
                        o = 4 * (g % 2)
                        if g < 2:
                            pe.wait_ge(scalar_done, scalar.after(f"tk{b}_2"))
                        if g >= 2:
                            pe.wait_ge(vector_done, vector.after(f"am{b}_{g - 2}"))
                        for t in (2 * g, 2 * g + 1):
                            for hf in range(2):
                                r = slice(64 * hf, 64 * hf + 64)
                                for q, src in ((0, BT), (2, KP)):
                                    last = mm(ps[:, o + q + hf, (t % 2) * T:(t % 2) * T + T]
                                              .rearrange("p (a b) -> p a b", a=2), src[r, t, bs], AR[r, t, :, bs])
                        last.then_inc(tensor_done, tensor.step(f"A{b}_{g}"))
                    pe.wait_ge(vector_done, vector.after(f"x{b}"))
                    for g in range(4):
                        if g >= 2:
                            pe.wait_ge(vector_done, vector.after(f"tc{b}_0_{g - 2}"))
                        for n in range(4):
                            last = TE.transpose(ps[:, g % 2, n * P:n * P + P], X[:, 4 * g + n, :], ident)
                        last.then_inc(tensor_done, tensor.step(f"Y{b}_0_{g}"))
                    for l in range(1, LV):
                        for k, g in lv_order(l):
                            if k == "Y":
                                pe.wait_ge(vector_done, vector.after(f"tc{b}_{l - 1}_{g}"))
                                if g >= 2:
                                    pe.wait_ge(scalar_done, scalar.after(f"yc{b}_{l}_{g - 2}"))
                                elif l >= 2:
                                    pe.wait_ge(scalar_done, scalar.after(f"yc{b}_{l - 1}_{g + 2}"))
                                if l == 1 and g == 0:
                                    pe.wait_ge(vector_done, vector.after(f"tc{b}_0_3"))
                                for n in range(4 * g, 4 * g + 4):
                                    last = mm(ps[:, g % 2, n % 4 * P:n % 4 * P + P], X[:, n, :], Ti[:, n, :])
                            else:
                                pe.wait_ge(scalar_done, scalar.after(f"yc{b}_{l}_{g}"))
                                if g >= 2:
                                    pe.wait_ge(vector_done, vector.after(f"tc{b}_{l}_{g - 2}"))
                                elif l >= 2:
                                    pe.wait_ge(vector_done, vector.after(f"tc{b}_{l - 1}_{g + 2}"))
                                for n in range(4 * g, 4 * g + 4):
                                    c_ = slice(n % 4 * P, n % 4 * P + P)
                                    if l < LV - 1:
                                        mm(ps[:, 2 + g % 2, c_], TT[:, n, :], Y[:, n, :])
                                    last = mm(ps[:, 4 + g % 2, c_], Y[:, n, :], TT[:, n, :])
                            last.then_inc(tensor_done, tensor.step(f"{k}{b}_{l}_{g}"))
                    pe.wait_ge(vector_done, vector.after(f"z{b}"))
                    for c in (2 * b, 2 * b + 1):
                        o_ = 64 * (c % 2)
                        r, cs = slice(o_, o_ + 64), slice(o_, o_ + 64)
                        v2 = tok[:, 2, :]
                        if c:
                            pe.wait_ge(vector_done, vector.after(f"s{c - 1}"))
                        for t in range(KT):
                            bk, at = t // 4, t % 4 * P
                            if c:
                                mm(ps[r, bk, at:at + P], AR[:, t, 0, toks(c)], S2[:, t, :], True, False)
                            for n in (2 * t, 2 * t + 1):
                                at = n % 8 * 64
                                last = mm(ps[r, bk, at:at + 64], AK[:, n, 0, cs], v2[:, n * 64:n * 64 + 64], c == 0, True)
                        last.then_inc(tensor_done, tensor.step(f"rhs{c}"))
                        pe.wait_ge(vector_done, vector.after(f"rh{c}"))
                        for n in range(RH):
                            last = mm(ps[r, 2 + n // 8, n % 8 * 64:n % 8 * 64 + 64], TT[:, n, cs], RHS[:, n * 64:n * 64 + 64])
                        last.then_inc(tensor_done, tensor.step(f"sa{c}"))
                        pe.wait_ge(scalar_done, scalar.after(f"sac{c}"))
                        for t in range(KT):
                            if c:
                                mm(ps[:, 4, t * 64:t * 64 + 64], S2[:, t, :], AR[:, t, 1, toks(c)], True, False)
                            for n in (2 * t, 2 * t + 1):
                                o = ps[64 * (n % 2):64 * (n % 2) + 64, 4, t * 64:t * 64 + 64]
                                mm(o, SA[:, n * 64:n * 64 + 64], AB[:, n, 1, cs], c == 0, False)
                                last = mm(o, v2[:, n * 64:n * 64 + 64], AK[:, n, 1, cs], False, True)
                        last.then_inc(tensor_done, tensor.step(f"y{c}"))
                        if c < 3:
                            for t in range(KT):
                                o = ps[:, 5 + t // 4, t % 4 * P:t % 4 * P + P]
                                w = slice(t * P, t * P + P)
                                mm(o, tok[r, 0, w], SA[r, w], True, False)
                                last = mm(o, tok[r, 1, w], tok[r, 2, w], False, True)
                            last.then_inc(tensor_done, tensor.step(f"st{c}"))
                pe.wait_ge(vector_done, vector.after("yo3"))
                for t in range(KT):
                    last = mm(ps[:, t // 2, t % 2 * T:t % 2 * T + T], pairs, VT[:, t, :])
                last.then_inc(tensor_done, tensor.step("mean"))
                pe.wait_ge(scalar_done, scalar.after("sqy"))
                for t in range(KT):
                    last = mm(ps[0:16, 4, 0:T], C("onehot2")[:, 14 - 2 * t:30 - 2 * t], BT[:, t, :], t == 0, t == KT - 1)
                last.then_inc(tensor_done, tensor.step("var"))
                pe.wait_ge(vector_done, vector.after("rs"))
                for t in range(KT):
                    last = mm(ps[:, t // 2, t % 2 * T:t % 2 * T + T], sel2[0:16, t, :], rr[0:16, :])
                last.then_inc(tensor_done, tensor.step("bc"))
                pe.wait_ge(vector_done, vector.after("m"))
                out_pe(pe, "second", u0 + 98, M)

            names = ("ca ga gb gtb sa si sw aa g2 ea th p1 p2 p3 mu nk gc "
                     "cx ya u t1 lw cum cl r k kr k2 bp tmp").split()

            def dv(t, name):
                return bufs[t % 2][names.index(name)]

            def act_prog(act):
                lo, _ = par_off["lru_a"]
                A.activation(col[:, 0, :], par[:, lo:lo + 8], ACT.Abs).then_inc(scalar_done, scalar.step("spa"))
                act.wait_ge(scalar_done, scalar.after("spa"))
                A.activation(col[:, 1, :], col[:, 0, :], ACT.Exp, scale=-1.0).then_inc(scalar_done, scalar.step("spe"))
                act.wait_ge(vector_done, vector.after("sp1"))
                A.activation(col[:, 3, :], col[:, 2, :], ACT.Ln).then_inc(scalar_done, scalar.step("spl"))
                act.wait_ge(vector_done, vector.after("lx"))
                A.activation(lx[0:64, 0, :], lx[0:64, 0, :], ACT.Tanh)
                A.activation(lx[:, 1, :], lx[:, 1, :], ACT.Sigmoid).then_inc(scalar_done, scalar.step("lora"))
                for t in range(KT):
                    d = lambda n: dv(t, n)
                    st = lambda ins, n: ins.then_inc(scalar_done, scalar.step(f"{t}_{n}"))
                    if t >= 2:
                        act.wait_ge(vector_done, vector.after(f"{t - 2}_bo"))
                    act.wait_ge(products[(unit(t, 0)) % RING], uses(unit(t, 0)))
                    st(A.activation(d("ca"), bank(0), ACT.Copy), "ca")
                    act.wait_ge(products[(unit(t, 3)) % RING], uses(unit(t, 3)))
                    st(A.activation(d("ga"), bank(3), ACT.Sigmoid, bias=G("merge_b", t)), "ga")
                    act.wait_ge(products[(unit(t, 5)) % RING], uses(unit(t, 5)))
                    st(A.activation(d("gb"), bank(5), ACT.Gelu_apprx_tanh), "gb")
                    act.wait_ge(products[(unit(t, 6)) % RING], uses(unit(t, 6)))
                    st(A.activation(d("gtb"), bank(6), ACT.Sigmoid, bias=G("merge_b", 8 + t)), "gtb")
                    act.wait_ge(tensor_done, tensor.after(f"{t}_lru"))
                    A.activation(d("sa"), bank(7), ACT.Sigmoid, bias=G("lru_ba", t))
                    st(A.activation(d("si"), bank(8), ACT.Sigmoid, bias=G("lru_bi", t)), "lg")
                    act.wait_ge(tensor_done, tensor.after(f"{t}_small"))
                    A.activation(d("sw"), bank(9), ACT.Sigmoid, bias=G("w0", t))
                    A.activation(d("aa"), bank(10), ACT.Sigmoid, bias=G("a0", t))
                    st(A.activation(d("g2"), bank(11), ACT.Copy), "wd")
                    act.wait_ge(scalar_done, scalar.after(f"{t}_lg"))
                    if t == 0:
                        act.wait_ge(vector_done, vector.after("sp"))
                    A.activation(d("ea"), d("sa"), ACT.Exp, scale=col[:, 8, t:t + 1])
                    st(A.activation(d("th"), d("sa"), ACT.Tanh, scale=col[:, 9, t:t + 1]), "ea")
                    act.wait_ge(vector_done, vector.after(f"{t}_cum"))
                    A.activation(d("p1"), d("cum"), ACT.Exp)
                    A.activation(d("p2"), d("cum"), ACT.Exp, scale=-1.0)
                    st(A.activation(d("p3"), d("cl"), ACT.Exp), "dec")
                    act.wait_ge(products[(unit(t, 15)) % RING], uses(unit(t, 15)))
                    st(A.activation(d("gc"), bank(15), ACT.Sigmoid, bias=G("merge_b", 16 + t)), "gc")
                    act.wait_ge(vector_done, vector.after(f"{t}_t1"))
                    st(A.activation(d("mu"), d("t1"), ACT.Sqrt), "mult")
                    act.wait_ge(tensor_done, tensor.after(f"{t}_kk"))
                    st(A.activation(d("nk"), bank(16), ACT.Sqrt), "nk")
                for b in range(NB):
                    for j in range(3):
                        act.wait_ge(tensor_done, tensor.after(f"tok{b}_{j}"))
                        if j == 0 and b == 0:
                            act.wait_ge(vector_done, vector.after("7_bo"))
                        for k in range(2):
                            last = A.activation(tok[:, j, k * 512:(k + 1) * 512], ps[:, 2 * j + k, :], ACT.Copy)
                        last.then_inc(scalar_done, scalar.step(f"tk{b}_{j}"))
                    for l in range(1, LV):
                        for g in range(4):
                            act.wait_ge(tensor_done, tensor.after(f"Y{b}_{l}_{g}"))
                            A.activation(Y[:, 4 * g:4 * g + 4, :],
                                                  ps[:, g % 2, :].rearrange("p (a b) -> p a b", a=4), ACT.Copy).then_inc(scalar_done, scalar.step(f"yc{b}_{l}_{g}"))
                    for c in (2 * b, 2 * b + 1):
                        r = slice(64 * (c % 2), 64 * (c % 2) + 64)
                        act.wait_ge(tensor_done, tensor.after(f"sa{c}"))
                        for k in range(2):
                            last = A.activation(SA[r, 512 * k:512 * k + 512], ps[r, 2 + k, :], ACT.Copy)
                        last.then_inc(scalar_done, scalar.step(f"sac{c}"))
                act.wait_ge(vector_done, vector.after("cen"))
                A.activation(BT, VT, ACT.Square).then_inc(scalar_done, scalar.step("sqy"))
                act.wait_ge(tensor_done, tensor.after("var"))
                rms = C("rms")
                A.activation(rr[0:16, :], ps[0:16, 4, 0:T], ACT.Sqrt, bias=rms[0:16, 7:8],
                                      scale=rms[0:16, 6:7]).then_inc(scalar_done, scalar.step("sd"))

            def shifted(dst, src, n, name=None):
                V.tensor_scalar(dst, src, omm[:, n:n + 1], None, MUL).then_inc(s_vc, vc.step())
                V.wait_ge(s_vc, vc.n)
                return V.scalar_tensor_tensor(dst[:, 1:T], src[:, 0:T - 1], G("mu", n), dst[:, 1:T], MUL, ADD)

            def dve_prog(dve):
                lo, n_ = par_off["mu"]
                V.tensor_scalar(omm, par[:, lo:lo + n_], -1.0, 1.0, MUL, ADD).then_inc(vector_done, vector.step("omm"))
                dve.wait_ge(scalar_done, scalar.after("spe"))
                e_, w_ = col[:, 1, :], col[:, 2, :]
                V.tensor_scalar(w_, e_, 1.0, None, ADD).then_inc(vector_done, vector.step("sp1"))
                dve.wait_ge(vector_done, vector.after("sp1"))
                V.tensor_scalar(col[:, 4, :], w_, -1.0, None, ADD).then_inc(s_vc, vc.step())
                V.wait_ge(s_vc, vc.n)
                V.tensor_scalar(col[:, 5, :], col[:, 4, :], 0.0, None, ALU.is_equal).then_inc(s_vc, vc.step())
                V.wait_ge(s_vc, vc.n)
                V.tensor_tensor(col[:, 4, :], col[:, 4, :], col[:, 5, :], ADD).then_inc(s_vc, vc.step())
                V.wait_ge(s_vc, vc.n)
                V.reciprocal(col[:, 4, :], col[:, 4, :]).then_inc(s_vc, vc.step())
                V.wait_ge(s_vc, vc.n)
                dve.wait_ge(scalar_done, scalar.after("spl"))
                V.tensor_tensor(col[:, 4, :], col[:, 4, :], col[:, 3, :], MUL).then_inc(s_vc, vc.step())
                V.wait_ge(s_vc, vc.n)
                V.tensor_tensor(col[:, 4, :], col[:, 4, :], col[:, 5, :], ADD).then_inc(s_vc, vc.step())
                V.wait_ge(s_vc, vc.n)
                V.tensor_tensor(col[:, 4, :], col[:, 4, :], e_, MUL).then_inc(s_vc, vc.step())
                V.wait_ge(s_vc, vc.n)
                la, _ = par_off["lru_a"]
                V.scalar_tensor_tensor(col[:, 6, :], par[:, la:la + 8], 0.0, col[:, 4, :], MAXOP, ADD).then_inc(s_vc, vc.step())
                V.wait_ge(s_vc, vc.n)
                V.tensor_scalar(col[:, 8, :], col[:, 6, :], -8.0, None, MUL)
                V.tensor_scalar(col[:, 9, :], col[:, 6, :], 8.0, None, MUL).then_inc(vector_done, vector.step("sp"))
                for n in range(2):
                    dve.wait_ge(products[(u0 + n) % RING], uses(u0 + n))
                    last = shifted(lx[:, n, :], bank(n), 24 + n)
                last.then_inc(vector_done, vector.step("lx"))
                for t in range(KT):
                    d = lambda n: dv(t, n)
                    st = lambda ins, n: ins.then_inc(vector_done, vector.step(f"{t}_{n}"))
                    now = lambda n: dve.wait_ge(vector_done, vector.after(f"{t}_{n}"))
                    aw = lambda n: dve.wait_ge(scalar_done, scalar.after(f"{t}_{n}"))
                    aw("ca")
                    dve.wait_ge(products[(unit(t, 1)) % RING], uses(unit(t, 1)))
                    st(V.tensor_tensor(d("cx"), d("ca"), bank(1), MUL), "xa")
                    now("xa")
                    V.tensor_scalar(d("ya"), d("cx"), G("conv_a", 16 + t), None, MUL).then_inc(s_vc, vc.step())
                    V.wait_ge(s_vc, vc.n)
                    for q in (1, 2):
                        V.scalar_tensor_tensor(d("ya")[:, q:T], d("cx")[:, 0:T - q], G("conv_a", 8 * (2 - q) + t),
                                                     d("ya")[:, q:T], MUL, ADD).then_inc(s_vc, vc.step())
                        V.wait_ge(s_vc, vc.n)
                    dve.wait_ge(products[(unit(t, 2)) % RING], uses(unit(t, 2)))
                    st(V.tensor_tensor(d("ya"), d("ya"), bank(2), MUL), "ba")
                    dve.wait_ge(products[(unit(t, 4)) % RING], uses(unit(t, 4)))
                    V.tensor_scalar(d("u"), bank(4), G("lru_conv", 24 + t), G("lru_cb", t), MUL, ADD).then_inc(s_vc, vc.step())
                    V.wait_ge(s_vc, vc.n)
                    for q in (1, 2, 3):
                        last = V.scalar_tensor_tensor(d("u")[:, q:T], bank(4)[:, 0:T - q],
                                                      G("lru_conv", 8 * (3 - q) + t), d("u")[:, q:T], MUL, ADD)
                        if q < 3:
                            last.then_inc(s_vc, vc.step())
                            V.wait_ge(s_vc, vc.n)
                    st(last, "u")
                    aw("ga")
                    V.tensor_tensor(M[:, t, :], d("ya"), d("ga"), MUL)
                    aw("gtb")
                    V.tensor_tensor(d("gb"), d("gb"), d("gtb"), MUL)
                    aw("lg")
                    V.tensor_tensor(d("si"), d("si"), d("u"), MUL)
                    aw("ea")
                    V.tensor_tensor(d("t1"), d("ea"), d("ea"), MUL).then_inc(s_vc, vc.step())
                    V.wait_ge(s_vc, vc.n)
                    st(V.scalar_tensor_tensor(d("t1"), d("t1"), 1.0, d("th"), ADD, MUL), "t1")
                    aw("wd")
                    V.tensor_scalar(d("lw"), d("sw"), LOG_DECAY, None, MUL).then_inc(s_vc, vc.step())
                    V.wait_ge(s_vc, vc.n)
                    V.tensor_tensor_scan(d("cum"), C("reset64"), d("lw"), 0.0, MUL, ADD).then_inc(s_vc, vc.step())
                    V.wait_ge(s_vc, vc.n)
                    st(V.tensor_tensor(d("cl"), d("cum"), d("lw"), SUB), "cum")
                    dve.wait_ge(products[(unit(t, 12)) % RING], uses(unit(t, 12)))
                    st(shifted(d("r"), bank(12), t), "r")
                    dve.wait_ge(products[(unit(t, 13)) % RING], uses(unit(t, 13)))
                    st(shifted(d("k"), bank(13), 8 + t), "k")
                    dve.wait_ge(products[(unit(t, 14)) % RING], uses(unit(t, 14)))
                    st(shifted(VT[:, t, :], bank(14), 16 + t), "v")
                    V.tensor_scalar(d("kr"), d("k"), G("kk", t), None, MUL).then_inc(s_vc, vc.step())
                    V.wait_ge(s_vc, vc.n)
                    st(V.tensor_tensor(d("k2"), d("kr"), d("kr"), MUL), "k2")
                    V.tensor_scalar(d("tmp"), d("aa"), -1.0, G("ka", t), ADD, MUL).then_inc(s_vc, vc.step())
                    V.wait_ge(s_vc, vc.n)
                    V.scalar_tensor_tensor(d("k"), d("tmp"), 1.0, d("k"), ADD, MUL).then_inc(s_vc, vc.step())
                    V.wait_ge(s_vc, vc.n)
                    st(V.scalar_tensor_tensor(d("bp"), d("r"), G("rk", t), d("k"), MUL, MUL), "bp")
                    aw("dec")
                    V.tensor_tensor(AR[:, t, 1, :], d("r"), d("p1"), MUL)
                    V.tensor_tensor(KP[:, t, :], d("k"), d("p2"), MUL)
                    V.tensor_copy(EC[:, t, :], d("p1")[:, RC - 1:T:RC])
                    aw("mult")
                    V.memset(d("mu")[:, 0:1], 1.0).then_inc(s_vc, vc.step())
                    V.wait_ge(s_vc, vc.n)
                    V.tensor_tensor(d("si"), d("si"), d("mu"), MUL).then_inc(s_vc, vc.step())
                    V.wait_ge(s_vc, vc.n)
                    V.tensor_tensor_scan(d("th"), d("ea"), d("si"), 0.0, MUL, ADD).then_inc(s_vc, vc.step())
                    V.wait_ge(s_vc, vc.n)
                    V.tensor_tensor(d("th"), d("th"), d("gb"), MUL).then_inc(s_vc, vc.step())
                    V.wait_ge(s_vc, vc.n)
                    V.tensor_tensor(M[:, t, :], M[:, t, :], d("th"), ADD).then_inc(s_vc, vc.step())
                    V.wait_ge(s_vc, vc.n)
                    aw("nk")
                    V.tensor_scalar(d("nk"), d("nk"), 1e-12, None, MAXOP).then_inc(s_vc, vc.step())
                    V.wait_ge(s_vc, vc.n)
                    V.reciprocal(d("nk"), d("nk")).then_inc(s_vc, vc.step())
                    V.wait_ge(s_vc, vc.n)
                    V.tensor_tensor(d("kr"), d("kr"), d("nk"), MUL).then_inc(s_vc, vc.step())
                    V.wait_ge(s_vc, vc.n)
                    V.tensor_tensor(AR[:, t, 0, :], d("kr"), d("p3"), MUL)
                    V.tensor_tensor(d("kr"), d("kr"), d("aa"), MUL).then_inc(s_vc, vc.step())
                    V.wait_ge(s_vc, vc.n)
                    V.tensor_tensor(BT[:, t, :], d("kr"), d("p2"), MUL)
                    V.tensor_tensor(GC[:, t, :], d("g2"), d("gc"), MUL).then_inc(s_vc, vc.step())
                    V.wait_ge(s_vc, vc.n)
                    dve.wait_ge(tensor_done, tensor.after(f"{t}_bonus"))
                    V.tensor_tensor(d("tmp"), bank(17), VT[:, t, :], MUL).then_inc(s_vc, vc.step())
                    V.wait_ge(s_vc, vc.n)
                    V.scalar_tensor_tensor(d("tmp"), d("tmp"), G("lnx_b", t), GC[:, t, :], ADD, MUL).then_inc(s_vc, vc.step())
                    V.wait_ge(s_vc, vc.n)
                    st(V.tensor_tensor(M[:, t, :], M[:, t, :], d("tmp"), ADD), "bo")
                mask2 = con[:, con_off["strict64"][0]:con_off["strict64"][0] + 2 * P]
                for b in range(NB):
                    v4 = lambda ap: ap.rearrange("p (t h) a b -> p t h (a b)", h=2)
                    for g in range(4):
                        dve.wait_ge(tensor_done, tensor.after(f"A{b}_{g}"))
                        o = 4 * (g % 2)
                        for hf in range(2):
                            for q, dst in ((0, AB), (2, AK)):
                                last = V.tensor_tensor(v4(dst)[:, 2 * g:2 * g + 2, hf, :],
                                                       ps[:, o + q + hf, :].rearrange("p (a b) -> p a b", a=2),
                                                       over(mask2, 2), MUL)
                        last.then_inc(vector_done, vector.step(f"am{b}_{g}"))
                    dve.wait_ge(vector_done, vector.after(f"am{b}_3"))
                    V.tensor_tensor(X, AB[:, :, 0, :], over(levels[:, 0, :], RH), MUL).then_inc(vector_done, vector.step(f"x{b}"))
                    dve.wait_ge(vector_done, vector.after(f"x{b}"))
                    for g in range(4):
                        s4 = slice(4 * g, 4 * g + 4)
                        dve.wait_ge(tensor_done, tensor.after(f"Y{b}_0_{g}"))
                        V.tensor_tensor(Ti[:, s4, :], over(ident, 4), ps[:, g % 2, :].rearrange("p (a b) -> p a b", a=4), SUB)
                        V.tensor_tensor(TT[:, s4, :], over(ident, 4), X[:, s4, :], SUB).then_inc(s_vc, vc.step())
                        V.wait_ge(s_vc, vc.n)
                        V.tensor_tensor(X[:, s4, :], AB[:, s4, 0, :], over(levels[:, 1, :], 4), MUL).then_inc(vector_done, vector.step(f"tc{b}_0_{g}"))
                    for l in range(1, LV):
                        for g in range(4):
                            s4 = slice(4 * g, 4 * g + 4)
                            dve.wait_ge(tensor_done, tensor.after(f"U{b}_{l}_{g}"))
                            if l < LV - 1:
                                V.tensor_tensor(Ti[:, s4, :], Ti[:, s4, :],
                                                ps[:, 2 + g % 2, :].rearrange("p (a b) -> p a b", a=4), SUB)
                                V.tensor_tensor(X[:, s4, :], AB[:, s4, 0, :], over(levels[:, l + 1, :], 4), MUL)
                            V.tensor_tensor(TT[:, s4, :], TT[:, s4, :],
                                                     ps[:, 4 + g % 2, :].rearrange("p (a b) -> p a b", a=4), SUB).then_inc(vector_done, vector.step(f"tc{b}_{l}_{g}"))
                    if b == 0:
                        V.memset(S2, 0.0)
                    V.memset(Ti, 0.0).then_inc(vector_done, vector.step(f"z{b}"))
                    for c in (2 * b, 2 * b + 1):
                        r = slice(64 * (c % 2), 64 * (c % 2) + 64)
                        dve.wait_ge(tensor_done, tensor.after(f"rhs{c}"))
                        if c % 2 == 0:
                            dve.wait_ge(vector_done, vector.after(f"z{b}"))
                        for k in range(2):
                            last = V.tensor_scalar(RHS[r, 512 * k:512 * k + 512], ps[r, k, :], -1.0, None, MUL)
                        last.then_inc(vector_done, vector.step(f"rh{c}"))
                        dve.wait_ge(tensor_done, tensor.after(f"y{c}"))
                        V.tensor_copy(VT[:, :, toks(c)], ps[:, 4, :].rearrange("p (a b) -> p a b", a=8)).then_inc(vector_done, vector.step(f"yo{c}"))
                        if c < 3:
                            dve.wait_ge(tensor_done, tensor.after(f"st{c}"))
                            for hf in range(2):
                                w = slice(64 * hf, 64 * hf + 64)
                                for k in range(2):
                                    last = V.tensor_tensor(S2[w, 4 * k:4 * k + 4, w],
                                                           ps[w, 5 + k, :].rearrange("p (a b) -> p a b", a=4)[:, :, w],
                                                           S2[w, 4 * k:4 * k + 4, w], ADD)
                            last.then_inc(s_vc, vc.step())
                            V.wait_ge(s_vc, vc.n)
                            for hf in range(2):
                                w = slice(64 * hf, 64 * hf + 64)
                                last = V.tensor_tensor(S2[w, :, w], S2[w, :, w], each(EC[w, :, c], RN), MUL)
                            last.then_inc(vector_done, vector.step(f"s{c}"))
                dve.wait_ge(tensor_done, tensor.after("mean"))
                for k in range(4):
                    last = V.scalar_tensor_tensor(VT[:, 2 * k:2 * k + 2, :], ps[:, k, :].rearrange("p (a b) -> p a b", a=2),
                                                  -1.0 / RN, VT[:, 2 * k:2 * k + 2, :], MUL, ADD)
                last.then_inc(vector_done, vector.step("cen"))
                dve.wait_ge(scalar_done, scalar.after("sd"))
                V.reciprocal(rr[0:16, :], rr[0:16, :]).then_inc(vector_done, vector.step("rs"))
                dve.wait_ge(tensor_done, tensor.after("bc"))
                for t in range(KT):
                    last = V.scalar_tensor_tensor(VT[:, t, :], VT[:, t, :], G("lnx_g", t),
                                                  ps[:, t // 2, t % 2 * T:t % 2 * T + T], MUL, MUL)
                last.then_inc(s_vc, vc.step())
                V.wait_ge(s_vc, vc.n)
                V.tensor_tensor(VT, VT, GC, MUL).then_inc(s_vc, vc.step())
                V.wait_ge(s_vc, vc.n)
                V.tensor_tensor(M, M, VT, ADD).then_inc(vector_done, vector.step("m"))
                out_dve(dve, "second", u0 + 98)
            return pe_prog, act_prog, dve_prog
        mixers = {}
        if "even" in stages:
            mixers["even"] = even_mixer()
        if "odd" in stages:
            mixers["odd"] = odd_mixer()
        if "second" in stages:
            mixers["second"] = second_mixer()
        ffns = {s: Ffn(s) for s in stages if s[:3] == "ffn" or s == "mlp"}
        block = ctx.enter_context(nc.Block())

        @block.sync
        def _(sp):
            def load(s, u):
                sp.dma_start(ring[:, s, :], a_w[u].rearrange("a p n -> (a p) n")
                             if not isinstance(u, int) else a_w[u]).then_inc(arrived[s], 16)
            for dst, src in ((x[:, :, :], a_x), (con[:, :], a_con), (par[:, :], a_par), (pin[:, :, :, :], a_p)):
                sp.dma_start(dst, src).then_inc(s_const, 16)
            rounds, rest = total_units // RING, total_units % RING
            for s in range(RING):
                load(s, s)
            if rounds > 1:
                with sp.Fori(1, rounds) as i:
                    for s in range(RING):
                        sp.wait_ge(products[s], i)
                        load(s, bass.ds(i * RING + s, 1))
            for s in range(rest):
                sp.wait_ge(products[s], rounds)
                load(s, rounds * RING + s)
            n = len(stages)
            sp.wait_ge(s_h, n + 1)
            sp.dma_start(out, h[:, :, :]).then_inc(s_out, 16)
            sp.wait_ge(s_out, 16)

        @block.tensor
        def _(pe):
            pe.wait_ge(s_const, 16 * 4)
            for n, s in enumerate(stages):
                if s[:3] == "ple":
                    ple_in_pe(pe, s)
                norm_pe(pe, n)
                pe.wait_ge(s_h, n + 1)
                if s in ffns:
                    ffn_pe(pe, ffns[s])
                elif s[:3] == "ple":
                    ple_pe(pe, s)
                else:
                    mixers[s][0](pe)
            norm_pe(pe, len(stages))

        @block.scalar
        def _(act):
            act.wait_ge(s_const, 16 * 4)
            for n, s in enumerate(stages):
                norm_act(act, n)
                if s in ffns:
                    ffn_act(act, ffns[s])
                elif s[:3] == "ple":
                    ple_act(act, s)
                else:
                    mixers[s][1](act)
            norm_act(act, len(stages))

        @block.vector
        def _(dve):
            dve.wait_ge(s_const, 16 * 4)
            for n, s in enumerate(stages):
                norm_dve(dve, n, NORM_OF[s])
                if s in ffns:
                    ffn_dve(dve, ffns[s])
                elif s[:3] == "ple":
                    ple_dve(dve, s)
                else:
                    mixers[s][2](dve)
            norm_dve(dve, len(stages), "final")


def kernel(**inputs):
    import concourse.bacc as bacc
    from concourse.bass_utils import run_bass_kernel_spmd

    a = {k: np.asarray(v) for k, v in inputs.items()}
    units = [u for s in STAGES for u in stage_units(s, a)]
    arrays = {
        "x_t": np.ascontiguousarray(a["x"][0].T.reshape(KT, P, T).transpose(1, 0, 2)),
        "p_t": np.ascontiguousarray(a["p"][:, 0].transpose(0, 2, 1).reshape(2, 2, P, T).transpose(2, 0, 1, 3)),
        "weights": np.stack(units),
        "parameters": parameter_columns(a),
        "shape_constants": shape_constants(),
    }
    nc = bacc.Bacc("TRN2", target_bir_lowering=False, num_devices=1)
    aps = [nc.dram_tensor(n, v.shape, mybir.dt.float32, kind="ExternalInput").ap() for n, v in arrays.items()]
    out = nc.dram_tensor("out_t", (P, KT, T), mybir.dt.float32, kind="ExternalOutput").ap()
    build(nc, *aps, out)
    r = run_bass_kernel_spmd(nc, [arrays], core_ids=[0])
    y = np.asarray(r.results[0]["out_t"])
    return np.ascontiguousarray(y.transpose(2, 1, 0).reshape(1, T, D))
```

```python
import numpy as np
import concourse.bass as bass
from concourse import mybir
from contextlib import ExitStack

T, P, D = 256, 128, 1024
KT = D // P
NB = T // P
UNIT = 8 * P
RING = 3
TURN = 6
D_FF, D_FF2 = 2816, 4096
FJ, FJ2 = D_FF // P, D_FF2 // P
EPS = 1e-6
NEG, TAKEN = -1e30, -3e38
MLA_H, MLA_QK, MLA_NOPE, MLA_V = 8, 96, 64, 64
GH, GD = 4, 128
DSA_H, DSA_KV, IDX_H, IDX_D, TOPK = 8, 2, 8, 64, 64
RH, RN, RC = 16, 64, 64
LNX_EPS = RN * 1e-5
LOG_DECAY = -float(np.exp(np.float32(-0.5)))

STAGES = ["ffn0", "even", "ffn1", "ple0", "ffn2", "odd", "ffn3", "ple1", "second", "mlp"]
NORM_OF = {"ffn0": "ln_ffn1_0", "even": "ln_mix_0", "ffn1": "ln_ffn2_0", "ple0": "ln_ple_0",
           "ffn2": "ln_ffn1_1", "odd": "ln_mix_1", "ffn3": "ln_ffn2_1", "ple1": "ln_ple_1",
           "second": "norm1", "mlp": "norm2"}

PARAMS = [("ln_ffn1_0", 8), ("ln_mix_0", 8), ("ln_ffn2_0", 8), ("ln_ple_0", 8),
          ("ln_ffn1_1", 8), ("ln_mix_1", 8), ("ln_ffn2_1", 8), ("ln_ple_1", 8),
          ("norm1", 8), ("norm2", 8), ("final", 8),
          ("q_a", 3), ("kv_a", 2), ("mla_q", 1), ("mla_k", 1), ("gconv", 48),
          ("a_log", 1), ("dt_bias", 1), ("out_norm", 1),
          ("dsa_q", 1), ("dsa_k", 1), ("kidx", 1),
          ("merge_b", 24), ("conv_a", 24), ("lru_conv", 32), ("lru_cb", 8), ("lru_ba", 8),
          ("lru_bi", 8), ("lru_a", 8), ("mu", 26), ("w0", 8), ("a0", 8), ("kk", 8), ("ka", 8),
          ("rk", 8), ("lnx_g", 8), ("lnx_b", 8)]
CONSTS = [("ident", 128), ("ones", 128), ("pairs", 128), ("onehot", 31), ("onehot2", 30),
          ("levels", 7 * 128), ("incl", 128), ("strict64", 128),
          ("incl64", 128), ("causal", 256), ("cos", 256), ("sin", 256), ("rot", 96), ("reset64", 256),
          ("rms", 8)]


def offsets(table):
    out, at = {}, 0
    for name, n in table:
        out[name] = (at, n)
        at += n
    return out, at


def shape_constants():
    off, n = offsets(CONSTS)
    c = np.zeros((P, n), np.float32)

    def put(name, a):
        at, _ = off[name]
        a = np.asarray(a, np.float32)
        c[:a.shape[0], at:at + a.shape[1]] = a
    p, i = np.arange(P)[:, None], np.arange(P)[None, :]
    put("ident", p == i)
    put("ones", np.ones((P, P)))
    put("pairs", p // 64 == i // 64)
    oh = np.zeros((P, 31)); oh[:, 15] = 1
    put("onehot", oh)
    oh2 = np.zeros((P, 30)); oh2[:64, 14] = 1; oh2[64:, 15] = 1
    put("onehot2", oh2)
    lv = [(p // (2 * b) == i // (2 * b)) & ((i // b) % 2 == 1) & ((p // b) % 2 == 0)
          for b in (1, 2, 4, 8, 16, 32, 64)]
    put("levels", np.concatenate(lv, 1))
    put("incl", p <= i)
    put("strict64", (p < i) & (p // 64 == i // 64))
    put("incl64", (p <= i) & (p // 64 == i // 64))
    put("causal", np.concatenate([np.zeros((P, P)), np.where(i <= p, 0, NEG)], 1))
    half = 16
    inv = (np.float32(10000.0) ** (-np.arange(half, dtype=np.float32) / np.float32(half))).astype(np.float32)
    ang = (np.arange(T, dtype=np.float32)[None, :] * inv[:, None]).astype(np.float32)
    cos, sin = np.ones((96, T)), np.zeros((96, T))
    cos[64:80], cos[80:96], sin[64:80], sin[80:96] = np.cos(ang), np.cos(ang), np.sin(ang), np.sin(ang)
    put("cos", cos)
    put("sin", sin)
    rot = np.zeros((96, 96))
    for m in range(16):
        rot[80 + m, 64 + m], rot[64 + m, 80 + m] = -1, 1
    put("rot", rot)
    put("reset64", np.tile(np.arange(T) % RC != 0, (P, 1)))
    rms = np.zeros((P, 8), np.float32)
    rms[:, 0], rms[:, 1] = 1.0, EPS
    rms[0, 0], rms[1, 0] = 1 / 384, 1 / 256
    rms[:, 2], rms[:, 3] = 1 / 96, EPS
    rms[:, 4], rms[:, 5] = 1 / 128, EPS
    rms[10, 4] = 1 / 64
    rms[:, 6], rms[:, 7] = 1 / 64, LNX_EPS
    put("rms", rms)
    return c


def columns(v):
    v = np.asarray(v).reshape(-1)
    pad = np.zeros(-(-v.size // P) * P, v.dtype)
    pad[:v.size] = v
    return pad.reshape(-1, P).T


def parameter_columns(a):
    off, n = offsets(PARAMS)
    out = np.zeros((P, n), np.float32)

    def put(name, c):
        at, w = off[name]
        assert c.shape[1] == w, name
        out[:c.shape[0], at:at + w] = c
    for l in range(2):
        for name in ("ln_ffn1", "ln_mix", "ln_ffn2", "ln_ple"):
            put(f"{name}_{l}", columns(a[name][l]))
    put("norm1", columns(a["norm1_g_2"][0]))
    put("norm2", columns(a["norm2_g_2"][0]))
    put("final", columns(a["final_g_2"]))
    put("q_a", columns(a["mla_q_a_norm"][0]))
    put("kv_a", columns(a["mla_kv_a_norm"][0]))
    put("mla_q", columns(a["mla_q_norm"][0]))
    put("mla_k", columns(a["mla_k_norm"][0]))
    put("gconv", np.concatenate([columns(a["gdn_conv_w"][0][j]) for j in range(4)], 1))
    put("a_log", columns(a["gdn_a_log"][0]))
    put("dt_bias", columns(a["gdn_dt_bias"][0]))
    put("out_norm", columns(a["gdn_out_norm"][0]))
    put("dsa_q", columns(a["dsa_q_norm"][0]))
    put("dsa_k", columns(a["dsa_k_norm"][0]))
    put("kidx", columns(np.tile(a["dsa_kidx_norm"][0], 2)))
    put("merge_b", columns(a["merge_b_2"][0]))
    put("conv_a", np.concatenate([columns(a["conv_a_w_2"][0][j]) for j in range(3)], 1))
    put("lru_conv", np.concatenate([columns(a["lru_conv_w_2"][0][j]) for j in range(4)], 1))
    for name, src in (("lru_cb", "lru_conv_b_2"), ("lru_ba", "lru_ba_2"), ("lru_bi", "lru_bi_2"),
                      ("lru_a", "lru_a_param_2"), ("mu", "rwkv_mu_2"), ("w0", "rwkv_w0_2"),
                      ("a0", "rwkv_a0_2"), ("kk", "rwkv_kk_2"), ("ka", "rwkv_ka_2"), ("rk", "rwkv_rk_2"),
                      ("lnx_g", "rwkv_lnx_g_2"), ("lnx_b", "rwkv_lnx_b_2")):
        put(name, columns(a[src][0]))
    return out


def as_unit(m):
    u = np.zeros((P, UNIT), m.dtype)
    k = m.shape[0] // P
    u[:, :k * P] = m.reshape(k, P, P).transpose(1, 0, 2).reshape(P, k * P)
    return u


def tiles_unit(tiles):
    u = np.zeros((P, UNIT), np.float32)
    for i, m in enumerate(tiles):
        u[:m.shape[0], i * P:i * P + m.shape[1]] = m
    return u


def placed(w, parts):
    out = np.zeros((w.shape[0], P), w.dtype)
    for at, first, n in parts:
        out[:, at:at + n] = w[:, first:first + n]
    return out


def col_units(w, first, n):
    return [as_unit(w[:, first + i * P:first + (i + 1) * P]) for i in range(n)]


def ffn_units(gu, down, width, gated):
    out, n = [], width // P
    for j in range(n + 1):
        if j < n:
            out += col_units(gu, j * P, 1)
            if gated:
                out += col_units(gu, width + j * P, 1)
        if j >= 1:
            out.append(np.ascontiguousarray(down[(j - 1) * P:j * P]))
    return out


def stage_units(name, a):
    if name.startswith("ffn"):
        k = int(name[3])
        pre = ("ffn1", "ffn2")[k % 2]
        return ffn_units(a[pre + "_w_gu"][k // 2], a[pre + "_w_down"][k // 2], D_FF, True)
    if name.startswith("ple"):
        l = int(name[3])
        pin = a["ple_w_in"][l]
        return [tiles_unit([pin[k * P:(k + 1) * P, m * P:(m + 1) * P] for m in range(4 * g, 4 * g + 4)
                            for k in range(2)]) for g in range(2)] + col_units(a["ple_w_gate"][l], 0, 8)
    if name == "even":
        w = a["even_w_in"][0]
        out = col_units(w, 0, 5)
        ab = 640 + 32 + 1536 + 512
        out.append(as_unit(placed(w, [(0, ab, 4), (32, ab + 4, 4), (64, 640, 32)])))
        out += col_units(w, 672, 16)
        q, kv = a["mla_w_q_up"][0], a["mla_w_kv_up"][0]
        qt = [q[k * P:(k + 1) * P, h * 96:(h + 1) * 96] for h in range(8) for k in range(3)]
        out += [tiles_unit(qt[8 * i:8 * i + 8]) for i in range(3)]
        kv = kv.reshape(256, 8, 128)
        kn = kv[:, :, :64].reshape(256, 512)
        out.append(tiles_unit([kn[k * P:(k + 1) * P, m * P:(m + 1) * P] for m in range(4) for k in range(2)]))
        vv = kv[:, :, 64:].reshape(256, 512)
        out.append(np.concatenate([vv[:P], vv[P:]], 1))
        return out + col_units(a["even_w_out"][0], 0, 8)
    if name == "odd":
        w = a["odd_w_in"][0]
        out = col_units(w, 0, 10)
        ki = 1024 + 512 + 512
        out.append(as_unit(placed(w, [(0, ki, 64), (64, ki, 64)])))
        out += col_units(w, 1536, 4)
        vw = np.concatenate([w[:, 1280:1536], w[:, ki + 64:ki + 72]], 1).reshape(8, P, 264)
        for ks in ((0, 1, 2), (3, 4, 5), (6, 7)):
            u = np.zeros((P, UNIT), w.dtype)
            for n, k in enumerate(ks):
                u[:, n * 264:(n + 1) * 264] = vw[k]
            out.append(u)
        return out + col_units(a["odd_w_out"][0], 0, 8)
    if name == "second":
        w = a["w_in_2"][0]
        base_c = 3 * D + 2 * D + 3 * D
        out = col_units(w, base_c + 3 * D, 2)
        wa, wi = a["lru_wa_2"][0], a["lru_wi_2"][0]
        for t in range(8):
            cols = [D, 2 * D, 0, 5 * D, 3 * D, 4 * D, 6 * D, None, base_c, base_c + D, base_c + 2 * D, 7 * D]
            for c in cols:
                if c is not None:
                    out += col_units(w, c + t * P, 1)
                    continue
                s = slice(t * P, (t + 1) * P)
                u = np.zeros((P, UNIT), w.dtype)
                u[:64, 0:64], u[64:, 64:128] = wa[2 * t], wa[2 * t + 1]
                u[:64, 128:192], u[64:, 192:256] = wi[2 * t], wi[2 * t + 1]
                u[:64, 256:384] = a["rwkv_w2_2"][0][:, s]
                u[64:, 384:512] = a["rwkv_a2_2"][0][:, s]
                u[:, 512:640] = a["rwkv_g2_2"][0][:, s]
                out.append(u)
        return out + col_units(a["w_out_2"][0], 0, 8)
    assert name == "mlp"
    return ffn_units(a["mlp_w1_2"][0], a["mlp_w2_2"][0], D_FF2, False)


UNITS_OF = {"ffn": 3 * FJ, "ple": 10, "eve": 22 + 5 + 8, "odd": 18 + 8, "sec": 2 + 96 + 8, "mlp": 2 * FJ2}


class Steps:

    def __init__(self, sem, names):
        self.sem, self.names, self.n = sem, list(names), 0
        assert len(set(self.names)) == len(self.names)

    def step(self, name):
        assert self.names[self.n] == name, (name, self.names[self.n])
        self.n += 1
        return 1

    def after(self, name):
        return self.names.index(name) + 1


def build(nc, a_x, a_p, a_w, a_par, a_con, out, stages=STAGES):
    f32 = mybir.dt.float32
    ALU, ACT, AX = mybir.AluOpType, mybir.ActivationFunctionType, mybir.AxisListType
    MUL, ADD, SUB, MAXOP, MINOP = ALU.mult, ALU.add, ALU.subtract, ALU.max, ALU.min
    par_off, par_n = offsets(PARAMS)
    con_off, con_n = offsets(CONSTS)
    unit_base, total_units = {}, 0
    for s in stages:
        unit_base[s] = total_units
        total_units += UNITS_OF[s[:3]]

    ctx = ExitStack()
    with ctx:
        def sb(name, shape):
            return ctx.enter_context(nc.sbuf_tensor(name, shape, f32))

        def sem(name):
            return ctx.enter_context(nc.semaphore(name))

        def sbr(name, shape):
            return ctx.enter_context(nc.sbuf_tensor(name, shape, mybir.dt.float32r))

        x = sb("x", [P, KT, T])
        h_hi, h_lo = sbr("h_hi", [P, KT, T]), sbr("h_lo", [P, KT, T])
        raw = sb("raw", [P, RING, UNIT])
        w_hi, w_lo = sbr("w_hi", [P, RING, UNIT]), sbr("w_lo", [P, RING, UNIT])
        a_hi, a_lo = sbr("a_hi", [P, 3, T]), sbr("a_lo", [P, 3, T])
        par = sb("par", [P, par_n])
        con = sb("con", [P, con_n])
        rstd = sb("rstd", [P, T])
        root_of = sb("root_of_a_constant", [P, 1])
        ps = ctx.enter_context(nc.psum_tensor("ps", [P, 8, 512], f32))
        ARENA = 31736
        arena = sb("arena", [P, ARENA])

        def f(ap):
            return ap.bitcast(f32)

        class Carve:
            def __init__(self):
                self.at = 0

            def __call__(self, *shape):
                n = int(np.prod(shape))
                ap = arena[:, self.at:self.at + n]
                self.at += n
                assert self.at <= ARENA, self.at
                names = " ".join("abcd"[:len(shape)])
                if len(shape) == 1:
                    return ap
                return ap.rearrange(f"p ({names}) -> p {names}", **dict(zip("abcd", shape)))

        def C(name):
            at, n = con_off[name]
            return con[:, at:at + n]

        def G(name, i=0, rows=P):
            at = par_off[name][0] + i
            return par[0:rows, at:at + 1]

        def over(ap, n):
            return ap.unsqueeze(1).to_broadcast([ap.shape[0], n, ap.shape[1]])

        def each(ap, n):
            return ap.unsqueeze(2).to_broadcast([ap.shape[0], ap.shape[1], n])

        ident, ones, pairs = C("ident"), C("ones"), C("pairs")
        whole = arena[:, 0:KT * T].rearrange("p (a b) -> p a b", a=KT)

        def sel(n, r0=0, r1=16, m=P):
            return ident[r0:r1, r0 + n:r0 + n + 1].to_broadcast([r1 - r0, m])
        levels = C("levels").rearrange("p (n m) -> p n m", n=7)

        arrived = [sem(f"weights_in_{s}") for s in range(RING)]
        s_hi, s_lo, s_prod = sem("hi_ready"), sem("lo_ready"), sem("products_done")
        s_const, s_out, s_pin = sem("constants_in"), sem("out_stored"), sem("p_in")
        s_x = sem("x_ready")
        s_sq, s_sum, s_sd = sem("norm_squares"), sem("norm_sum"), sem("norm_sqrt")
        s_nrm, s_hr, s_h = sem("normed"), sem("h_rounded"), sem("h_ready")
        s_vc = sem("vector_chain")
        s_nl, s_act = sem("nonlinearity_done"), sem("ffn_act_ready")
        s_mul, s_rnd = sem("ffn_act_multiplied"), sem("ffn_act_rounded")
        s_p = sem("p_split")
        s_gate, s_pw = sem("ple_gate_ready"), sem("ple_tile_added")
        s_add = sem("projection_added")
        order = {s: n for n, s in enumerate(stages)}
        n_ple = {s: n for n, s in enumerate([s for s in stages if s[:3] == "ple"])}
        n_lin = {s: n for n, s in enumerate([s for s in stages if s in ("even", "odd", "second")])}
        ffn_j0, at = {}, 0
        for s in stages:
            ffn_j0[s] = at
            at += FJ if s[:3] == "ffn" else FJ2 if s == "mlp" else 0

        def sems_of(stage):
            return sem(stage + "_tensor_steps"), sem(stage + "_scalar_steps"), sem(stage + "_vector_steps")

        V, A, TE = nc.vector, nc.scalar, nc.tensor
        
        class Links:
            n = 0

            def step(self):
                self.n += 1
                return 1
        vc = Links()

        def loads(u, i=None):
            v = 16 * (u // RING + 1)
            return v if i is None else i * (16 * TURN // RING) + v

        def nth(u, i=None):
            return u + 1 if i is None else i * TURN + (u + 1)

        split_next = {"act": 0, "dve": 0}

        def act_split(act, last, i=None):
            for u in range(split_next["act"], min(last + 1, total_units)):
                act.wait_ge(arrived[u % RING], loads(u, i))
                if u >= RING:
                    act.wait_ge(s_prod, nth(u - RING, i))
                A.activation(w_hi[:, u % RING, :], raw[:, u % RING, :], ACT.Copy).then_inc(s_hi, 1)
                split_next["act"] = u + 1

        def dve_split(dve, last, i=None):
            for u in range(split_next["dve"], min(last + 1, total_units)):
                dve.wait_ge(s_hi, nth(u, i))
                V.tensor_tensor(w_lo[:, u % RING, :], raw[:, u % RING, :], f(w_hi[:, u % RING, :]), SUB)\
                    .then_inc(s_lo, 1)
                split_next["dve"] = u + 1

        def cut(ap_hi, ap_lo, src):
            V.tensor_copy(ap_hi, src).then_inc(s_vc, vc.step())
            V.wait_ge(s_vc, vc.n)
            return V.tensor_tensor(ap_lo, src, f(ap_hi), SUB)

        def mm(o, lhsT, rhs, start=True, stop=True):
            return TE.matmul(o, lhsT, rhs, start=start, stop=stop, skip_group_check=True)

        def mm3(o, l_hi, l_lo, r_hi, r_lo, start=True, stop=True):
            mm(o, l_lo, r_hi, start, False)
            mm(o, l_hi, r_lo, False, False)
            return mm(o, l_hi, r_hi, False, stop)

        def wmm(o, u, k, hi, lo, start=True, stop=True):
            c_ = slice(k * P, k * P + P)
            return mm3(o, w_hi[:, u % RING, c_], w_lo[:, u % RING, c_], hi, lo, start, stop)

        def linear(pe, u, o, i=None, norm=None):
            hi, lo = h_hi, h_lo
            pe.wait_ge(s_lo, nth(u, i))
            for k in range(KT):
                if norm is not None and k % 2 == 0:
                    pe.wait_ge(s_h, 4 * norm + k // 2 + 1)
                last = wmm(o, u, k, hi[:, k, :], lo[:, k, :], k == 0, k == KT - 1)
            last.then_inc(s_prod, 1)

        eps_col = con[:, con_off["rms"][0] + 1:con_off["rms"][0] + 2]

        def pair_of(p_):
            return slice(2 * p_, 2 * p_ + 2)

        def norm_act(act, n):
            for p_ in range(4):
                if n:
                    act.wait_ge(s_x, 4 * (n - 1) + p_ + 1)
                A.activation(whole[:, pair_of(p_), :], x[:, pair_of(p_), :], ACT.Square).then_inc(s_sq, 1)
            if n == 0:
                act_split(act, 2)
            A.activation(root_of[:, :], ones[:, 0:1], ACT.Sqrt)
            act.wait_ge(s_sum, n + 1)
            A.activation(rstd[:, :], ps[:, 7, 0:T], ACT.Sqrt, bias=eps_col, scale=1.0 / D).then_inc(s_sd, 1)
            if n == len(stages):
                return
            for p_ in range(4):
                act.wait_ge(s_nrm, 4 * n + p_ + 1)
                A.activation(h_hi[:, pair_of(p_), :], whole[:, pair_of(p_), :], ACT.Copy).then_inc(s_hr, 1)
            act_split(act, unit_base[stages[n]] + 2)

        def norm_pe(pe, n):
            for k in range(KT):
                if k % 2 == 0:
                    pe.wait_ge(s_sq, 4 * n + k // 2 + 1)
                last = mm(ps[:, 7, 0:T], ones, whole[:, k, :], k == 0, k == KT - 1)
            last.then_inc(s_sum, 1)

        def norm_dve(dve, n, name):
            if n == 0:
                dve_split(dve, 2)
            dve.wait_ge(s_sd, n + 1)
            V.reciprocal(rstd[:, :], rstd[:, :]).then_inc(s_vc, vc.step())
            V.wait_ge(s_vc, vc.n)

            def rest(p_):
                dve.wait_ge(s_hr, 4 * n + p_ + 1)
                V.tensor_tensor(h_lo[:, pair_of(p_), :], whole[:, pair_of(p_), :],
                                f(h_hi[:, pair_of(p_), :]), SUB).then_inc(s_h, 1)
            for p_ in range(4):
                for k in (2 * p_, 2 * p_ + 1):
                    last = V.scalar_tensor_tensor(whole[:, k, :], x[:, k, :], G(name, k), rstd[:, :], MUL, MUL)
                last.then_inc(s_nrm, 1)
                if p_ and n < len(stages):
                    rest(p_ - 1)
            if n < len(stages):
                rest(3)
                dve_split(dve, unit_base[stages[n]] + 2)

        sg, ab = (arena[:, at:at + 3 * T].rearrange("p (a b) -> p a b", a=3) for at in (2560, 2560 + 3 * T))

        class Ffn:
            def __init__(self, stage):
                self.gated = stage != "mlp"
                self.per, self.n = (3, FJ) if self.gated else (2, FJ2)
                self.bufs = TURN // self.per
                self.u0, self.j0, self.norm = unit_base[stage], ffn_j0[stage], order[stage]
                self.rounds = (self.n - 2) // self.bufs - (stages[-1] == stage)

            def up(self, j):
                return self.u0 + (self.per * j - 1 if j else 0)

            def down(self, j):
                return self.u0 + (self.per * (j + 2) - 2 if j < self.n - 1 else self.per * self.n - 1)

            def ahead(self, j):
                return self.u0 + (self.per + 1 if j == 0 else self.per * j + self.per + 1)

        def turns(eng, f_, who, body):
            body(0, None)
            body(1, None)
            at_ = split_next.get(who)
            with eng.Fori(0, f_.rounds) as i:
                for j in range(2, 2 + f_.bufs):
                    body(j, i)
            if who in split_next:
                split_next[who] = at_ + TURN * f_.rounds
            for j in range(2 + f_.bufs * f_.rounds, f_.n):
                body(j, None)

        def count(f_, j, i):
            return f_.j0 + j + 1 if i is None else i * f_.bufs + (f_.j0 + j + 1)

        def ffn_pe(pe, f_):
            def down(j, i):
                pe.wait_ge(s_act, count(f_, j, i))
                u = f_.down(j)
                pe.wait_ge(s_lo, nth(u, i))
                for m in range(KT):
                    first = j == 0 and m % 2 == 0
                    last = wmm(ps[:, m // 2, m % 2 * T:m % 2 * T + T], u, m, a_hi[:, j % f_.bufs, :],
                               a_lo[:, j % f_.bufs, :], first, j == f_.n - 1)
                last.then_inc(s_prod, 1)

            def body(j, i):
                if j >= f_.bufs:
                    pe.wait_ge(s_act, count(f_, j - f_.bufs, i))
                for half in range(f_.per - 1):
                    linear(pe, f_.up(j) + half, ps[:, 4 + j % f_.bufs, half * T:half * T + T], i=i,
                           norm=f_.norm if j + half == 0 else None)
                if j >= 1:
                    down(j - 1, i)
            turns(pe, f_, "pe", body)
            down(f_.n - 1, None)

        def ffn_act(act, f_):
            def body(j, i):
                if f_.gated:
                    act_split(act, f_.ahead(j) - 2, i)
                act.wait_ge(s_prod, nth(f_.up(j) + f_.per - 2, i))
                if j >= f_.bufs:
                    act.wait_ge(s_act, count(f_, j - f_.bufs, i))
                A.activation(sg[:, j % f_.bufs, :], ps[:, 4 + j % f_.bufs, 0:T],
                             ACT.Silu if f_.gated else ACT.Relu).then_inc(s_nl, 1)
                act_split(act, f_.ahead(j), i)
            turns(act, f_, "act", body)

        def ffn_dve(dve, f_):
            def body(j, i):
                if f_.gated:
                    dve_split(dve, f_.ahead(j) - 2, i)
                dve.wait_ge(s_nl, count(f_, j, i))
                if j >= f_.bufs:
                    dve.wait_ge(s_prod, nth(f_.down(j - f_.bufs), i))
                b_, o = sg[:, j % f_.bufs, :], ab[:, j % f_.bufs, :]
                V.tensor_tensor(o, b_, ps[:, 4 + j % f_.bufs, T:2 * T] if f_.gated else b_, MUL).then_inc(s_mul, 1)
                dve.wait_ge(s_mul, count(f_, j, i))
                V.tensor_copy(a_hi[:, j % f_.bufs, :], o).then_inc(s_rnd, 1)
                dve.wait_ge(s_rnd, count(f_, j, i))
                V.tensor_tensor(a_lo[:, j % f_.bufs, :], o, f(a_hi[:, j % f_.bufs, :]), SUB).then_inc(s_act, 1)
                dve_split(dve, f_.ahead(j), i)
            turns(dve, f_, "dve", body)
            dve.wait_ge(s_prod, nth(f_.down(f_.n - 1)))
            for b in range(4):
                V.scalar_tensor_tensor(x[:, pair_of(b), :], ps[:, b, :].rearrange("p (a t) -> p a t", a=2),
                                       0.5 if f_.gated else 1.0, x[:, pair_of(b), :], MUL, ADD).then_inc(s_x, 1)

        pin = arena[:, KT * T:KT * T + 2 * T].rearrange("p (a b) -> p a b", a=2)

        def ple_in_dve(dve, s):
            dve.wait_ge(s_pin, 16 * (n_ple[s] + 1))
            cut(a_hi[:, 0:2, :], a_lo[:, 0:2, :], pin).then_inc(s_p, 1)

        def ple_in_pe(pe, s):
            if order[s]:
                pe.wait_ge(s_x, 4 * order[s])
            pe.wait_ge(s_p, n_ple[s] + 1)
            for g in range(2):
                u = unit_base[s] + g
                pe.wait_ge(s_lo, nth(u))
                for m in range(4 * g, 4 * g + 4):
                    for k in range(2):
                        last = wmm(ps[:, m // 2, m % 2 * T:m % 2 * T + T], u, (m % 4) * 2 + k,
                                   a_hi[:, k, :], a_lo[:, k, :], k == 0, k == 1)
                last.then_inc(s_prod, 1)

        def ple_pe(pe, s):
            base = 8 * n_ple[s]
            for m in range(KT):
                if m >= 3:
                    pe.wait_ge(s_gate, base + m - 2)
                linear(pe, unit_base[s] + 2 + m, ps[:, 4 + m % 3, 0:T], norm=None if m else order[s])

        def ple_act(act, s):
            base = 8 * n_ple[s]
            for m in range(KT):
                u = unit_base[s] + 2 + m
                act_split(act, u + 2)
                act.wait_ge(s_prod, nth(u))
                if m >= 3:
                    act.wait_ge(s_pw, base + m - 2)
                A.activation(sg[:, m % 3, :], ps[:, 4 + m % 3, 0:T], ACT.Sigmoid).then_inc(s_gate, 1)

        def ple_dve(dve, s):
            base = 8 * n_ple[s]
            for m in range(KT):
                dve_split(dve, unit_base[s] + 4 + m)
                dve.wait_ge(s_gate, base + m + 1)
                V.tensor_tensor(ab[:, m % 3, :], sg[:, m % 3, :],
                                ps[:, m // 2, m % 2 * T:m % 2 * T + T], MUL).then_inc(s_pw, 1)
                dve.wait_ge(s_pw, base + m + 1)
                last = V.tensor_tensor(x[:, m, :], x[:, m, :], ab[:, m % 3, :], ADD)
                if m % 2:
                    last.then_inc(s_x, 1)

        def out_pe(pe, s, u0):
            for m in range(KT):
                if m >= 3 and m % 2:
                    pe.wait_ge(s_add, 4 * n_lin[s] + (m - 3) // 2 + 1)
                elif m >= 3:
                    pe.wait_ge(s_x, 4 * order[s] + (m - 3) // 2 + 1)
                linear(pe, u0 + m, ps[:, 4 + m % 3, 0:T])

        def out_act(act, u0):
            act_split(act, u0 + KT + 1)

        def out_dve(dve, s, u0):
            for m in range(KT):
                dve_split(dve, u0 + m + 2)
                dve.wait_ge(s_prod, nth(u0 + m))
                V.tensor_tensor(x[:, m, :], x[:, m, :], ps[:, 4 + m % 3, 0:T], ADD)\
                    .then_inc(s_x if m % 2 else s_add, 1)

        class Att:
            def __init__(self, S, PT, mx, sm, q, k, v, o, evac, scale, mask):
                self.S, self.PT, self.mx, self.sm = S, PT, mx, sm
                self.q, self.k, self.v, self.o, self.evac = q, k, v, o, evac
                self.scale, self.mask = scale, mask

            def scores(self, qb):
                nk = (qb + 1) * P
                return self.S.rearrange("p a b -> p (a b)")[:, 0:8 * nk].rearrange("p (a b) -> p a b", b=nk)

        def att_steps():
            pe = [f"{n}{qb}_{b}" for qb in range(2) for n, k in (("s", 2 * qb + 2), ("t", 2 * qb + 2), ("o", 1))
                  for b in range(k)]
            act = [n for qb in range(2) for n in [f"exp{qb}"] + [f"pt{qb}_{b}" for b in range(2 * qb + 2)]]
            dve = [f"{n}{qb}" for qb in range(2) for n in ("max", "prob", "out")]
            return pe, act, dve

        def att_pe(pe, a, pe_s, act_s, dve_s):
            for qb in range(2):
                per = 4 // (qb + 1)
                nk = (qb + 1) * P
                if qb:
                    pe.wait_ge(dve_s.sem, dve_s.after("out0"))
                for b in range(2 * qb + 2):
                    for n in range(per):
                        hd = b * per + n
                        last = mm(ps[:, b, n * nk:(n + 1) * nk], a.q(hd, qb), a.k(hd, nk))
                    last.then_inc(pe_s.sem, pe_s.step(f"s{qb}_{b}"))
                pe.wait_ge(dve_s.sem, dve_s.after(f"prob{qb}"))
                S = a.scores(qb)
                for i in range(8 * (qb + 1)):
                    hd, kb = i // (qb + 1), i % (qb + 1)
                    last = TE.transpose(ps[:, 4 + i // 4, i % 4 * P:i % 4 * P + P],
                                        S[:, hd, kb * P:kb * P + P], ident)
                    if i % 4 == 3:
                        last.then_inc(pe_s.sem, pe_s.step(f"t{qb}_{i // 4}"))
                for hd in range(8):
                    i = hd * (qb + 1)
                    pe.wait_ge(act_s.sem, act_s.after(f"pt{qb}_{(i + qb) // 4}"))
                    for kb in range(qb + 1):
                        last = mm(a.o(hd), a.v(hd, kb), a.PT[:, i + kb, :], kb == 0, kb == qb)
                last.then_inc(pe_s.sem, pe_s.step(f"o{qb}_0"))

        def att_act(act, a, pe_s, act_s, dve_s):
            for qb in range(2):
                act.wait_ge(dve_s.sem, dve_s.after(f"max{qb}"))
                S = a.scores(qb)
                for hd in range(8):
                    last = A.activation(S[:, hd, :], S[:, hd, :], ACT.Exp, bias=a.mx[:, hd:hd + 1],
                                        accum_out=a.sm[:, hd:hd + 1])
                last.then_inc(act_s.sem, act_s.step(f"exp{qb}"))
                for b in range(2 * qb + 2):
                    act.wait_ge(pe_s.sem, pe_s.after(f"t{qb}_{b}"))
                    A.activation(a.PT[:, 4 * b:4 * b + 4, :],
                                            ps[:, 4 + b, :].rearrange("p (a b) -> p a b", a=4), ACT.Copy).then_inc(act_s.sem, act_s.step(f"pt{qb}_{b}"))

        def att_dve(dve, a, pe_s, act_s, dve_s):
            for qb in range(2):
                per, nk = 4 // (qb + 1), (qb + 1) * P
                S = a.scores(qb)
                if qb:
                    dve.wait_ge(pe_s.sem, pe_s.after("t0_1"))
                for b in range(2 * qb + 2):
                    dve.wait_ge(pe_s.sem, pe_s.after(f"s{qb}_{b}"))
                    last = V.scalar_tensor_tensor(S[:, b * per:(b + 1) * per, :],
                                                  ps[:, b, :].rearrange("p (a b) -> p a b", b=nk), a.scale,
                                                  over(a.mask(qb), per), MUL, ADD)
                last.then_inc(s_vc, vc.step())
                V.wait_ge(s_vc, vc.n)
                V.tensor_reduce(a.mx, S, AX.X, MAXOP).then_inc(s_vc, vc.step())
                V.wait_ge(s_vc, vc.n)
                V.tensor_scalar(a.mx, a.mx, -1.0, None, MUL).then_inc(dve_s.sem, dve_s.step(f"max{qb}"))
                dve.wait_ge(act_s.sem, act_s.after(f"exp{qb}"))
                V.reciprocal(a.sm, a.sm).then_inc(s_vc, vc.step())
                V.wait_ge(s_vc, vc.n)
                V.tensor_tensor(S, S, each(a.sm, nk), MUL).then_inc(dve_s.sem, dve_s.step(f"prob{qb}"))
                dve.wait_ge(pe_s.sem, pe_s.after(f"o{qb}_0"))
                a.evac(qb).then_inc(dve_s.sem, dve_s.step(f"out{qb}"))

        def even_mixer():
            u0 = unit_base["even"]
            cv = Carve()
            low = cv(5, T)
            misc = cv(T)
            qkv = cv(12, T)
            zs = cv(4, T)
            sq = cv(16, T)
            rr = cv(T)
            og = cv(4, T)
            mark = cv.at
            qT, kT = cv(8, T), cv(8, T)
            vm = cv(2, 512)
            S, PT = cv(8, T), cv(16, P)
            mx, sm = cv(8), cv(8)
            tmp = cv(2, T)
            cv.at = mark
            gcB, beB, egB = cv(4, T), cv(4, T), cv(4, T)
            gcol, bcol = cv(NB, 4), cv(NB, 4)
            dl = cv(NB, 4)
            ktok, vtok = cv(NB, 4, P), cv(NB, 4, P)
            Dm, AT, QK = cv(NB, 4, P), cv(NB, 4, P), cv(NB, 4, P)
            X, Ti, TT, Y = cv(NB, 4, P), cv(NB, 4, P), cv(NB, 4, P), cv(NB, 4, P)
            kbg, qg = cv(4, T), cv(4, T)
            rhs, vn, St = cv(4, P), cv(4, P), cv(4, P)
            tensor_done, scalar_done, vector_done = sems_of("even")
            ape, aact, advn = att_steps()
            LV = 7
            pe_names = (["n1", "bc1", "n2"] + [x_ for p in range(8) for x_ in (f"b2_{p}", f"rot{p}")] + ape
                        + ["gb"] + ["gcol", "kk0", "kk1", "tr0", "tr1", "tr2", "tr3"]
                        + [f"{n}{l}_{c}" for l in range(LV) for n in ("y", "inv") for c in range(NB)]
                        + ["vn0", "og0", "st0", "ks1", "vn1", "og1"] + ["n3", "bc3"])
            act_names = (["low", "misc", "z0", "z1", "z2", "z3", "qkv", "sq1", "sd1", "q0", "q1", "q2", "q3", "k", "sq2", "sd2"]
                         + aact + ["gabs", "gexp", "gln", "beta", "eg", "dm0", "dm1", "edl", "ktr0", "ktr1"]
                         + ["sq3", "sd3"])
            dve_names = ([f"cv{n}" for n in range(12)] + ["r1", "lown", "l2", "kn", "r2"]
                         + [x_ for p in range(8) for x_ in (f"nm{p}", f"rope{p}")] + advn
                         + ["g", "gc", "kk", "gcols", "dd0", "dd1", "aqk", "vb",  "x0"]
                         + [f"{n}{l}_{c}" for l in range(LV) for n in ("yc", "tc") for c in range(NB)]
                         + ["r0", "v0", "o0", "s0", "r1b", "v1", "o1", "r3", "ob"])
            tensor = Steps(tensor_done, pe_names)
            scalar = Steps(scalar_done, act_names)
            vector = Steps(vector_done, dve_names)

            def o_tile(hd):
                return ps[64 * (hd % 2):64 * (hd % 2) + 64, 0, hd // 2 * P:hd // 2 * P + P]

            def evac(qb):
                o, src = (slice(0, P), slice(0, 4), slice(qb * P, qb * P + P)), \
                    ps[:, 0, :].rearrange("p (a b) -> p a b", a=4)
                return cut(h_hi[o], h_lo[o], src)
            causal = C("causal")
            att = Att(S, PT, mx, sm,
                      lambda hd, qb: qT[0:96, hd, qb * P:qb * P + P], lambda hd, nk: kT[0:96, hd, 0:nk],
                      lambda hd, kb: vm[:, kb, hd * 64:hd * 64 + 64], o_tile, evac, MLA_QK ** -0.5,
                      lambda qb: causal[:, P - qb * P:2 * P])
            rms = C("rms")
            in_bank = lambda n: 4 + n % 3
            pair_bank = (6, 7, 0, 1)

            def pair(b, rows=P):
                return ps[0:rows, b, :].rearrange("p (a b) -> p a b", a=2)

            def in_read(eng, n):
                if n < 5:
                    eng.wait_ge(scalar_done, scalar.after("low"))
                elif n == 5:
                    eng.wait_ge(scalar_done, scalar.after("misc"))
                elif n < 18:
                    eng.wait_ge(vector_done, vector.after(f"cv{n - 6}"))
                else:
                    eng.wait_ge(scalar_done, scalar.after(f"z{n - 18}"))

            def blk(c):
                return slice(c * P, (c + 1) * P)

            def pe_prog(pe):
                for n in range(22):
                    if n < 5:
                        b = n
                    else:
                        b = 5 + (n - 5) % 3
                        if n >= 8:
                            in_read(pe, n - 3)
                    linear(pe, u0 + n, ps[:, b, 0:T], norm=None if n else order["even"])
                pe.wait_ge(scalar_done, scalar.after("sq1"))
                for n in range(13):
                    row = 0 if n < 3 else 1 if n < 5 else n - 3
                    last = mm(ps[0:16, 0, 0:T], C("onehot")[:, 15 - row:31 - row], sq[:, n, :], n == 0, n == 12)
                last.then_inc(tensor_done, tensor.step("n1"))
                pe.wait_ge(vector_done, vector.after("r1"))
                in_read(pe, 21)
                for r in range(10):
                    last = mm(ps[:, 1 + r // 2, r % 2 * T:r % 2 * T + T], sel(r), rr[0:16, :])
                last.then_inc(tensor_done, tensor.step("bc1"))
                pe.wait_ge(vector_done, vector.after("lown"))
                for hd in range(8):
                    for k in range(3):
                        t = hd * 3 + k
                        if t % 8 == 0:
                            pe.wait_ge(s_lo, nth(u0 + 22 + t // 8))
                        sl, c_ = (u0 + 22 + t // 8) % RING, slice(t % 8 * P, t % 8 * P + 96)
                        last = mm3(ps[0:96, pair_bank[hd // 2], hd % 2 * T:hd % 2 * T + T], w_hi[:, sl, c_],
                                   w_lo[:, sl, c_], h_hi[:, k, :], h_lo[:, k, :], k == 0, k == 2)
                        if t % 8 == 7:
                            last.then_inc(s_prod, 1)
                pe.wait_ge(vector_done, vector.after("l2"))
                pe.wait_ge(s_lo, nth(u0 + 25))
                for m in range(4):
                    for k in range(2):
                        last = wmm(ps[:, 2 + m, 0:T], u0 + 25, 2 * m + k, h_hi[:, 3 + k, :], h_lo[:, 3 + k, :],
                                   k == 0, k == 1)
                last.then_inc(s_prod, 1)
                pe.wait_ge(s_lo, nth(u0 + 26))
                pe.wait_ge(scalar_done, scalar.after("q1"))
                for tb in range(NB):
                    for k in range(2):
                        sl, c_ = (u0 + 26) % RING, slice(k * 512, (k + 1) * 512)
                        last = mm3(ps[:, 6 + tb, :], h_hi[:, 3 + k, blk(tb)], h_lo[:, 3 + k, blk(tb)],
                                   w_hi[:, sl, c_], w_lo[:, sl, c_], k == 0, k == 1)
                last.then_inc(s_prod, 1)
                pe.wait_ge(scalar_done, scalar.after("sq2"))
                for n in range(16):
                    last = mm(ps[0:16, 0, 0:T], C("onehot")[0:96, 15 - n:31 - n], sq[0:96, n, :], n == 0, n == 15)
                last.then_inc(tensor_done, tensor.step("n2"))
                pe.wait_ge(vector_done, vector.after("r2"))
                for p_ in range(8):
                    if p_ >= 2:
                        pe.wait_ge(vector_done, vector.after(f"nm{p_ - 2}"))
                    for r in (2 * p_, 2 * p_ + 1):
                        last = mm(ps[0:96, 1 + p_ % 2, r % 2 * T:r % 2 * T + T], sel(r, m=96), rr[0:16, :])
                    last.then_inc(tensor_done, tensor.step(f"b2_{p_}"))
                    pe.wait_ge(vector_done, vector.after(f"nm{p_}"))
                    src = (qT if p_ < 4 else kT)[0:96, p_ % 4 * 2:p_ % 4 * 2 + 2, :]
                    mm(ps[0:96, 3 + p_ % 2, :], C("rot")[0:96, :], src).then_inc(tensor_done, tensor.step(f"rot{p_}"))
                pe.wait_ge(vector_done, vector.after("rope7"))
                att_pe(pe, att, tensor, scalar, vector)
                pe.wait_ge(vector_done, vector.after("gc"))
                pe.wait_ge(scalar_done, scalar.after("beta"))
                for g in range(4):
                    mm(ps[:, 4 + g // 2, g % 2 * T:g % 2 * T + T], sel(g, 0, 4), rr[0:4, :])
                    last = mm(ps[:, 6 + g // 2, g % 2 * T:g % 2 * T + T], sel(g, 32, 36), rr[32:36, :])
                last.then_inc(tensor_done, tensor.step("gb"))
                for c in range(NB):
                    mm(ps[:, 0, 4 * c:4 * c + 4], rr[0:4, blk(c)], ident[0:4, 0:4])
                    last = mm(ps[:, 1, 4 * c:4 * c + 4], rr[32:36, blk(c)], ident[32:36, 32:36])
                last.then_inc(tensor_done, tensor.step("gcol"))
                pe.wait_ge(vector_done, vector.after("gcols"))
                pe.wait_ge(scalar_done, scalar.after("eg"))
                pe.wait_ge(vector_done, vector.after("kk"))
                for c in range(NB):
                    for g in range(4):
                        k_, q_ = qkv[:, 4 + g, blk(c)], qkv[:, g, blk(c)]
                        mm(ps[:, c, g * P:g * P + P], k_, k_)
                        last = mm(ps[:, 2 + c, g * P:g * P + P], k_, q_)
                    last.then_inc(tensor_done, tensor.step(f"kk{c}"))
                for c in range(NB):
                    for j in range(2):
                        for g in range(4):
                            last = TE.transpose(ps[:, 4 + 2 * c + j, g * P:g * P + P],
                                                qkv[:, 4 + 4 * j + g, blk(c)], ident)
                        last.then_inc(tensor_done, tensor.step(f"tr{2 * c + j}"))
                pe.wait_ge(vector_done, vector.after("vb"))
                pe.wait_ge(scalar_done, scalar.after("ktr1"))
                for l in range(LV):
                    for c in range(NB):
                        if l == 0:
                            pe.wait_ge(vector_done, vector.after("x0"))
                        else:
                            pe.wait_ge(vector_done, vector.after(f"tc{l - 1}_{c}"))
                        for g in range(4):
                            last = mm(ps[:, c, g * P:g * P + P], X[:, c, g, :], Ti[:, c, g, :])
                        last.then_inc(tensor_done, tensor.step(f"y{l}_{c}"))
                    for c in range(NB):
                        pe.wait_ge(vector_done, vector.after(f"yc{l}_{c}"))
                        for g in range(4):
                            mm(ps[:, 2 + c, g * P:g * P + P], TT[:, c, g, :], Y[:, c, g, :])
                            last = mm(ps[:, 4 + c, g * P:g * P + P], Y[:, c, g, :], TT[:, c, g, :])
                        last.then_inc(tensor_done, tensor.step(f"inv{l}_{c}"))
                for c in range(NB):
                    if c:
                        pe.wait_ge(vector_done, vector.after("s0"))
                        for g in range(4):
                            last = mm(ps[:, 6, g * P:g * P + P], kbg[:, g, blk(c)], St[:, g, :])
                        last.then_inc(tensor_done, tensor.step("ks1"))
                    pe.wait_ge(vector_done, vector.after("r0" if c == 0 else "r1b"))
                    for g in range(4):
                        last = mm(ps[:, 7, g * P:g * P + P], TT[:, c, g, :], rhs[:, g, :])
                    last.then_inc(tensor_done, tensor.step(f"vn{c}"))
                    pe.wait_ge(vector_done, vector.after(f"v{c}"))
                    for g in range(4):
                        if c:
                            mm(ps[:, c, g * P:g * P + P], St[:, g, :], qg[:, g, blk(c)], True, False)
                        last = mm(ps[:, c, g * P:g * P + P], vn[:, g, :], QK[:, c, g, :], c == 0, True)
                    last.then_inc(tensor_done, tensor.step(f"og{c}"))
                    if c == 0:
                        for g in range(4):
                            last = mm(ps[:, 5, g * P:g * P + P], ktok[:, 0, g, :], vn[:, g, :])
                        last.then_inc(tensor_done, tensor.step("st0"))
                pe.wait_ge(scalar_done, scalar.after("sq3"))
                for g in range(4):
                    last = mm(ps[0:16, 2, 0:T], C("onehot")[:, 15 - g:31 - g], sq[:, g, :], g == 0, g == 3)
                last.then_inc(tensor_done, tensor.step("n3"))
                pe.wait_ge(vector_done, vector.after("r3"))
                for g in range(4):
                    last = mm(ps[:, 3 + g // 2, g % 2 * T:g % 2 * T + T], sel(g, 0, 4), rr[0:4, :])
                last.then_inc(tensor_done, tensor.step("bc3"))
                pe.wait_ge(vector_done, vector.after("ob"))
                out_pe(pe, "even", u0 + 27)

            def act_prog(act):
                for n in range(5):
                    act_split(act, u0 + n + 2)
                    act.wait_ge(s_prod, nth(u0 + n))
                    A.activation(low[:, n, :], ps[:, n, 0:T], ACT.Copy)
                    last = A.activation(sq[:, n, :], ps[:, n, 0:T], ACT.Square)
                last.then_inc(scalar_done, scalar.step("low"))
                act_split(act, u0 + 7)
                act.wait_ge(s_prod, nth(u0 + 5))
                A.activation(misc, ps[:, 5, 0:T], ACT.Copy).then_inc(scalar_done, scalar.step("misc"))
                for n in range(18, 22):
                    act_split(act, u0 + n + 2)
                    act.wait_ge(s_prod, nth(u0 + n))
                    A.activation(zs[:, n - 18, :], ps[:, 5 + (n - 5) % 3, 0:T], ACT.Silu).then_inc(scalar_done, scalar.step(f"z{n - 18}"))
                act_split(act, u0 + 24)
                act.wait_ge(vector_done, vector.after("cv11"))
                A.activation(qkv, qkv, ACT.Silu).then_inc(scalar_done, scalar.step("qkv"))
                act.wait_ge(scalar_done, scalar.after("qkv"))
                A.activation(sq[:, 5:13, :], qkv[:, 0:8, :], ACT.Square).then_inc(scalar_done, scalar.step("sq1"))
                act.wait_ge(tensor_done, tensor.after("n1"))
                A.activation(rr[0:16, :], ps[0:16, 0, 0:T], ACT.Sqrt, bias=rms[0:16, 1:2],
                                      scale=rms[0:16, 0:1]).then_inc(scalar_done, scalar.step("sd1"))
                for p_ in range(4):
                    n = 22 + (6 * p_ + 5) // 8
                    act_split(act, u0 + n + 2)
                    act.wait_ge(s_prod, nth(u0 + n))
                    b = pair_bank[p_]
                    A.activation(qT[0:96, 2 * p_:2 * p_ + 2, :], pair(b, 96), ACT.Copy)
                    A.activation(sq[0:96, 2 * p_:2 * p_ + 2, :], pair(b, 96), ACT.Square).then_inc(scalar_done, scalar.step(f"q{p_}"))
                act_split(act, u0 + 27)
                act.wait_ge(s_prod, nth(u0 + 25))
                for hd in range(8):
                    r = slice(64 * (hd % 2), 64 * (hd % 2) + 64)
                    last = A.activation(kT[0:64, hd, :], ps[r, 2 + hd // 2, 0:T], ACT.Copy)
                last.then_inc(scalar_done, scalar.step("k"))
                act_split(act, u0 + 28)
                act.wait_ge(s_prod, nth(u0 + 26))
                for tb in range(NB):
                    A.activation(vm[:, tb, :], ps[:, 6 + tb, :], ACT.Copy)
                act_split(act, u0 + 29)
                act.wait_ge(vector_done, vector.after("kn"))
                act.wait_ge(scalar_done, scalar.after("k"))
                A.activation(sq[0:96, 8:16, :], kT[0:96, :, :], ACT.Square).then_inc(scalar_done, scalar.step("sq2"))
                act.wait_ge(tensor_done, tensor.after("n2"))
                A.activation(rr[0:16, :], ps[0:16, 0, 0:T], ACT.Sqrt, bias=rms[0:16, 3:4],
                                      scale=rms[0:16, 2:3]).then_inc(scalar_done, scalar.step("sd2"))
                att_act(act, att, tensor, scalar, vector)
                A.activation(tiny[0:4, 0, :], misc[0:4, :], ACT.Abs, bias=G("dt_bias", 0, 4)).then_inc(scalar_done, scalar.step("gabs"))
                act.wait_ge(scalar_done, scalar.after("gabs"))
                A.activation(tiny[0:4, 3, 0:1], G("a_log", 0, 4), ACT.Exp)
                A.activation(tiny[0:4, 0, :], tiny[0:4, 0, :], ACT.Exp, scale=-1.0).then_inc(scalar_done, scalar.step("gexp"))
                act.wait_ge(scalar_done, scalar.after("gexp"))
                A.activation(tiny[0:4, 1, :], tiny[0:4, 0, :], ACT.Ln, bias=1.0).then_inc(scalar_done, scalar.step("gln"))
                A.activation(rr[32:36, :], misc[32:36, :], ACT.Sigmoid).then_inc(scalar_done, scalar.step("beta"))
                act.wait_ge(tensor_done, tensor.after("gb"))
                for g in range(2):
                    last = A.activation(egB[:, 2 * g:2 * g + 2, :], pair(4 + g), ACT.Exp)
                last.then_inc(scalar_done, scalar.step("eg"))
                for c in range(NB):
                    act.wait_ge(vector_done, vector.after(f"dd{c}"))
                    A.activation(Dm[:, c, :, :], Dm[:, c, :, :], ACT.Exp).then_inc(scalar_done, scalar.step(f"dm{c}"))
                A.activation(dl, dl, ACT.Exp).then_inc(scalar_done, scalar.step("edl"))
                act.wait_ge(scalar_done, scalar.after("edl"))
                for c in range(NB):
                    act.wait_ge(tensor_done, tensor.after(f"tr{2 * c}"))
                    for g in range(4):
                        last = A.activation(ktok[:, c, g, :], ps[:, 4 + 2 * c, g * P:g * P + P], ACT.Copy,
                                            scale=dl[:, c, g:g + 1])
                    last.then_inc(scalar_done, scalar.step(f"ktr{c}"))
                act.wait_ge(vector_done, vector.after("o1"))
                A.activation(sq[:, 0:4, :], og, ACT.Square).then_inc(scalar_done, scalar.step("sq3"))
                act.wait_ge(tensor_done, tensor.after("n3"))
                A.activation(rr[0:4, :], ps[0:4, 2, 0:T], ACT.Sqrt, bias=rms[0:4, 5:6],
                                      scale=rms[0:4, 4:5]).then_inc(scalar_done, scalar.step("sd3"))
                out_act(act, u0 + 27)

            tiny = sq[:, 12:16, :]

            def dve_prog(dve):
                for n in range(12):
                    dve_split(dve, u0 + 8 + n)
                    dve.wait_ge(s_prod, nth(u0 + 6 + n))
                    src, dst = ps[:, 5 + (n + 1) % 3, 0:T], qkv[:, n, :]
                    V.tensor_scalar(dst, src, G("gconv", 36 + n), None, MUL).then_inc(s_vc, vc.step())
                    V.wait_ge(s_vc, vc.n)
                    for d in (1, 2, 3):
                        last = V.scalar_tensor_tensor(dst[:, d:T], src[:, 0:T - d], G("gconv", 12 * (3 - d) + n),
                                                      dst[:, d:T], MUL, ADD)
                        if d < 3:
                            last.then_inc(s_vc, vc.step())
                            V.wait_ge(s_vc, vc.n)
                    last.then_inc(vector_done, vector.step(f"cv{n}"))
                dve_split(dve, u0 + 24)
                dve.wait_ge(scalar_done, scalar.after("sd1"))
                V.reciprocal(rr[0:16, :], rr[0:16, :]).then_inc(vector_done, vector.step("r1"))
                dve.wait_ge(tensor_done, tensor.after("bc1"))
                for n in range(5):
                    last = V.scalar_tensor_tensor(low[:, n, :], low[:, n, :],
                                                  G("q_a", n) if n < 3 else G("kv_a", n - 3),
                                                  ps[:, 1, (n // 3) * T:(n // 3) * T + T], MUL, MUL)
                last.then_inc(s_vc, vc.step())
                V.wait_ge(s_vc, vc.n)
                cut(h_hi[:, 0:5, :], h_lo[:, 0:5, :], low).then_inc(vector_done, vector.step("lown"))
                for n in range(4):
                    last = V.tensor_tensor(qkv[:, 2 * n:2 * n + 2, :], qkv[:, 2 * n:2 * n + 2, :], pair(2 + n), MUL)
                last.then_inc(vector_done, vector.step("l2"))
                dve_split(dve, u0 + 29)
                dve.wait_ge(scalar_done, scalar.after("misc"))
                V.tensor_copy(kT[64:96, :, :], over(misc[64:96, :], 8)).then_inc(vector_done, vector.step("kn"))
                dve.wait_ge(scalar_done, scalar.after("sd2"))
                V.reciprocal(rr[0:16, :], rr[0:16, :]).then_inc(vector_done, vector.step("r2"))
                for p_ in range(8):
                    buf = (qT if p_ < 4 else kT)[0:96, p_ % 4 * 2:p_ % 4 * 2 + 2, :]
                    dve.wait_ge(tensor_done, tensor.after(f"b2_{p_}"))
                    V.scalar_tensor_tensor(buf, buf, G("mla_q" if p_ < 4 else "mla_k", 0, 96),
                                                    pair(1 + p_ % 2, 96), MUL, MUL).then_inc(vector_done, vector.step(f"nm{p_}"))
                    dve.wait_ge(tensor_done, tensor.after(f"rot{p_}"))
                    V.tensor_tensor(tmp[0:96, :, :], pair(3 + p_ % 2, 96), over(C("sin")[0:96, :], 2), MUL)
                    V.tensor_tensor(buf, buf, over(C("cos")[0:96, :], 2), MUL).then_inc(s_vc, vc.step())
                    V.wait_ge(s_vc, vc.n)
                    V.tensor_tensor(buf, buf, tmp[0:96, :, :], ADD).then_inc(vector_done, vector.step(f"rope{p_}"))
                att_dve(dve, att, tensor, scalar, vector)
                dve.wait_ge(scalar_done, scalar.after("gln"))
                V.tensor_scalar(tiny[0:4, 2, :], misc[0:4, :], G("dt_bias", 0, 4), 0.0, ADD, MAXOP).then_inc(s_vc, vc.step())
                V.wait_ge(s_vc, vc.n)
                V.tensor_tensor(tiny[0:4, 2, :], tiny[0:4, 2, :], tiny[0:4, 1, :], ADD).then_inc(s_vc, vc.step())
                V.wait_ge(s_vc, vc.n)
                V.tensor_scalar(tiny[0:4, 2, :], tiny[0:4, 2, :], tiny[0:4, 3, 0:1], -1.0, MUL, MUL).then_inc(vector_done, vector.step("g"))
                dve.wait_ge(vector_done, vector.after("g"))
                for c in range(NB):
                    last = V.tensor_tensor_scan(rr[0:4, blk(c)], ones[0:4, :], tiny[0:4, 2, blk(c)], 0.0, MUL, ADD)
                last.then_inc(vector_done, vector.step("gc"))
                dve.wait_ge(tensor_done, tensor.after("gb"))
                dve.wait_ge(scalar_done, scalar.after("eg"))
                for g in range(2):
                    V.tensor_copy(gcB[:, 2 * g:2 * g + 2, :], pair(4 + g))
                    last = V.tensor_copy(beB[:, 2 * g:2 * g + 2, :], pair(6 + g))
                last.then_inc(vector_done, vector.step("kk"))
                dve.wait_ge(tensor_done, tensor.after("gcol"))
                V.tensor_copy(gcol.rearrange("p a b -> p (a b)"), ps[:, 0, 0:8])
                V.tensor_copy(bcol.rearrange("p a b -> p (a b)"), ps[:, 1, 0:8]).then_inc(vector_done, vector.step("gcols"))
                dve.wait_ge(vector_done, vector.after("gcols"))
                for c in range(NB):
                    for g in range(4):
                        last = V.tensor_scalar(Dm[:, c, g, :], gcB[:, g, blk(c)], gcol[:, c, g:g + 1], 0.0, SUB, MINOP)
                    V.tensor_tensor(dl[:, c, :], gcB[:, :, c * P + P - 1], gcol[:, c, :], SUB).then_inc(vector_done, vector.step(f"dd{c}"))
                V.tensor_tensor(kbg, qkv[:, 4:8, :], beB, MUL).then_inc(s_vc, vc.step())
                V.wait_ge(s_vc, vc.n)
                V.tensor_tensor(kbg, kbg, egB, MUL).then_inc(s_vc, vc.step())
                V.wait_ge(s_vc, vc.n)
                V.scalar_tensor_tensor(qg.rearrange("p a b -> p (a b)"), qkv[:, 0:4, :].rearrange("p a b -> p (a b)"), GD ** -0.5,
                                       egB.rearrange("p a b -> p (a b)"), MUL, MUL)
                for c in range(NB):
                    dve.wait_ge(tensor_done, tensor.after(f"kk{c}"))
                    dve.wait_ge(scalar_done, scalar.after(f"dm{c}"))
                    fl = lambda ap: ap[:, c, :, :].rearrange("p a b -> p (a b)")
                    V.tensor_tensor(fl(AT), ps[:, c, :], fl(Dm), MUL)
                    V.scalar_tensor_tensor(fl(QK), ps[:, 2 + c, :], GD ** -0.5, fl(Dm), MUL, MUL).then_inc(s_vc, vc.step())
                    V.wait_ge(s_vc, vc.n)
                    V.tensor_tensor(AT[:, c, :, :], AT[:, c, :, :], beB[:, :, blk(c)], MUL)
                    last = V.tensor_tensor(QK[:, c, :, :], QK[:, c, :, :], over(C("incl"), 4), MUL)
                last.then_inc(vector_done, vector.step("aqk"))
                for c in range(NB):
                    dve.wait_ge(tensor_done, tensor.after(f"tr{2 * c + 1}"))
                    for g in range(4):
                        last = V.tensor_scalar(vtok[:, c, g, :], ps[:, 5 + 2 * c, g * P:g * P + P],
                                               bcol[:, c, g:g + 1], None, MUL)
                last.then_inc(vector_done, vector.step("vb"))
                dve.wait_ge(vector_done, vector.after("vb"))
                for c in range(NB):
                    V.tensor_copy(Ti[:, c, :, :], over(ident, 4))
                    V.tensor_copy(TT[:, c, :, :], over(ident, 4))
                    last = V.tensor_tensor(X[:, c, :, :], AT[:, c, :, :], over(levels[:, 0, :], 4), MUL)
                last.then_inc(vector_done, vector.step("x0"))
                for l in range(LV):
                    for c in range(NB):
                        dve.wait_ge(tensor_done, tensor.after(f"y{l}_{c}"))
                        V.tensor_copy(Y[:, c, :, :], ps[:, c, :].rearrange("p (a b) -> p a b", a=4)).then_inc(vector_done, vector.step(f"yc{l}_{c}"))
                        if l + 1 < LV:
                            V.tensor_tensor(X[:, c, :, :], AT[:, c, :, :], over(levels[:, l + 1, :], 4), MUL)
                    for c in range(NB):
                        dve.wait_ge(tensor_done, tensor.after(f"inv{l}_{c}"))
                        fl = lambda ap: ap[:, c, :, :].rearrange("p a b -> p (a b)")
                        V.tensor_tensor(fl(Ti), fl(Ti), ps[:, 2 + c, :], SUB)
                        V.tensor_tensor(fl(TT), fl(TT), ps[:, 4 + c, :], SUB).then_inc(vector_done, vector.step(f"tc{l}_{c}"))
                flat = lambda ap: ap.rearrange("p a b -> p (a b)")
                V.tensor_copy(rhs, vtok[:, 0, :, :]).then_inc(vector_done, vector.step("r0"))
                dve.wait_ge(tensor_done, tensor.after("vn0"))
                V.tensor_copy(flat(vn), ps[:, 7, :]).then_inc(vector_done, vector.step("v0"))
                dve.wait_ge(tensor_done, tensor.after("og0"))
                V.tensor_copy(og[:, :, 0:P], ps[:, 0, :].rearrange("p (a b) -> p a b", a=4)).then_inc(vector_done, vector.step("o0"))
                dve.wait_ge(tensor_done, tensor.after("st0"))
                V.tensor_copy(flat(St), ps[:, 5, :]).then_inc(vector_done, vector.step("s0"))
                dve.wait_ge(tensor_done, tensor.after("ks1"))
                V.tensor_tensor(flat(rhs), vtok[:, 1, :, :].rearrange("p a b -> p (a b)"), ps[:, 6, :], SUB).then_inc(vector_done, vector.step("r1b"))
                dve.wait_ge(tensor_done, tensor.after("vn1"))
                V.tensor_copy(flat(vn), ps[:, 7, :]).then_inc(vector_done, vector.step("v1"))
                dve.wait_ge(tensor_done, tensor.after("og1"))
                V.tensor_copy(og[:, :, P:T], ps[:, 1, :].rearrange("p (a b) -> p a b", a=4)).then_inc(vector_done, vector.step("o1"))
                dve.wait_ge(scalar_done, scalar.after("sd3"))
                V.reciprocal(rr[0:4, :], rr[0:4, :]).then_inc(vector_done, vector.step("r3"))
                V.tensor_tensor(zs, zs, og, MUL).then_inc(s_vc, vc.step())
                V.wait_ge(s_vc, vc.n)
                dve.wait_ge(tensor_done, tensor.after("bc3"))
                for g in range(2):
                    last = V.scalar_tensor_tensor(og[:, 2 * g:2 * g + 2, :], zs[:, 2 * g:2 * g + 2, :],
                                                  G("out_norm"), pair(3 + g), MUL, MUL)
                last.then_inc(s_vc, vc.step())
                V.wait_ge(s_vc, vc.n)
                cut(h_hi[:, 4:8, :], h_lo[:, 4:8, :], og).then_inc(vector_done, vector.step("ob"))
                out_dve(dve, "even", u0 + 27)
            return pe_prog, act_prog, dve_prog

        def odd_mixer():
            u0 = unit_base["odd"]
            cv = Carve()
            qk = cv(11, T)
            qi = cv(4, T)
            sq = cv(11, T)
            rr = cv(T)
            vt = cv(NB, 264)
            rl = cv(4, T)
            sc = cv(NB, T)
            wk = cv(NB, T)
            m8 = cv(8)
            S, PT = cv(8, T), cv(16, P)
            mx, sm = cv(8), cv(8)
            ape, aact, advn = att_steps()
            every = [(qb, hd) for qb in range(NB) for hd in range(IDX_H)]
            tensor_done, scalar_done, vector_done = sems_of("odd")
            tensor = Steps(tensor_done, ["n1", "bc1"] + [f"ix{i}" for i in range(16)] + ape)
            scalar = Steps(scalar_done, [f"in{n}" for n in range(15)] + ["sd1"] + [f"rl{i}" for i in range(16)] + aact)
            vector = Steps(vector_done, ["vt", "r1", "nq"] + [f"sc{i}" for i in range(16)] + ["mask"] + advn)
            causal, rms = C("causal"), C("rms")

            def keys(qb):
                return causal[:, P - qb * P:2 * P]

            def evac(qb):
                for b in range(2):
                    last = V.tensor_copy(h_hi[:, 4 * b:4 * b + 4, qb * P:qb * P + P],
                                         ps[:, b, :].rearrange("p (a b) -> p a b", a=4))
                last.then_inc(s_vc, vc.step())
                V.wait_ge(s_vc, vc.n)
                for b in range(2):
                    last = V.tensor_tensor(h_lo[:, 4 * b:4 * b + 4, qb * P:qb * P + P],
                                           ps[:, b, :].rearrange("p (a b) -> p a b", a=4),
                                           f(h_hi[:, 4 * b:4 * b + 4, qb * P:qb * P + P]), SUB)
                return last
            att = Att(S, PT, mx, sm,
                      lambda hd, qb: qk[:, hd, qb * P:qb * P + P], lambda hd, nk: qk[:, 8 + hd // 4, 0:nk],
                      lambda hd, kb: vt[:, kb, hd // 4 * P:hd // 4 * P + P],
                      lambda hd: ps[:, hd // 4, hd % 4 * P:hd % 4 * P + P], evac, P ** -0.5,
                      lambda qb: wk[:, qb, 0:(qb + 1) * P])

            def pe_prog(pe):
                for n in range(15):
                    if n >= 3:
                        pe.wait_ge(scalar_done, scalar.after(f"in{n - 3}"))
                    linear(pe, u0 + n, ps[:, 4 + n % 3, 0:T], norm=None if n else order["odd"])
                for g, ks in enumerate(((0, 1, 2), (3, 4, 5), (6, 7))):
                    u = u0 + 15 + g
                    pe.wait_ge(s_lo, nth(u))
                    for j, k in enumerate(ks):
                        for tb in range(NB):
                            tk, c_ = slice(tb * P, tb * P + P), slice(j * 264, j * 264 + 264)
                            last = mm3(ps[:, tb, 0:264], h_hi[:, k, tk], h_lo[:, k, tk],
                                       w_hi[:, u % RING, c_], w_lo[:, u % RING, c_], k == 0, k == 7)
                    last.then_inc(s_prod, 1)
                pe.wait_ge(scalar_done, scalar.after("in10"))
                for n in range(11):
                    rows = P if n < 10 else IDX_D
                    last = mm(ps[0:16, 2, 0:T], C("onehot")[0:rows, 15 - n:31 - n], sq[0:rows, n, :], n == 0, n == 10)
                last.then_inc(tensor_done, tensor.step("n1"))
                pe.wait_ge(vector_done, vector.after("r1"))
                pe.wait_ge(scalar_done, scalar.after("in14"))
                for r in range(11):
                    last = mm(ps[:, 2 + r // 2, r % 2 * T:r % 2 * T + T], sel(r), rr[0:16, :])
                last.then_inc(tensor_done, tensor.step("bc1"))
                pe.wait_ge(vector_done, vector.after("nq"))
                for i, (qb, hd) in enumerate(every):
                    r = slice(64 * (hd % 2), 64 * (hd % 2) + 64)
                    if i >= 4:
                        pe.wait_ge(scalar_done, scalar.after(f"rl{i - 4}"))
                    mm(ps[:, i % 4, 0:(qb + 1) * P], qi[r, hd // 2, qb * P:qb * P + P],
                                qk[r, 10, 0:(qb + 1) * P]).then_inc(tensor_done, tensor.step(f"ix{i}"))
                pe.wait_ge(scalar_done, scalar.after("rl15"))
                att_pe(pe, att, tensor, scalar, vector)
                pe.wait_ge(vector_done, vector.after("out1"))
                out_pe(pe, "odd", u0 + 18)

            def act_prog(act):
                for n in range(15):
                    act_split(act, u0 + n + 2)
                    act.wait_ge(s_prod, nth(u0 + n))
                    src = ps[:, 4 + n % 3, 0:T]
                    if n < 11:
                        A.activation(qk[:, n, :], src, ACT.Copy)
                        A.activation(sq[:, n, :], src, ACT.Square).then_inc(scalar_done, scalar.step(f"in{n}"))
                    else:
                        A.activation(qi[:, n - 11, :], src, ACT.Copy).then_inc(scalar_done, scalar.step(f"in{n}"))
                act_split(act, u0 + 20)
                act.wait_ge(tensor_done, tensor.after("n1"))
                A.activation(rr[0:16, :], ps[0:16, 2, 0:T], ACT.Sqrt, bias=rms[0:16, 5:6],
                                      scale=rms[0:16, 4:5]).then_inc(scalar_done, scalar.step("sd1"))
                for i, (qb, hd) in enumerate(every):
                    act.wait_ge(tensor_done, tensor.after(f"ix{i}"))
                    if i >= 4:
                        act.wait_ge(vector_done, vector.after(f"sc{i - 4}"))
                    A.activation(rl[:, i % 4, 0:(qb + 1) * P], ps[:, i % 4, 0:(qb + 1) * P], ACT.Relu).then_inc(scalar_done, scalar.step(f"rl{i}"))
                att_act(act, att, tensor, scalar, vector)
                out_act(act, u0 + 18)

            def dve_prog(dve):
                dve_split(dve, u0 + 20)
                dve.wait_ge(s_prod, nth(u0 + 17))
                for tb in range(NB):
                    last = V.tensor_copy(vt[:, tb, :], ps[:, tb, 0:264])
                last.then_inc(vector_done, vector.step("vt"))
                dve.wait_ge(scalar_done, scalar.after("sd1"))
                V.reciprocal(rr[0:16, :], rr[0:16, :]).then_inc(vector_done, vector.step("r1"))
                dve.wait_ge(tensor_done, tensor.after("bc1"))
                for g in range(5):
                    V.scalar_tensor_tensor(qk[:, 2 * g:2 * g + 2, :], qk[:, 2 * g:2 * g + 2, :],
                                           G("dsa_q" if g < 4 else "dsa_k"),
                                           ps[:, 2 + g, :].rearrange("p (a b) -> p a b", a=2), MUL, MUL)
                V.scalar_tensor_tensor(qk[:, 10, :], qk[:, 10, :], G("kidx"), ps[:, 7, 0:T], MUL, MUL).then_inc(vector_done, vector.step("nq"))
                dve.wait_ge(vector_done, vector.after("vt"))
                for i, (qb, hd) in enumerate(every):
                    n = (qb + 1) * P
                    dve.wait_ge(scalar_done, scalar.after(f"rl{i}"))
                    if hd:
                        dve.wait_ge(vector_done, vector.after(f"sc{i - 1}"))
                    V.scalar_tensor_tensor(sc[:, qb, 0:n], rl[:, i % 4, 0:n], vt[:, qb, 256 + hd:257 + hd],
                                                    sc[:, qb, 0:n] if hd else keys(qb), MUL, ADD).then_inc(vector_done, vector.step(f"sc{i}"))
                dve.wait_ge(vector_done, vector.after("sc15"))
                for qb in range(NB):
                    n = (qb + 1) * P
                    w = wk[:, qb, 0:n]
                    for j in range(TOPK // 8):
                        src = sc[:, qb, 0:n] if j == 0 else w
                        V.max(m8, src).then_inc(s_vc, vc.step())
                        V.wait_ge(s_vc, vc.n)
                        V.match_replace(w, m8, src, TAKEN).then_inc(s_vc, vc.step())
                        V.wait_ge(s_vc, vc.n)
                    V.tensor_scalar(w, w, 0.5 * TAKEN, -NEG, ALU.is_le, MUL).then_inc(s_vc, vc.step())
                    V.wait_ge(s_vc, vc.n)
                    last = V.scalar_tensor_tensor(w, w, NEG, keys(qb), ADD, ADD)
                last.then_inc(vector_done, vector.step("mask"))
                dve.wait_ge(vector_done, vector.after("mask"))
                att_dve(dve, att, tensor, scalar, vector)
                out_dve(dve, "odd", u0 + 18)
            return pe_prog, act_prog, dve_prog

        def second_mixer():
            u0 = unit_base["second"]
            cv = Carve()
            AR = cv(KT, 2, T)
            BT, KP, VT = cv(KT, T), cv(KT, T), cv(KT, T)
            GC = cv(KT, T)
            EC = cv(KT, T // RC)
            S2 = cv(KT, P)
            lx = cv(2, T)
            col = cv(11, 8)
            omm = cv(26)
            mark = cv.at
            bufs = [[cv(T) for _ in range(30)] for _ in range(2)]
            M = cv(KT, T)
            cv.at = mark
            tok = cv(3, KT * P)
            AB, AK = cv(RH, 2, P), cv(RH, 2, P)
            Ti, TT, Y = cv(RH, P), cv(RH, P), cv(RH, P)
            X = x.rearrange("p a b -> p (a b)").rearrange("p (a b) -> p a b", b=P)
            RHS, SA = Ti.rearrange("p a b -> p (a b)")[:, 0:1024], Ti.rearrange("p a b -> p (a b)")[:, 1024:2048]
            rr = lx[:, 0, :]
            LV = 6
            lv_groups = [(l, g) for l in range(LV) for g in range(4)]

            def lv_order(l):
                return [("Y", 0), ("Y", 1), ("U", 0), ("Y", 2), ("U", 1), ("Y", 3), ("U", 2), ("U", 3)]

            tensor_done, scalar_done, vector_done = sems_of("second")
            stored = nc.dram_tensor("stored", (2, P, KT, T), f32).ap()
            s_x_out, s_x_in, s_m_out, s_m_in = sem("x_stored"), sem("x_back"), sem("m_stored"), sem("m_back")
            pe_names, act_names, dve_names = [], ["spa", "spe", "spl", "lora"], ["omm", "sp1", "sp", "lx", "lxc"]
            for t in range(KT):
                pe_names += [f"{t}_lru", f"{t}_kk", f"{t}_bonus"]
                act_names += [f"{t}_{n}" for n in ("ca", "ga", "gb", "gtb", "lg", "wd", "ea", "dec", "gc", "mult", "nk")]
                dve_names += [f"{t}_{n}" for n in ("xa", "ba", "u", "t1", "cum", "r", "k", "v", "k2", "bp", "bo")]
            for b in range(NB):
                pe_names += [f"tok{b}_{j}" for j in range(3)] + [f"A{b}_{g}" for g in range(4)]
                pe_names += [f"{k}{b}_{0}_{g}" for g in range(4) for k in "Y"]
                pe_names += [f"{k}{b}_{l}_{g}" for l in range(1, LV) for k, g in lv_order(l)]
                act_names += [f"tk{b}_{j}" for j in range(3)]
                act_names += [f"yc{b}_{l}_{g}" for l in range(1, LV) for g in range(4)]
                dve_names += [f"am{b}_{g}" for g in range(4)] + [f"x{b}"]
                dve_names += [f"tc{b}_{l}_{g}" for l in range(LV) for g in range(4)] + [f"z{b}"]
                for c in (2 * b, 2 * b + 1):
                    pe_names += [f"rhs{c}", f"sa{c}", f"y{c}"] + ([f"st{c}"] if c < 3 else [])
                    act_names += [f"sac{c}"]
                    dve_names += [f"rh{c}", f"yo{c}"] + ([f"s{c}"] if c < 3 else [])
            pe_names += ["mean", "var", "bc"]
            act_names += ["sqy", "sd"]
            dve_names += ["cen", "rs", "m"]
            tensor = Steps(tensor_done, pe_names)
            scalar = Steps(scalar_done, act_names)
            vector = Steps(vector_done, dve_names)
            small = 7

            def nth_unit(t, n):
                return u0 + 2 + 12 * t + n

            def unit(t, i):
                return u0 + 2 + 12 * t + (i if i < 7 else i - 4)

            reader = {0: ("a", "ca"), 1: ("v", "xa"), 2: ("v", "ba"), 3: ("a", "ga"), 4: ("v", "u"), 5: ("a", "gb"),
                      6: ("a", "gtb"), 7: ("a", "lg"), 8: ("a", "lg"), 9: ("a", "wd"), 10: ("a", "wd"),
                      11: ("a", "wd"), 12: ("v", "r"), 13: ("v", "k"), 14: ("v", "v"), 15: ("a", "gc"),
                      16: ("a", "nk"), 17: ("v", "bo")}

            def bank(i):
                return ps[:, i % 6, 0:T]

            def bank_free(pe, t, i):
                tt_, j = (t, i - 6) if i >= 6 else (t - 1, i + 12)
                if tt_ >= 0:
                    e, name = reader[j]
                    by = scalar if e == "a" else vector
                    pe.wait_ge(by.sem, by.after(f"{tt_}_{name}"))

            def toks(c):
                return slice(RC * c, RC * c + RC)

            def pe_prog(pe):
                for n in range(2):
                    linear(pe, u0 + n, bank(n), norm=None if n else order["second"])
                pe.wait_ge(vector_done, vector.after("lx"))
                pe.wait_ge(vector_done, vector.after("lxc"))
                for t in range(KT):
                    for i in range(7):
                        bank_free(pe, t, i)
                        linear(pe, unit(t, i), bank(i))
                    u = u0 + 2 + 12 * t + small
                    pe.wait_ge(s_lo, nth(u))
                    pe.wait_ge(vector_done, vector.after(f"{t}_u"))
                    for i in (7, 8):
                        bank_free(pe, t, i)
                        last = wmm(bank(i), u, i - 7, a_hi[:, 0, :], a_lo[:, 0, :])
                    last.then_inc(tensor_done, tensor.step(f"{t}_lru"))
                    for i in (9, 10, 11):
                        bank_free(pe, t, i)
                        last = wmm(bank(i), u, i - 7, a_hi[:, (1, 1, 2)[i - 9], :], a_lo[:, (1, 1, 2)[i - 9], :])
                    last.then_inc(s_prod, 1)
                    for i in range(12, 16):
                        bank_free(pe, t, i)
                        linear(pe, unit(t, i), bank(i))
                    bank_free(pe, t, 16)
                    pe.wait_ge(vector_done, vector.after(f"{t}_k2"))
                    mm(bank(16), pairs, dv(t, "k2")).then_inc(tensor_done, tensor.step(f"{t}_kk"))
                    bank_free(pe, t, 17)
                    pe.wait_ge(vector_done, vector.after(f"{t}_bp"))
                    mm(bank(17), pairs, dv(t, "bp")).then_inc(tensor_done, tensor.step(f"{t}_bonus"))
                for b in range(NB):
                    bs = slice(b * P, b * P + P)
                    if b == 0:
                        pe.wait_ge(vector_done, vector.after("7_bo"))
                    else:
                        pe.wait_ge(vector_done, vector.after("s1"))
                    for j, src in enumerate((BT, KP, VT)):
                        for t in range(KT):
                            last = TE.transpose(ps[:, 2 * j + t // 4, t % 4 * P:t % 4 * P + P], src[:, t, bs], ident)
                        last.then_inc(tensor_done, tensor.step(f"tok{b}_{j}"))
                    for g in range(4):
                        o = 4 * (g % 2)
                        if g < 2:
                            pe.wait_ge(scalar_done, scalar.after(f"tk{b}_2"))
                        if g >= 2:
                            pe.wait_ge(vector_done, vector.after(f"am{b}_{g - 2}"))
                        for t in (2 * g, 2 * g + 1):
                            for hf in range(2):
                                r = slice(64 * hf, 64 * hf + 64)
                                for q, src in ((0, BT), (2, KP)):
                                    last = mm(ps[:, o + q + hf, (t % 2) * T:(t % 2) * T + T]
                                              .rearrange("p (a b) -> p a b", a=2), src[r, t, bs], AR[r, t, :, bs])
                        last.then_inc(tensor_done, tensor.step(f"A{b}_{g}"))
                    pe.wait_ge(vector_done, vector.after(f"x{b}"))
                    for g in range(4):
                        if g >= 2:
                            pe.wait_ge(vector_done, vector.after(f"tc{b}_0_{g - 2}"))
                        for n in range(4):
                            last = TE.transpose(ps[:, g % 2, n * P:n * P + P], X[:, 4 * g + n, :], ident)
                        last.then_inc(tensor_done, tensor.step(f"Y{b}_0_{g}"))
                    for l in range(1, LV):
                        for k, g in lv_order(l):
                            if k == "Y":
                                pe.wait_ge(vector_done, vector.after(f"tc{b}_{l - 1}_{g}"))
                                if g >= 2:
                                    pe.wait_ge(scalar_done, scalar.after(f"yc{b}_{l}_{g - 2}"))
                                elif l >= 2:
                                    pe.wait_ge(scalar_done, scalar.after(f"yc{b}_{l - 1}_{g + 2}"))
                                if l == 1 and g == 0:
                                    pe.wait_ge(vector_done, vector.after(f"tc{b}_0_3"))
                                for n in range(4 * g, 4 * g + 4):
                                    last = mm(ps[:, g % 2, n % 4 * P:n % 4 * P + P], X[:, n, :], Ti[:, n, :])
                            else:
                                pe.wait_ge(scalar_done, scalar.after(f"yc{b}_{l}_{g}"))
                                if g >= 2:
                                    pe.wait_ge(vector_done, vector.after(f"tc{b}_{l}_{g - 2}"))
                                elif l >= 2:
                                    pe.wait_ge(vector_done, vector.after(f"tc{b}_{l - 1}_{g + 2}"))
                                for n in range(4 * g, 4 * g + 4):
                                    c_ = slice(n % 4 * P, n % 4 * P + P)
                                    if l < LV - 1:
                                        mm(ps[:, 2 + g % 2, c_], TT[:, n, :], Y[:, n, :])
                                    last = mm(ps[:, 4 + g % 2, c_], Y[:, n, :], TT[:, n, :])
                            last.then_inc(tensor_done, tensor.step(f"{k}{b}_{l}_{g}"))
                    pe.wait_ge(vector_done, vector.after(f"z{b}"))
                    for c in (2 * b, 2 * b + 1):
                        o_ = 64 * (c % 2)
                        r, cs = slice(o_, o_ + 64), slice(o_, o_ + 64)
                        v2 = tok[:, 2, :]
                        if c:
                            pe.wait_ge(vector_done, vector.after(f"s{c - 1}"))
                        for t in range(KT):
                            bk, at = t // 4, t % 4 * P
                            if c:
                                mm(ps[r, bk, at:at + P], AR[:, t, 0, toks(c)], S2[:, t, :], True, False)
                            for n in (2 * t, 2 * t + 1):
                                at = n % 8 * 64
                                last = mm(ps[r, bk, at:at + 64], AK[:, n, 0, cs], v2[:, n * 64:n * 64 + 64], c == 0, True)
                        last.then_inc(tensor_done, tensor.step(f"rhs{c}"))
                        pe.wait_ge(vector_done, vector.after(f"rh{c}"))
                        for n in range(RH):
                            last = mm(ps[r, 2 + n // 8, n % 8 * 64:n % 8 * 64 + 64], TT[:, n, cs], RHS[:, n * 64:n * 64 + 64])
                        last.then_inc(tensor_done, tensor.step(f"sa{c}"))
                        pe.wait_ge(scalar_done, scalar.after(f"sac{c}"))
                        for t in range(KT):
                            if c:
                                mm(ps[:, 4, t * 64:t * 64 + 64], S2[:, t, :], AR[:, t, 1, toks(c)], True, False)
                            for n in (2 * t, 2 * t + 1):
                                o = ps[64 * (n % 2):64 * (n % 2) + 64, 4, t * 64:t * 64 + 64]
                                mm(o, SA[:, n * 64:n * 64 + 64], AB[:, n, 1, cs], c == 0, False)
                                last = mm(o, v2[:, n * 64:n * 64 + 64], AK[:, n, 1, cs], False, True)
                        last.then_inc(tensor_done, tensor.step(f"y{c}"))
                        if c < 3:
                            for t in range(KT):
                                o = ps[:, 5 + t // 4, t % 4 * P:t % 4 * P + P]
                                w = slice(t * P, t * P + P)
                                mm(o, tok[r, 0, w], SA[r, w], True, False)
                                last = mm(o, tok[r, 1, w], tok[r, 2, w], False, True)
                            last.then_inc(tensor_done, tensor.step(f"st{c}"))
                pe.wait_ge(vector_done, vector.after("yo3"))
                for t in range(KT):
                    last = mm(ps[:, t // 2, t % 2 * T:t % 2 * T + T], pairs, VT[:, t, :])
                last.then_inc(tensor_done, tensor.step("mean"))
                pe.wait_ge(scalar_done, scalar.after("sqy"))
                for t in range(KT):
                    last = mm(ps[0:16, 4, 0:T], C("onehot2")[:, 14 - 2 * t:30 - 2 * t], BT[:, t, :], t == 0, t == KT - 1)
                last.then_inc(tensor_done, tensor.step("var"))
                pe.wait_ge(vector_done, vector.after("rs"))
                for t in range(KT):
                    for hf in range(2):
                        last = mm(ps[64 * hf:64 * hf + 64, t // 2, t % 2 * T:t % 2 * T + T],
                                  sel(2 * t + hf, m=64), rr[0:16, :])
                last.then_inc(tensor_done, tensor.step("bc"))
                pe.wait_ge(vector_done, vector.after("m"))
                out_pe(pe, "second", u0 + 98)

            names = ("ca ga gb gtb sa si sw aa g2 ea th p1 p2 p3 mu nk gc "
                     "cx ya u t1 lw cum cl r k kr k2 bp tmp").split()

            def dv(t, name):
                return bufs[t % 2][names.index(name)]

            def act_prog(act):
                lo, _ = par_off["lru_a"]
                A.activation(col[:, 0, :], par[:, lo:lo + 8], ACT.Abs).then_inc(scalar_done, scalar.step("spa"))
                act.wait_ge(scalar_done, scalar.after("spa"))
                A.activation(col[:, 1, :], col[:, 0, :], ACT.Exp, scale=-1.0).then_inc(scalar_done, scalar.step("spe"))
                act.wait_ge(vector_done, vector.after("sp1"))
                A.activation(col[:, 3, :], col[:, 2, :], ACT.Ln).then_inc(scalar_done, scalar.step("spl"))
                act.wait_ge(vector_done, vector.after("lx"))
                act_split(act, nth_unit(0, 2))
                A.activation(lx[0:64, 0, :], lx[0:64, 0, :], ACT.Tanh)
                A.activation(lx[:, 1, :], lx[:, 1, :], ACT.Sigmoid).then_inc(scalar_done, scalar.step("lora"))
                for t in range(KT):
                    d = lambda n: dv(t, n)
                    st = lambda ins, n: ins.then_inc(scalar_done, scalar.step(f"{t}_{n}"))
                    if t >= 2:
                        act.wait_ge(vector_done, vector.after(f"{t - 2}_bo"))
                    act_split(act, nth_unit(t, 2))
                    act.wait_ge(s_prod, nth(unit(t, 0)))
                    st(A.activation(d("ca"), bank(0), ACT.Copy), "ca")
                    act_split(act, nth_unit(t, 5))
                    act.wait_ge(s_prod, nth(unit(t, 3)))
                    st(A.activation(d("ga"), bank(3), ACT.Sigmoid, bias=G("merge_b", t)), "ga")
                    act_split(act, nth_unit(t, 7))
                    act.wait_ge(s_prod, nth(unit(t, 5)))
                    st(A.activation(d("gb"), bank(5), ACT.Gelu_apprx_tanh), "gb")
                    act_split(act, nth_unit(t, 8))
                    act.wait_ge(s_prod, nth(unit(t, 6)))
                    st(A.activation(d("gtb"), bank(6), ACT.Sigmoid, bias=G("merge_b", 8 + t)), "gtb")
                    act_split(act, nth_unit(t, 9))
                    act.wait_ge(tensor_done, tensor.after(f"{t}_lru"))
                    A.activation(d("sa"), bank(7), ACT.Sigmoid, bias=G("lru_ba", t))
                    st(A.activation(d("si"), bank(8), ACT.Sigmoid, bias=G("lru_bi", t)), "lg")
                    act.wait_ge(s_prod, nth(nth_unit(t, small)))
                    A.activation(d("sw"), bank(9), ACT.Sigmoid, bias=G("w0", t))
                    A.activation(d("aa"), bank(10), ACT.Sigmoid, bias=G("a0", t))
                    st(A.activation(d("g2"), bank(11), ACT.Copy), "wd")
                    act_split(act, nth_unit(t, 10))
                    act.wait_ge(scalar_done, scalar.after(f"{t}_lg"))
                    if t == 0:
                        act.wait_ge(vector_done, vector.after("sp"))
                    A.activation(d("ea"), d("sa"), ACT.Exp, scale=col[:, 8, t:t + 1])
                    st(A.activation(d("th"), d("sa"), ACT.Tanh, scale=col[:, 9, t:t + 1]), "ea")
                    act.wait_ge(vector_done, vector.after(f"{t}_cum"))
                    A.activation(d("p1"), d("cum"), ACT.Exp)
                    A.activation(d("p2"), d("cum"), ACT.Exp, scale=-1.0)
                    st(A.activation(d("p3"), d("cl"), ACT.Exp), "dec")
                    act_split(act, nth_unit(t, 13))
                    act.wait_ge(s_prod, nth(unit(t, 15)))
                    st(A.activation(d("gc"), bank(15), ACT.Sigmoid, bias=G("merge_b", 16 + t)), "gc")
                    act_split(act, nth_unit(t, 14))
                    act.wait_ge(vector_done, vector.after(f"{t}_t1"))
                    st(A.activation(d("mu"), d("t1"), ACT.Sqrt), "mult")
                    act.wait_ge(tensor_done, tensor.after(f"{t}_kk"))
                    st(A.activation(d("nk"), bank(16), ACT.Sqrt), "nk")
                for b in range(NB):
                    for j in range(3):
                        act.wait_ge(tensor_done, tensor.after(f"tok{b}_{j}"))
                        if j == 0 and b == 0:
                            act.wait_ge(vector_done, vector.after("7_bo"))
                        for k in range(2):
                            last = A.activation(tok[:, j, k * 512:(k + 1) * 512], ps[:, 2 * j + k, :], ACT.Copy)
                        last.then_inc(scalar_done, scalar.step(f"tk{b}_{j}"))
                    for l in range(1, LV):
                        for g in range(4):
                            act.wait_ge(tensor_done, tensor.after(f"Y{b}_{l}_{g}"))
                            if b == 0 and l == 1 and g == 0:
                                act.wait_ge(s_m_out, 16)
                            A.activation(Y[:, 4 * g:4 * g + 4, :],
                                                  ps[:, g % 2, :].rearrange("p (a b) -> p a b", a=4), ACT.Copy).then_inc(scalar_done, scalar.step(f"yc{b}_{l}_{g}"))
                    for c in (2 * b, 2 * b + 1):
                        r = slice(64 * (c % 2), 64 * (c % 2) + 64)
                        act.wait_ge(tensor_done, tensor.after(f"sa{c}"))
                        for k in range(2):
                            last = A.activation(SA[r, 512 * k:512 * k + 512], ps[r, 2 + k, :], ACT.Copy)
                        last.then_inc(scalar_done, scalar.step(f"sac{c}"))
                act.wait_ge(vector_done, vector.after("cen"))
                A.activation(BT, VT, ACT.Square).then_inc(scalar_done, scalar.step("sqy"))
                act.wait_ge(tensor_done, tensor.after("var"))
                rms = C("rms")
                A.activation(rr[0:16, :], ps[0:16, 4, 0:T], ACT.Sqrt, bias=rms[0:16, 7:8],
                                      scale=rms[0:16, 6:7]).then_inc(scalar_done, scalar.step("sd"))
                out_act(act, u0 + 98)

            def shifted(dst, src, n, name=None):
                V.tensor_scalar(dst, src, omm[:, n:n + 1], None, MUL).then_inc(s_vc, vc.step())
                V.wait_ge(s_vc, vc.n)
                return V.scalar_tensor_tensor(dst[:, 1:T], src[:, 0:T - 1], G("mu", n), dst[:, 1:T], MUL, ADD)

            def dve_prog(dve):
                lo, n_ = par_off["mu"]
                V.tensor_scalar(omm, par[:, lo:lo + n_], -1.0, 1.0, MUL, ADD).then_inc(vector_done, vector.step("omm"))
                dve.wait_ge(scalar_done, scalar.after("spe"))
                e_, w_ = col[:, 1, :], col[:, 2, :]
                V.tensor_scalar(w_, e_, 1.0, None, ADD).then_inc(vector_done, vector.step("sp1"))
                dve.wait_ge(vector_done, vector.after("sp1"))
                V.tensor_scalar(col[:, 4, :], w_, -1.0, None, ADD).then_inc(s_vc, vc.step())
                V.wait_ge(s_vc, vc.n)
                V.tensor_scalar(col[:, 5, :], col[:, 4, :], 0.0, None, ALU.is_equal).then_inc(s_vc, vc.step())
                V.wait_ge(s_vc, vc.n)
                V.tensor_tensor(col[:, 4, :], col[:, 4, :], col[:, 5, :], ADD).then_inc(s_vc, vc.step())
                V.wait_ge(s_vc, vc.n)
                V.reciprocal(col[:, 4, :], col[:, 4, :]).then_inc(s_vc, vc.step())
                V.wait_ge(s_vc, vc.n)
                dve.wait_ge(scalar_done, scalar.after("spl"))
                V.tensor_tensor(col[:, 4, :], col[:, 4, :], col[:, 3, :], MUL).then_inc(s_vc, vc.step())
                V.wait_ge(s_vc, vc.n)
                V.tensor_tensor(col[:, 4, :], col[:, 4, :], col[:, 5, :], ADD).then_inc(s_vc, vc.step())
                V.wait_ge(s_vc, vc.n)
                V.tensor_tensor(col[:, 4, :], col[:, 4, :], e_, MUL).then_inc(s_vc, vc.step())
                V.wait_ge(s_vc, vc.n)
                la, _ = par_off["lru_a"]
                V.scalar_tensor_tensor(col[:, 6, :], par[:, la:la + 8], 0.0, col[:, 4, :], MAXOP, ADD).then_inc(s_vc, vc.step())
                V.wait_ge(s_vc, vc.n)
                V.tensor_scalar(col[:, 8, :], col[:, 6, :], -8.0, None, MUL)
                V.tensor_scalar(col[:, 9, :], col[:, 6, :], 8.0, None, MUL).then_inc(vector_done, vector.step("sp"))
                for n in range(2):
                    dve.wait_ge(s_prod, nth(u0 + n))
                    last = shifted(lx[:, n, :], bank(n), 24 + n)
                last.then_inc(vector_done, vector.step("lx"))
                dve_split(dve, nth_unit(0, 2))
                dve.wait_ge(scalar_done, scalar.after("lora"))
                cut(a_hi[:, 1:3, :], a_lo[:, 1:3, :], lx).then_inc(vector_done, vector.step("lxc"))
                for t in range(KT):
                    d = lambda n: dv(t, n)
                    st = lambda ins, n: ins.then_inc(vector_done, vector.step(f"{t}_{n}"))
                    now = lambda n: dve.wait_ge(vector_done, vector.after(f"{t}_{n}"))
                    aw = lambda n: dve.wait_ge(scalar_done, scalar.after(f"{t}_{n}"))
                    aw("ca")
                    dve_split(dve, nth_unit(t, 3))
                    dve.wait_ge(s_prod, nth(unit(t, 1)))
                    st(V.tensor_tensor(d("cx"), d("ca"), bank(1), MUL), "xa")
                    now("xa")
                    V.tensor_scalar(d("ya"), d("cx"), G("conv_a", 16 + t), None, MUL).then_inc(s_vc, vc.step())
                    V.wait_ge(s_vc, vc.n)
                    for q in (1, 2):
                        V.scalar_tensor_tensor(d("ya")[:, q:T], d("cx")[:, 0:T - q], G("conv_a", 8 * (2 - q) + t),
                                                     d("ya")[:, q:T], MUL, ADD).then_inc(s_vc, vc.step())
                        V.wait_ge(s_vc, vc.n)
                    dve_split(dve, nth_unit(t, 4))
                    dve.wait_ge(s_prod, nth(unit(t, 2)))
                    st(V.tensor_tensor(d("ya"), d("ya"), bank(2), MUL), "ba")
                    dve_split(dve, nth_unit(t, 6))
                    dve.wait_ge(s_prod, nth(unit(t, 4)))
                    V.tensor_scalar(d("u"), bank(4), G("lru_conv", 24 + t), G("lru_cb", t), MUL, ADD).then_inc(s_vc, vc.step())
                    V.wait_ge(s_vc, vc.n)
                    for q in (1, 2, 3):
                        last = V.scalar_tensor_tensor(d("u")[:, q:T], bank(4)[:, 0:T - q],
                                                      G("lru_conv", 8 * (3 - q) + t), d("u")[:, q:T], MUL, ADD)
                        if q < 3:
                            last.then_inc(s_vc, vc.step())
                            V.wait_ge(s_vc, vc.n)
                    last.then_inc(s_vc, vc.step())
                    if t:
                        dve.wait_ge(s_prod, nth(nth_unit(t - 1, small)))
                    V.wait_ge(s_vc, vc.n)
                    st(cut(a_hi[:, 0, :], a_lo[:, 0, :], d("u")), "u")
                    dve_split(dve, nth_unit(t, 8))
                    aw("ga")
                    V.tensor_tensor(M[:, t, :], d("ya"), d("ga"), MUL)
                    aw("gtb")
                    V.tensor_tensor(d("gb"), d("gb"), d("gtb"), MUL)
                    dve_split(dve, nth_unit(t, 9))
                    aw("lg")
                    V.tensor_tensor(d("si"), d("si"), d("u"), MUL)
                    aw("ea")
                    V.tensor_tensor(d("t1"), d("ea"), d("ea"), MUL).then_inc(s_vc, vc.step())
                    V.wait_ge(s_vc, vc.n)
                    st(V.scalar_tensor_tensor(d("t1"), d("t1"), 1.0, d("th"), ADD, MUL), "t1")
                    aw("wd")
                    V.tensor_scalar(d("lw"), d("sw"), LOG_DECAY, None, MUL).then_inc(s_vc, vc.step())
                    V.wait_ge(s_vc, vc.n)
                    V.tensor_tensor_scan(d("cum"), C("reset64"), d("lw"), 0.0, MUL, ADD).then_inc(s_vc, vc.step())
                    V.wait_ge(s_vc, vc.n)
                    st(V.tensor_tensor(d("cl"), d("cum"), d("lw"), SUB), "cum")
                    dve_split(dve, nth_unit(t, 10))
                    dve.wait_ge(s_prod, nth(unit(t, 12)))
                    st(shifted(d("r"), bank(12), t), "r")
                    dve_split(dve, nth_unit(t, 11))
                    dve.wait_ge(s_prod, nth(unit(t, 13)))
                    st(shifted(d("k"), bank(13), 8 + t), "k")
                    dve_split(dve, nth_unit(t, 12))
                    dve.wait_ge(s_prod, nth(unit(t, 14)))
                    st(shifted(VT[:, t, :], bank(14), 16 + t), "v")
                    V.tensor_scalar(d("kr"), d("k"), G("kk", t), None, MUL).then_inc(s_vc, vc.step())
                    V.wait_ge(s_vc, vc.n)
                    st(V.tensor_tensor(d("k2"), d("kr"), d("kr"), MUL), "k2")
                    V.tensor_scalar(d("tmp"), d("aa"), -1.0, G("ka", t), ADD, MUL).then_inc(s_vc, vc.step())
                    V.wait_ge(s_vc, vc.n)
                    V.scalar_tensor_tensor(d("k"), d("tmp"), 1.0, d("k"), ADD, MUL).then_inc(s_vc, vc.step())
                    V.wait_ge(s_vc, vc.n)
                    st(V.scalar_tensor_tensor(d("bp"), d("r"), G("rk", t), d("k"), MUL, MUL), "bp")
                    aw("dec")
                    V.tensor_tensor(AR[:, t, 1, :], d("r"), d("p1"), MUL)
                    V.tensor_tensor(KP[:, t, :], d("k"), d("p2"), MUL)
                    V.tensor_copy(EC[:, t, :], d("p1")[:, RC - 1:T:RC])
                    dve_split(dve, nth_unit(t, 14))
                    aw("mult")
                    V.memset(d("mu")[:, 0:1], 1.0).then_inc(s_vc, vc.step())
                    V.wait_ge(s_vc, vc.n)
                    V.tensor_tensor(d("si"), d("si"), d("mu"), MUL).then_inc(s_vc, vc.step())
                    V.wait_ge(s_vc, vc.n)
                    V.tensor_tensor_scan(d("th"), d("ea"), d("si"), 0.0, MUL, ADD).then_inc(s_vc, vc.step())
                    V.wait_ge(s_vc, vc.n)
                    V.tensor_tensor(d("th"), d("th"), d("gb"), MUL).then_inc(s_vc, vc.step())
                    V.wait_ge(s_vc, vc.n)
                    V.tensor_tensor(M[:, t, :], M[:, t, :], d("th"), ADD).then_inc(s_vc, vc.step())
                    V.wait_ge(s_vc, vc.n)
                    aw("nk")
                    V.tensor_scalar(d("nk"), d("nk"), 1e-12, None, MAXOP).then_inc(s_vc, vc.step())
                    V.wait_ge(s_vc, vc.n)
                    V.reciprocal(d("nk"), d("nk")).then_inc(s_vc, vc.step())
                    V.wait_ge(s_vc, vc.n)
                    V.tensor_tensor(d("kr"), d("kr"), d("nk"), MUL).then_inc(s_vc, vc.step())
                    V.wait_ge(s_vc, vc.n)
                    V.tensor_tensor(AR[:, t, 0, :], d("kr"), d("p3"), MUL)
                    V.tensor_tensor(d("kr"), d("kr"), d("aa"), MUL).then_inc(s_vc, vc.step())
                    V.wait_ge(s_vc, vc.n)
                    V.tensor_tensor(BT[:, t, :], d("kr"), d("p2"), MUL)
                    V.tensor_tensor(GC[:, t, :], d("g2"), d("gc"), MUL).then_inc(s_vc, vc.step())
                    V.wait_ge(s_vc, vc.n)
                    dve.wait_ge(tensor_done, tensor.after(f"{t}_bonus"))
                    V.tensor_tensor(d("tmp"), bank(17), VT[:, t, :], MUL).then_inc(s_vc, vc.step())
                    V.wait_ge(s_vc, vc.n)
                    V.scalar_tensor_tensor(d("tmp"), d("tmp"), G("lnx_b", t), GC[:, t, :], ADD, MUL).then_inc(s_vc, vc.step())
                    V.wait_ge(s_vc, vc.n)
                    st(V.tensor_tensor(M[:, t, :], M[:, t, :], d("tmp"), ADD), "bo")
                mask2 = con[:, con_off["strict64"][0]:con_off["strict64"][0] + 2 * P]
                for b in range(NB):
                    v4 = lambda ap: ap.rearrange("p (t h) a b -> p t h (a b)", h=2)
                    for g in range(4):
                        dve.wait_ge(tensor_done, tensor.after(f"A{b}_{g}"))
                        o = 4 * (g % 2)
                        for hf in range(2):
                            for q, dst in ((0, AB), (2, AK)):
                                last = V.tensor_tensor(v4(dst)[:, 2 * g:2 * g + 2, hf, :],
                                                       ps[:, o + q + hf, :].rearrange("p (a b) -> p a b", a=2),
                                                       over(mask2, 2), MUL)
                        last.then_inc(vector_done, vector.step(f"am{b}_{g}"))
                    dve.wait_ge(vector_done, vector.after(f"am{b}_3"))
                    if b == 0:
                        dve.wait_ge(s_x_out, 16)
                    V.tensor_tensor(X, AB[:, :, 0, :], over(levels[:, 0, :], RH), MUL).then_inc(vector_done, vector.step(f"x{b}"))
                    dve.wait_ge(vector_done, vector.after(f"x{b}"))
                    for g in range(4):
                        s4 = slice(4 * g, 4 * g + 4)
                        dve.wait_ge(tensor_done, tensor.after(f"Y{b}_0_{g}"))
                        V.tensor_tensor(Ti[:, s4, :], over(ident, 4), ps[:, g % 2, :].rearrange("p (a b) -> p a b", a=4), SUB)
                        V.tensor_tensor(TT[:, s4, :], over(ident, 4), X[:, s4, :], SUB).then_inc(s_vc, vc.step())
                        V.wait_ge(s_vc, vc.n)
                        V.tensor_tensor(X[:, s4, :], AB[:, s4, 0, :], over(levels[:, 1, :], 4), MUL).then_inc(vector_done, vector.step(f"tc{b}_0_{g}"))
                    for l in range(1, LV):
                        for g in range(4):
                            s4 = slice(4 * g, 4 * g + 4)
                            dve.wait_ge(tensor_done, tensor.after(f"U{b}_{l}_{g}"))
                            if l < LV - 1:
                                V.tensor_tensor(Ti[:, s4, :], Ti[:, s4, :],
                                                ps[:, 2 + g % 2, :].rearrange("p (a b) -> p a b", a=4), SUB)
                                V.tensor_tensor(X[:, s4, :], AB[:, s4, 0, :], over(levels[:, l + 1, :], 4), MUL)
                            V.tensor_tensor(TT[:, s4, :], TT[:, s4, :],
                                                     ps[:, 4 + g % 2, :].rearrange("p (a b) -> p a b", a=4), SUB).then_inc(vector_done, vector.step(f"tc{b}_{l}_{g}"))
                    if b == 0:
                        V.memset(S2, 0.0)
                    V.memset(Ti, 0.0).then_inc(vector_done, vector.step(f"z{b}"))
                    for c in (2 * b, 2 * b + 1):
                        r = slice(64 * (c % 2), 64 * (c % 2) + 64)
                        dve.wait_ge(tensor_done, tensor.after(f"rhs{c}"))
                        if c % 2 == 0:
                            dve.wait_ge(vector_done, vector.after(f"z{b}"))
                        for k in range(2):
                            last = V.tensor_scalar(RHS[r, 512 * k:512 * k + 512], ps[r, k, :], -1.0, None, MUL)
                        last.then_inc(vector_done, vector.step(f"rh{c}"))
                        dve.wait_ge(tensor_done, tensor.after(f"y{c}"))
                        V.tensor_copy(VT[:, :, toks(c)], ps[:, 4, :].rearrange("p (a b) -> p a b", a=8)).then_inc(vector_done, vector.step(f"yo{c}"))
                        if c < 3:
                            dve.wait_ge(tensor_done, tensor.after(f"st{c}"))
                            for hf in range(2):
                                w = slice(64 * hf, 64 * hf + 64)
                                for k in range(2):
                                    last = V.tensor_tensor(S2[w, 4 * k:4 * k + 4, w],
                                                           ps[w, 5 + k, :].rearrange("p (a b) -> p a b", a=4)[:, :, w],
                                                           S2[w, 4 * k:4 * k + 4, w], ADD)
                            last.then_inc(s_vc, vc.step())
                            V.wait_ge(s_vc, vc.n)
                            for hf in range(2):
                                w = slice(64 * hf, 64 * hf + 64)
                                last = V.tensor_tensor(S2[w, :, w], S2[w, :, w], each(EC[w, :, c], RN), MUL)
                            last.then_inc(vector_done, vector.step(f"s{c}"))
                dve.wait_ge(tensor_done, tensor.after("mean"))
                for k in range(4):
                    last = V.scalar_tensor_tensor(VT[:, 2 * k:2 * k + 2, :], ps[:, k, :].rearrange("p (a b) -> p a b", a=2),
                                                  -1.0 / RN, VT[:, 2 * k:2 * k + 2, :], MUL, ADD)
                last.then_inc(vector_done, vector.step("cen"))
                dve.wait_ge(scalar_done, scalar.after("sd"))
                V.reciprocal(rr[0:16, :], rr[0:16, :]).then_inc(vector_done, vector.step("rs"))
                dve.wait_ge(tensor_done, tensor.after("bc"))
                for t in range(KT):
                    last = V.scalar_tensor_tensor(VT[:, t, :], VT[:, t, :], G("lnx_g", t),
                                                  ps[:, t // 2, t % 2 * T:t % 2 * T + T], MUL, MUL)
                last.then_inc(s_vc, vc.step())
                V.wait_ge(s_vc, vc.n)
                V.tensor_tensor(VT, VT, GC, MUL).then_inc(s_vc, vc.step())
                V.wait_ge(s_vc, vc.n)
                dve.wait_ge(s_m_in, 16)
                V.tensor_tensor(M, M, VT, ADD).then_inc(s_vc, vc.step())
                V.wait_ge(s_vc, vc.n)
                cut(h_hi[:, :, :], h_lo[:, :, :], M).then_inc(vector_done, vector.step("m"))
                dve.wait_ge(s_x_in, 16)
                out_dve(dve, "second", u0 + 98)

            def spill_prog(pool):
                if order["second"]:
                    pool.wait_ge(s_x, 4 * order["second"])
                else:
                    pool.wait_ge(s_const, 16 * 3)
                pool.dma_start(stored[0], x[:, :, :]).then_inc(s_x_out, 16)
                pool.wait_ge(vector_done, vector.after("7_bo"))
                pool.dma_start(stored[1], M).then_inc(s_m_out, 16)
                pool.wait_ge(s_x_out, 16)
                pool.wait_ge(s_m_out, 16)
                pool.wait_ge(tensor_done, tensor.after(f"U1_{LV - 1}_3"))
                pool.dma_start(x[:, :, :], stored[0]).then_inc(s_x_in, 16)
                pool.dma_start(M, stored[1]).then_inc(s_m_in, 16)
            return pe_prog, act_prog, dve_prog, spill_prog
        mixers = {}
        if "even" in stages:
            mixers["even"] = even_mixer()
        if "odd" in stages:
            mixers["odd"] = odd_mixer()
        if "second" in stages:
            mixers["second"] = second_mixer()
        ffns = {s: Ffn(s) for s in stages if s[:3] == "ffn" or s == "mlp"}
        block = ctx.enter_context(nc.Block())

        @block.sync
        def _(sp):
            def load(s, u):
                sp.dma_start(raw[:, s, :], a_w[u].rearrange("a p n -> (a p) n")
                             if not isinstance(u, int) else a_w[u]).then_inc(arrived[s], 16)
            for dst, src in ((x[:, :, :], a_x), (con[:, :], a_con), (par[:, :], a_par)):
                sp.dma_start(dst, src).then_inc(s_const, 16)
            rounds, rest = total_units // RING, total_units % RING
            for s in range(RING):
                load(s, s)
            with sp.Fori(1, rounds) as i:
                for s in range(RING):
                    sp.wait_ge(s_lo, i * RING + (s - RING + 1))
                    load(s, bass.ds(i * RING + s, 1))
            for s in range(rest):
                u = rounds * RING + s
                sp.wait_ge(s_lo, nth(u - RING))
                load(s, u)
            for p_ in range(4):
                sp.wait_ge(s_nrm, 4 * len(stages) + p_ + 1)
                sp.dma_start(out[:, pair_of(p_), :], whole[:, pair_of(p_), :]).then_inc(s_out, 16)
            sp.wait_ge(s_out, 16 * 4)

        @block.gpsimd
        def _(pool):
            for s, n in n_ple.items():
                if order[s] > 1:
                    pool.wait_ge(s_x, 4 * (order[s] - 1))
                pool.dma_start(pin, a_p[:, int(s[3]), :, :]).then_inc(s_pin, 16)
            if "second" in stages:
                mixers["second"][3](pool)

        @block.tensor
        def _(pe):
            pe.wait_ge(s_const, 16 * 3)
            for n, s in enumerate(stages):
                norm_pe(pe, n)
                if s[:3] == "ple":
                    ple_in_pe(pe, s)
                if s in ffns:
                    ffn_pe(pe, ffns[s])
                elif s[:3] == "ple":
                    ple_pe(pe, s)
                else:
                    mixers[s][0](pe)
            norm_pe(pe, len(stages))

        @block.scalar
        def _(act):
            act.wait_ge(s_const, 16 * 3)
            for n, s in enumerate(stages):
                norm_act(act, n)
                if s in ffns:
                    ffn_act(act, ffns[s])
                elif s[:3] == "ple":
                    ple_act(act, s)
                else:
                    mixers[s][1](act)
            norm_act(act, len(stages))

        @block.vector
        def _(dve):
            dve.wait_ge(s_const, 16 * 3)
            for n, s in enumerate(stages):
                if s[:3] == "ple":
                    ple_in_dve(dve, s)
                norm_dve(dve, n, NORM_OF[s])
                if s in ffns:
                    ffn_dve(dve, ffns[s])
                elif s[:3] == "ple":
                    ple_dve(dve, s)
                else:
                    mixers[s][2](dve)
            norm_dve(dve, len(stages), "final")


def kernel(**inputs):
    import concourse.bacc as bacc
    from concourse.bass_utils import run_bass_kernel_spmd

    a = {k: np.asarray(v) for k, v in inputs.items()}
    units = [u for s in STAGES for u in stage_units(s, a)]
    arrays = {
        "x_t": np.ascontiguousarray(a["x"][0].T.reshape(KT, P, T).transpose(1, 0, 2)),
        "p_t": np.ascontiguousarray(a["p"][:, 0].transpose(0, 2, 1).reshape(2, 2, P, T).transpose(2, 0, 1, 3)),
        "weights": np.stack(units),
        "parameters": parameter_columns(a),
        "shape_constants": shape_constants(),
    }
    nc = bacc.Bacc("TRN2", target_bir_lowering=False, num_devices=1)
    aps = [nc.dram_tensor(n, v.shape, mybir.dt.float32, kind="ExternalInput").ap() for n, v in arrays.items()]
    out = nc.dram_tensor("out_t", (P, KT, T), mybir.dt.float32, kind="ExternalOutput").ap()
    build(nc, *aps, out)
    r = run_bass_kernel_spmd(nc, [arrays], core_ids=[0])
    y = np.asarray(r.results[0]["out_t"])
    return np.ascontiguousarray(y.transpose(2, 1, 0).reshape(1, T, D))
```
